# Optimizing a Trainium2 kernel written in Bass

```python
import math
import jax, jax.numpy as jnp
from jax import lax
import numpy as np

D_MODEL = 1024
BATCH = 1
SEQ = 1024
DEPTH = 2
DEC_BATCH = 1
DEC_SEQ = 32
PAST_LEN = 512

CHUNK = 64
N_EVEN = (DEPTH + 1) // 2
N_ODD = DEPTH // 2
SSM_WIDTH = D_MODEL // 2
SSM_GROUP = 16
SSM_GROUPS = SSM_WIDTH // SSM_GROUP
SSM_STATE = 64
DT_MIN = 1e-3
DT_MAX = 1e-1
HEAD_DIM = 64
N_HEADS = (D_MODEL // 2) // HEAD_DIM
N_KV_HEADS = 2
GQ = N_HEADS // N_KV_HEADS
WINDOW = 128
WINDOW_CHUNKS = WINDOW // CHUNK
ROPE_THETA = 10000.0
EVEN_IN = SSM_WIDTH + (N_HEADS + 2 * N_KV_HEADS) * HEAD_DIM
CONV_WIDTH = 3
N_MEM = 256
X_HEADS = 4
X_HEAD_DIM = D_MODEL // X_HEADS
D_FF = 2816
EPS = 1e-6
NEG = -1e30

kernel_name = 'hybrid_s5_swa_shortconv_stream_step'

F32 = jnp.float32

def rms_norm(x, g):
    xf = x.astype(F32)
    y = xf * lax.rsqrt(jnp.mean(xf * xf, axis=-1, keepdims=True) + EPS)
    return (y * g.astype(F32)).astype(x.dtype)

def rope(t, pos):
    half = HEAD_DIM // 2
    inv = ROPE_THETA ** (-jnp.arange(half, dtype=F32) * 2.0 / HEAD_DIM)
    ang = pos[:, None] * inv[None, :]
    cos = jnp.cos(ang)[None, :, None, :]
    sin = jnp.sin(ang)[None, :, None, :]
    tf = t.astype(F32)
    t1, t2 = tf[..., :half], tf[..., half:]
    return jnp.concatenate([t1 * cos - t2 * sin, t2 * cos + t1 * sin], axis=-1).astype(t.dtype)

def causal_conv(x, prev, w):
    seq = x.shape[1]
    xp = jnp.concatenate([prev.astype(x.dtype), x], axis=1)
    y = w[0] * xp[:, 0:seq]
    for j in range(1, CONV_WIDTH):
        y = y + w[j] * xp[:, j:j + seq]
    return y, xp[:, -(CONV_WIDTH - 1):]

def _scan_op(e1, e2):
    a1, b1 = e1
    a2, b2 = e2
    return a1 * a2, a2 * b1 + b2

def s5_mixer(u, h0_re, h0_im, a_re, a_im, log_dt, b_re, b_im, c_re, c_im, d, w_glu):
    bsz, seq, _ = u.shape
    uf = u.astype(F32).reshape(bsz, seq, SSM_GROUPS, SSM_GROUP)
    lam = lax.complex(a_re.astype(F32), a_im.astype(F32))
    dt = jnp.exp(log_dt.astype(F32))
    a_bar = jnp.exp(lam * dt)
    b_bar = ((a_bar - 1.0) / lam)[..., None] * lax.complex(b_re.astype(F32), b_im.astype(F32))
    bu = jnp.einsum('blgh,gph->blgp', uf.astype(jnp.complex64), b_bar)
    h0 = lax.complex(h0_re.astype(F32), h0_im.astype(F32))
    bu = bu.at[:, 0].add(a_bar[None] * h0)
    a_seq = jnp.broadcast_to(a_bar, bu.shape)
    _, h = lax.associative_scan(_scan_op, (a_seq, bu), axis=1)
    c = lax.complex(c_re.astype(F32), c_im.astype(F32))
    y = jnp.real(jnp.einsum('blgp,ghp->blgh', h, c)) + d.astype(F32) * uf
    y = y.reshape(bsz, seq, SSM_WIDTH)
    g = jax.nn.gelu(y)
    out = g * jax.nn.sigmoid(g @ w_glu.astype(F32))
    h_last = h[:, -1]
    return out.astype(u.dtype), jnp.real(h_last), jnp.imag(h_last)

def swa_attention(q, k, v, past_k, past_v, sinks, start):
    bsz, seq = q.shape[0], q.shape[1]
    n_blk = -(-seq // CHUNK)
    l_pad = n_blk * CHUNK
    pad = l_pad - seq
    front = WINDOW - past_k.shape[1]

    def pad4(t, a, b):
        return jnp.pad(t, ((0, 0), (a, b), (0, 0), (0, 0)))

    q = pad4(q, 0, pad)
    k_all = jnp.concatenate([pad4(past_k.astype(k.dtype), front, 0), pad4(k, 0, pad)], axis=1)
    v_all = jnp.concatenate([pad4(past_v.astype(v.dtype), front, 0), pad4(v, 0, pad)], axis=1)
    n_key = WINDOW + l_pad
    idx = jnp.arange(n_blk)[:, None] * CHUNK + jnp.arange(WINDOW + CHUNK)[None, :]
    k_blk = k_all[:, idx]
    v_blk = v_all[:, idx]
    slot = jnp.arange(n_key)
    k_pos = start - WINDOW + slot
    k_ok = (k_pos >= 0) & (slot < WINDOW + seq)
    k_pos_b = k_pos[idx]
    k_ok_b = k_ok[idx]
    q_pos = start + jnp.arange(l_pad).reshape(n_blk, CHUNK)
    q_chunk = q_pos // CHUNK
    k_chunk = k_pos_b // CHUNK
    mask = (k_ok_b[:, None, :]
            & (k_chunk[:, None, :] <= q_chunk[:, :, None])
            & (k_chunk[:, None, :] >= q_chunk[:, :, None] - WINDOW_CHUNKS))
    q_blk = q.reshape(bsz, n_blk, CHUNK, N_KV_HEADS, GQ, HEAD_DIM)
    s = jnp.einsum('bnqkgd,bnskd->bnkgqs', q_blk, k_blk, preferred_element_type=F32) * (HEAD_DIM ** -0.5)
    s = jnp.where(mask[None, :, None, None], s, NEG)
    sink = jnp.broadcast_to(sinks.astype(F32).reshape(1, 1, N_KV_HEADS, GQ, 1, 1), s.shape[:-1] + (1,))
    p = jax.nn.softmax(jnp.concatenate([s, sink], axis=-1), axis=-1)[..., :-1]
    o = jnp.einsum('bnkgqs,bnskd->bnqkgd', p.astype(v.dtype), v_blk)
    return o.reshape(bsz, l_pad, N_HEADS * HEAD_DIM)[:, :seq]

def cross_attention(h, mem_k, mem_v, wq, wo):
    bsz, seq, _ = h.shape
    q = (h @ wq).reshape(bsz, seq, X_HEADS, X_HEAD_DIM)
    s = jnp.einsum('blhd,bmhd->bhlm', q, mem_k, preferred_element_type=F32) * (X_HEAD_DIM ** -0.5)
    p = jax.nn.softmax(s, axis=-1).astype(mem_v.dtype)
    o = jnp.einsum('bhlm,bmhd->blhd', p, mem_v).reshape(bsz, seq, D_MODEL)
    return o @ wo

def conv_ffn(h, prev, w_up, conv_w, w_down):
    up = h @ w_up
    gate, val = up[..., :D_FF], up[..., D_FF:]
    gate_c, new_prev = causal_conv(gate, prev, conv_w)
    return (jax.nn.silu(gate_c) * val) @ w_down, new_prev

def trunk(x, start, past_k, past_v, ssm_re, ssm_im, conv_mix_prev, conv_ffn_prev, mem_k, mem_v, p):
    bsz, seq, _ = x.shape
    pos = (start + jnp.arange(seq)).astype(F32)
    new_k, new_v, new_re, new_im, new_cm, new_cf = [], [], [], [], [], []
    o0 = SSM_WIDTH
    o1 = o0 + N_HEADS * HEAD_DIM
    o2 = o1 + N_KV_HEADS * HEAD_DIM
    for layer in range(DEPTH):
        h = rms_norm(x, p['norm_mix'][layer])
        if layer % 2 == 0:
            e = layer // 2
            proj = h @ p['w_in_even'][e]
            u = proj[..., :o0]
            q = rope(proj[..., o0:o1].reshape(bsz, seq, N_HEADS, HEAD_DIM), pos)
            k = rope(proj[..., o1:o2].reshape(bsz, seq, N_KV_HEADS, HEAD_DIM), pos)
            v = proj[..., o2:].reshape(bsz, seq, N_KV_HEADS, HEAD_DIM)
            y_a, h_re, h_im = s5_mixer(u, ssm_re[e], ssm_im[e], p['ssm_a_re'][e], p['ssm_a_im'][e],
                                       p['ssm_log_dt'][e], p['ssm_b_re'][e], p['ssm_b_im'][e],
                                       p['ssm_c_re'][e], p['ssm_c_im'][e], p['ssm_d'][e], p['w_glu'][e])
            y_b = swa_attention(q, k, v, past_k[e], past_v[e], p['attn_sinks'][e], start)
            x = x + jnp.concatenate([y_a, y_b], axis=-1) @ p['w_out_even'][e]
            new_k.append(k)
            new_v.append(v)
            new_re.append(h_re)
            new_im.append(h_im)
        else:
            o = layer // 2
            proj = h @ p['w_in_odd'][o]
            gate_b, gate_c, z = jnp.split(proj, 3, axis=-1)
            z_conv, cm = causal_conv(gate_c * z, conv_mix_prev[o], p['conv_mix_w'][o])
            x = x + (gate_b * z_conv) @ p['w_out_odd'][o]
            new_cm.append(cm)
        h = rms_norm(x, p['norm_xattn'][layer])
        x = x + cross_attention(h, mem_k[layer], mem_v[layer], p['xattn_wq'][layer], p['xattn_wo'][layer])
        h = rms_norm(x, p['norm_ffn'][layer])
        f, cf = conv_ffn(h, conv_ffn_prev[layer], p['ffn_w_up'][layer], p['ffn_conv_w'][layer], p['ffn_w_down'][layer])
        x = x + f
        new_cf.append(cf)
    y = rms_norm(x, p['norm_final'])
    return (y, jnp.stack(new_k), jnp.stack(new_v), jnp.stack(new_re), jnp.stack(new_im),
            jnp.stack(new_cm), jnp.stack(new_cf))

def setup_inputs(seed: int = 0) -> dict:
    key = jax.random.key(seed)
    ks = iter(jax.random.split(key, 48))

    def nrm(shape, scale=1.0):
        return scale * jax.random.normal(next(ks), shape, F32)

    ne, no = N_EVEN, N_ODD
    win_rows = min(WINDOW, PAST_LEN)
    cw = CONV_WIDTH - 1
    inp = {}
    inp['x_prompt'] = nrm((BATCH, SEQ, D_MODEL))
    inp['x_sample'] = nrm((DEC_BATCH, DEC_SEQ, D_MODEL))
    inp['mem_prompt'] = nrm((BATCH, N_MEM, D_MODEL))
    inp['cache_win_k'] = nrm((ne, DEC_BATCH, win_rows, N_KV_HEADS, HEAD_DIM))
    inp['cache_win_v'] = nrm((ne, DEC_BATCH, win_rows, N_KV_HEADS, HEAD_DIM))
    inp['state_ssm_re'] = nrm((ne, DEC_BATCH, SSM_GROUPS, SSM_STATE), 0.05)
    inp['state_ssm_im'] = nrm((ne, DEC_BATCH, SSM_GROUPS, SSM_STATE), 0.05)
    inp['state_conv_mix'] = nrm((no, DEC_BATCH, cw, D_MODEL))
    inp['state_conv_ffn'] = nrm((DEPTH, DEC_BATCH, cw, D_FF))
    inp['cache_mem_k'] = nrm((DEPTH, DEC_BATCH, N_MEM, X_HEADS, X_HEAD_DIM))
    inp['cache_mem_v'] = nrm((DEPTH, DEC_BATCH, N_MEM, X_HEADS, X_HEAD_DIM))
    inp['norm_mix'] = 1.0 + nrm((DEPTH, D_MODEL), 0.02)
    inp['norm_xattn'] = 1.0 + nrm((DEPTH, D_MODEL), 0.02)
    inp['norm_ffn'] = 1.0 + nrm((DEPTH, D_MODEL), 0.02)
    inp['norm_final'] = 1.0 + nrm((D_MODEL,), 0.02)
    inp['w_in_even'] = nrm((ne, D_MODEL, EVEN_IN), D_MODEL ** -0.5)
    inp['w_out_even'] = nrm((ne, D_MODEL, D_MODEL), D_MODEL ** -0.5)
    inp['ssm_a_re'] = -0.5 + nrm((ne, SSM_GROUPS, SSM_STATE), 0.01)
    inp['ssm_a_im'] = jnp.pi * jnp.arange(SSM_STATE, dtype=F32) + nrm((ne, SSM_GROUPS, SSM_STATE), 0.01)
    inp['ssm_log_dt'] = jax.random.uniform(next(ks), (ne, SSM_GROUPS, SSM_STATE), F32,
                                           math.log(DT_MIN), math.log(DT_MAX))
    inp['ssm_b_re'] = nrm((ne, SSM_GROUPS, SSM_STATE, SSM_GROUP), (2 * SSM_GROUP) ** -0.5)
    inp['ssm_b_im'] = nrm((ne, SSM_GROUPS, SSM_STATE, SSM_GROUP), (2 * SSM_GROUP) ** -0.5)
    inp['ssm_c_re'] = nrm((ne, SSM_GROUPS, SSM_GROUP, SSM_STATE), SSM_STATE ** -0.5)
    inp['ssm_c_im'] = nrm((ne, SSM_GROUPS, SSM_GROUP, SSM_STATE), SSM_STATE ** -0.5)
    inp['ssm_d'] = nrm((ne, SSM_GROUPS, SSM_GROUP))
    inp['w_glu'] = nrm((ne, SSM_WIDTH, SSM_WIDTH), SSM_WIDTH ** -0.5)
    inp['attn_sinks'] = nrm((ne, N_HEADS), 0.5)
    inp['w_in_odd'] = nrm((no, D_MODEL, 3 * D_MODEL), D_MODEL ** -0.5)
    inp['conv_mix_w'] = nrm((no, CONV_WIDTH, D_MODEL), CONV_WIDTH ** -0.5)
    inp['w_out_odd'] = nrm((no, D_MODEL, D_MODEL), D_MODEL ** -0.5)
    inp['xattn_wq'] = nrm((DEPTH, D_MODEL, D_MODEL), D_MODEL ** -0.5)
    inp['xattn_wkv'] = nrm((DEPTH, D_MODEL, 2 * D_MODEL), D_MODEL ** -0.5)
    inp['xattn_wo'] = nrm((DEPTH, D_MODEL, D_MODEL), D_MODEL ** -0.5)
    inp['ffn_w_up'] = nrm((DEPTH, D_MODEL, 2 * D_FF), D_MODEL ** -0.5)
    inp['ffn_conv_w'] = nrm((DEPTH, CONV_WIDTH, D_FF), CONV_WIDTH ** -0.5)
    inp['ffn_w_down'] = nrm((DEPTH, D_FF, D_MODEL), D_FF ** -0.5)
    return inp

def reference(x_prompt, x_sample, mem_prompt, cache_win_k, cache_win_v, state_ssm_re, state_ssm_im,
              state_conv_mix, state_conv_ffn, cache_mem_k, cache_mem_v, norm_mix, norm_xattn, norm_ffn,
              norm_final, w_in_even, w_out_even, ssm_a_re, ssm_a_im, ssm_log_dt, ssm_b_re, ssm_b_im,
              ssm_c_re, ssm_c_im, ssm_d, w_glu, attn_sinks, w_in_odd, conv_mix_w, w_out_odd, xattn_wq,
              xattn_wkv, xattn_wo, ffn_w_up, ffn_conv_w, ffn_w_down):
    params = dict(norm_mix=norm_mix, norm_xattn=norm_xattn, norm_ffn=norm_ffn, norm_final=norm_final,
                  w_in_even=w_in_even, w_out_even=w_out_even, ssm_a_re=ssm_a_re, ssm_a_im=ssm_a_im,
                  ssm_log_dt=ssm_log_dt, ssm_b_re=ssm_b_re, ssm_b_im=ssm_b_im, ssm_c_re=ssm_c_re,
                  ssm_c_im=ssm_c_im, ssm_d=ssm_d, w_glu=w_glu, attn_sinks=attn_sinks, w_in_odd=w_in_odd,
                  conv_mix_w=conv_mix_w, w_out_odd=w_out_odd, xattn_wq=xattn_wq, xattn_wo=xattn_wo,
                  ffn_w_up=ffn_w_up, ffn_conv_w=ffn_conv_w, ffn_w_down=ffn_w_down)
    dt = x_prompt.dtype
    bp = x_prompt.shape[0]
    cw = CONV_WIDTH - 1
    kv = jnp.einsum('bmd,lde->lbme', mem_prompt, xattn_wkv)
    mem_k_p = kv[..., :D_MODEL].reshape(DEPTH, bp, N_MEM, X_HEADS, X_HEAD_DIM)
    mem_v_p = kv[..., D_MODEL:].reshape(DEPTH, bp, N_MEM, X_HEADS, X_HEAD_DIM)
    zk = jnp.zeros((N_EVEN, bp, WINDOW, N_KV_HEADS, HEAD_DIM), dt)
    zs = jnp.zeros((N_EVEN, bp, SSM_GROUPS, SSM_STATE), F32)
    zcm = jnp.zeros((N_ODD, bp, cw, D_MODEL), dt)
    zcf = jnp.zeros((DEPTH, bp, cw, D_FF), dt)
    y_prompt, k_p, v_p, ssm_re_p, ssm_im_p, conv_mix_p, conv_ffn_p = trunk(
        x_prompt, 0, zk, zk, zs, zs, zcm, zcf, mem_k_p, mem_v_p, params)
    win_k_p = k_p[:, :, -WINDOW:]
    win_v_p = v_p[:, :, -WINDOW:]
    y_sample, win_k_s, win_v_s, ssm_re_s, ssm_im_s, conv_mix_s, conv_ffn_s = trunk(
        x_sample, PAST_LEN, cache_win_k, cache_win_v, state_ssm_re, state_ssm_im,
        state_conv_mix, state_conv_ffn, cache_mem_k, cache_mem_v, params)
    return (y_prompt, y_sample, win_k_p, win_v_p, ssm_re_p, ssm_im_p, conv_mix_p, conv_ffn_p,
            mem_k_p, mem_v_p, win_k_s, win_v_s, ssm_re_s, ssm_im_s, conv_mix_s, conv_ffn_s)


_drawn_inputs = setup_inputs


def setup_inputs(seed=0):
    import zlib

    import numpy as np

    out = dict(_drawn_inputs(seed))
    spreads = {}
    factors = {'norm_xattn': 8.0, 'norm_final': 2.876, 'ssm_a_re': 3.975, 'attn_sinks': 8.0}
    for name, (base, spread) in spreads.items():
        noise = np.random.default_rng([zlib.crc32(name.encode()), seed]).standard_normal(out[name].shape)
        drawn = base * np.exp(spread * noise) if base else spread * noise
        out[name] = __import__('jax').numpy.asarray(drawn.astype(out[name].dtype))
    for name, factor in factors.items():
        out[name] = (out[name] * factor).astype(out[name].dtype)
    return out
```

```python
from contextlib import ExitStack

import numpy as np
import concourse.bass as bass
from concourse import mybir

F32, F32R, I32 = mybir.dt.float32, mybir.dt.float32r, mybir.dt.int32
ALU = mybir.AluOpType
ACT = mybir.ActivationFunctionType
AX = mybir.AxisListType

P = 128
D, KT = 1024, 8
SEQ, DEC = 1024, 32
NCH, CW = 3, 354
TW = NCH * CW
S0 = TW - DEC
F_FF, FT = 2816, 22
NMEM = 256
HEADS = 4
CK, NCK = 8, SEQ // 8
CC = NCK + 1 + DEC // CK
NEG = -1e30
BLK = 1024

PHASES = [("kv", 32, 32), ("inp", 10, 16), ("glu", 2, 4), ("out", 8, 32), ("x0", 16, 40), ("f0", 66, 132),
          ("c1", 32, 56), ("x1", 16, 40), ("f1", 66, 132)]
N0, T0 = {}, {}
_n = _t = 0
for _name, _b, _tl in PHASES:
    N0[_name], T0[_name] = _n, _t
    _n, _t = _n + _b, _t + _tl
NBLOCKS, NTILES = _n, _t
NEXT = {a[0]: b[0] for a, b in zip(PHASES, PHASES[1:])}

COLS = {}
_c = 0
for _name, _w in [("g_mix0", 8), ("g_x0", 8), ("g_f0", 8), ("g_mix1", 8), ("g_x1", 8), ("g_f1", 8), ("g_fin", 8),
                  ("cm_w", 24), ("cm_s", 16), ("cf_w0", 66), ("cf_s0", 44), ("cf_w1", 66), ("cf_s1", 44),
                  ("sink", 8), ("a_re", 16), ("a_im", 16), ("log_dt", 16), ("h0_re", 16), ("h0_im", 16)]:
    COLS[_name] = (_c, _w)
    _c += _w
NCOL = _c

INP = ["k", "v", "Rk", "u0", "VT", "u1", "u2", "u3", "q0", "q1", "Rq0", "q2", "Rq1", "q3", "Rq2", "Rq3"]
INP_BLOCKS = [x for x in INP if x[0] != "R" and x != "VT"]


class Steps:

    def __init__(self, sem, names):
        self.sem, self.n = sem, len(names)
        self.k = {x: i + 1 for i, x in enumerate(names)}

    def at(self, name, i=0):
        return self.sem, i * self.n + self.k[name]



GAIN = {"inp": "g_mix0", "x0": "g_x0", "f0": "g_f0", "c1": "g_mix1", "x1": "g_x1", "f1": "g_f1", "fin": "g_fin"}
QSLOT = {"k": 0, "q0": 1, "q1": 0, "q2": 1, "q3": 0}
ADDS = {"out": 32, "x0": 32, "f0": 88, "c1": 32, "x1": 32, "f1": 88}
CEXP = [1.0 / 5040, 1.0 / 720, 1.0 / 120, 1.0 / 24, 1.0 / 6, 0.5, 1.0]
CSIN = [1.0 / 6227020800, -1.0 / 39916800, 1.0 / 362880, -1.0 / 5040, 1.0 / 120, -1.0 / 6]
CCOS = [-1.0 / 87178291200, 1.0 / 479001600, -1.0 / 3628800, 1.0 / 40320, -1.0 / 720, 1.0 / 24, -0.5]
ROUND = 12582912.0
LN2 = (0.693359375, -2.12194440e-4)
PI3 = (3.140625, 9.67502593994140625e-4, 1.5099579909783764e-7)


def build(nc, a):
    with ExitStack() as ctx:
        cursor = [16512]

        def place(name, shape, dt=F32, offset=None):
            size = (4 * int(np.prod(shape[1:])) + 31) // 32 * 32
            if offset is None:
                offset = cursor[0]
                cursor[0] += size
            return nc.alloc_sbuf_tensor_at(name, shape, dt, offset=(offset + 31) // 32 * 32)

        def region(start, limit):
            start = (start + 31) // 32 * 32

            pos = [start]

            def put(name, shape, dt=F32):
                t = place(name, shape, dt, offset=pos[0])
                pos[0] += (4 * int(np.prod(shape[1:])) + 31) // 32 * 32
                assert pos[0] <= limit, (name, pos[0] - limit)
                return t
            return put

        def sem(name):
            return ctx.enter_context(nc.semaphore(name))

        X = place("X", [P, KT, TW])
        xh_off = cursor[0]
        XH = place("XH", [P, KT, TW], F32R)
        XL = place("XL", [P, KT, TW], F32R)
        x_end = cursor[0]
        WR = place("WR", [P, 2, BLK])
        WH = place("WH", [P, 2, BLK], F32R)
        WL = place("WL", [P, 2, BLK], F32R)
        hh_off = cursor[0]
        HH = place("HH", [P, 2, TW], F32R)
        HL = place("HL", [P, 2, TW], F32R)
        hh_end = cursor[0]
        RSTD = place("RSTD", [P, TW])
        LNV = place("LNV", [P, TW])
        COL = place("COL", [P, NCOL])
        IDENT = place("IDENT", [P, P])
        ONES = place("ONES", [P, P])
        EPSC = place("EPSC", [P, 1])
        RHO8 = place("RHO8", [P, 16])
        SMALL = place("SMALL", [P, 64])
        arena, end = cursor[0], 229344

        put = region(arena, end)
        MR = put("MR", [P, KT, NMEM])
        MH = put("MH", [P, KT, NMEM], F32R)
        ML = put("ML", [P, KT, NMEM], F32R)
        KVS = put("KVS", [P, 2, KT, NMEM])
        T3 = put("T3", [P, 16, 8, 16])
        DD = put("DD", [16, 512])
        put = region(xh_off, x_end)
        PR, PI = put("PR", [P, 16, 8, 16]), put("PI", [P, 16, 8, 16])
        T1, T2 = put("T1", [P, 16, 8, 16]), put("T2", [P, 16, 8, 16])
        BTP = put("BTP", [P, 2, 16, P])
        KR = put("KR", [P, 512])
        BR, BI = put("BR", [P, 16, 16]), put("BI", [P, 16, 16])
        BBR, BBI = put("BBR", [P, 16, 16]), put("BBI", [P, 16, 16])
        CR, CI, NCI = put("CR", [P, 16, 16]), put("CI", [P, 16, 16]), put("NCI", [P, 16, 16])
        AR, AI = put("AR", [P, 16, 9]), put("AI", [P, 16, 9])
        AS = put("AS", [P, 24, 16])
        ASI = put("ASI", [P, 16], I32)
        put = region(hh_off, hh_end)
        ERP, EIP = put("ERP", [P, 16, NCK + 1]), put("EIP", [P, 16, NCK + 1])

        put = region(arena, end)
        UJ = put("UJ", [P, 4, CK, CC])
        Q = put("Q", [P, 4, TW])
        KB = put("KB", [P, 1408])
        VB = put("VB", [P, 11, P])
        SMX = put("SMX", [P, 64])
        MASK = put("MASK", [P, 3, 256])
        ROT = put("ROT", [P, P])
        VTT = put("VTT", [P, TW])
        put = region(hh_off, hh_end)
        COS, SIN = put("COS", [P, TW]), put("SIN", [P, TW])
        QR = put("QR", [P, 2, TW])
        put = region(xh_off, x_end)
        UG = put("UG", [P, 32, CC])
        bt_off = xh_off + 4 * 32 * CC
        QS, KS, VS = put("QS", [P, 4, P]), put("KS", [P, 256]), put("VS", [P, 2, P])
        SB = put("SB", [P, 8, 256])
        PT = put("PT", [P, 8, 2, P])
        OS = put("OS", [P, 512])
        put = region(bt_off, x_end)
        BT = put("BT", [P, 2, 16, P])
        ER, EI = put("ER", [P, 16, NCK + 1]), put("EI", [P, 16, NCK + 1])
        HR, HI = put("HR", [P, 16, CC + 1]), put("HI", [P, 16, CC + 1])
        CM = place("CM", [P, 2, 16, P], offset=bt_off)
        TM = place("TM", [P, 32, P], offset=arena)
        TMR = place("TMR", [P, CK, 512], offset=hh_off)
        put = region(hh_off, hh_end)
        S1, S2 = put("S1", [P, 16, NCK]), put("S2", [P, 16, NCK])
        GY = place("GY", [P, 4, TW], offset=hh_off)
        put = region(arena + 4 * 4 * CK * CC, end)
        GH, GL = put("GH", [P, 4, TW], F32R), put("GL", [P, 4, TW], F32R)

        put = region(arena, end)
        SQ = put("SQ", [P, 2, TW])
        XQ = put("XQ", [P, 2, TW])
        KX = put("KX", [P, 2, 2, NMEM])
        VX = put("VX", [P, 2, 2, 2, P])
        PX, PXT, OX = put("PX", [P, 2, NMEM]), put("PXT", [P, 2, 2, P]), put("OX", [P, 2, NMEM])
        NX = put("NX", [P, 3, 4])
        put = region(arena + (2 * 4 * TW + 31) // 32 * 32, end)
        G = put("G", [P, 2, TW + 2])
        TAP = put("TAP", [P, 2, TW])
        ACTV, HID = put("ACTV", [P, TW]), put("HID", [P, TW])
        C2, RSTD2 = put("C2", [P, TW]), put("RSTD2", [P, TW])
        STF = put("STF", [P, 4, FT])
        FW = put("FW", [P, 2, 3])

        PS = ctx.enter_context(nc.psum_tensor("PS", [P, 8, 512], F32))

        def pset(s):
            return PS[:, 3 * s:3 * s + 3, 0:CW]

        def col(name, j=0, w=1):
            c = COLS[name][0] + j
            return COL[:, c:c + w]

        def tiled(x):
            return x.rearrange("p (c w) -> p c w", c=NCH)

        def chunk(x, c):
            return x[:, c * CW:(c + 1) * CW]

        ld = sem("first_loads")
        w_raw = [sem("w_raw_even"), sem("w_raw_odd")]
        w_hi, w_lo = sem("w_hi"), sem("w_lo")
        tile_done = sem("tile_done")
        kv_copy, kv_out = sem("kv_copy"), [sem(f"kv_out{x}") for x in range(4)]
        mem_hi, mem_lo = sem("mem_hi"), sem("mem_lo")
        par_ld, par_vec, par_pe, par_dma, par_act = (sem("par_" + x) for x in ("loads", "vec", "pe", "dma", "act"))
        x_ld, ready = sem("x_load"), sem("constants_ready")
        NORMS = ["inp", "x0", "f0", "c1", "x1", "f1", "fin"]
        n_act, n_sum, n_lo, n_tot, n_rs = {}, {}, {}, {}, {}
        for q in NORMS:
            n_act[q] = Steps(sem(f"norm_{q}_act"), [s + str(m) for m in range(KT) for s in (["sq", "hi"] if q != "fin" else ["sq"])])
            n_sum[q] = sem(f"norm_{q}_sum")
            n_lo[q] = sem(f"norm_{q}_lo")
            n_tot[q] = sem(f"norm_{q}_total")
            n_rs[q] = sem(f"norm_{q}_rstd")
        add = {q: sem(f"add_{q}") for q in ADDS}
        names = []
        for x in INP:
            if x == "Rk":
                names += ["sin_k", "cos_k", "rot_k", "rotS_k"]
            elif x[0] == "R":
                names += [s + x[1:] for s in ("sin_", "cos_", "rot_")]
            elif x[0] == "u":
                names += [x, x + "P", x + "S"]
            elif x != "VT":
                names += [x]
        ivec = Steps(sem("inp_vec"), names)
        iact = Steps(sem("inp_act"), ["VTa", "VTb"])
        zeroed, tm_made = sem("mixer_zeroed"), sem("tm_made")
        mix_ld, uj_out, ug_in = sem("mix_loads"), sem("u_to_dram"), sem("u_by_group")
        att_act = Steps(sem("att_act"), ["QS", "KS", "VS"] + [f"exp{h}" for h in range(8)] + ["esink", "PTa", "PTb", "YB"])
        att_vec = Steps(sem("att_vec"), ["s0", "s1", "s2", "s3", "max", "maxs", "neg", "ds", "sum", "rec", "PTc", "PTd", "OS"])
        att_pe = Steps(sem("att_pe"), ["S", "PTa", "PTb", "PTc", "PTd", "PV", "OT"])
        ssm_ld, cm_ld, ssm_pe, ssm_vec, ssm_act = (sem("ssm_" + x) for x in ("loads", "cm_load", "pe", "vec", "act"))
        y_out, y_in, small_out = sem("y_to_dram"), sem("y_back"), sem("new_state_out")
        four = range(4)
        glu_act = Steps(sem("glu_act"), [f"bh{j}" for j in four] + [s + str(j) for j in four for s in ("gp", "gs", "gh")]
                        + [s + str(j) for j in four for s in ("sig", "hi")])
        glu_vec = Steps(sem("glu_vec"), ["z"] + [f"bl{j}" for j in four] + [f"gl{j}" for j in four]
                        + [s + str(j) for j in four for s in ("mul", "lo")])
        xv, xa, xp, xld, xz = {}, {}, {}, {}, {}
        for l in (0, 1):
            xv[l] = Steps(sem(f"x{l}_vec"), ["q0", "q1"] + [f"{s}{t}" for k in range(12) for s, t in (
                ("mx", k), ("nm", k), ("rc", k - 2), ("ov", k - 2), ("lo", k - 3)) if 0 <= t < 9])
            xa[l] = Steps(sem(f"x{l}_act"), [f"{s}{t}" for k in range(12) for s, t in (
                ("ex", k), ("pt", k - 1), ("hi", k - 3)) if 0 <= t < 9])
            xp[l] = Steps(sem(f"x{l}_pe"), [f"{s}{t}" for k in range(12) for s, t in (
                ("S", k), ("T", k - 1), ("V", k - 2), ("O", k - 3)) if 0 <= t < 9])
            xld[l], xz[l] = sem(f"x{l}_kv_loads"), sem(f"x{l}_zeroed")
        fv, fa, fz = {}, {}, {}
        for l in (0, 1):
            fv[l] = Steps(sem(f"f{l}_vec"), ["gate0", "w0", "st0", "a0", "b0", "c0", "sm0", "hid0", "gate1", "lo0", "w1", "st1",
                                             "a1", "b1", "c1", "sm1", "hid1", "lo1"])
            fa[l] = Steps(sem(f"f{l}_act"), [s + str(e) for e in (0, 1) for s in ("silu", "na", "nb", "hi")])
            fz[l] = sem(f"f{l}_zeroed")
        cv = Steps(sem("c1_vec"), [s + str(e) for e in (0, 1) for s in ("cc", "zc", "w", "st", "a", "b", "c", "cr", "hid", "lo")])
        ca = Steps(sem("c1_act"), [s + str(e) for e in (0, 1) for s in ("na", "nb", "hi")])
        cz = sem("c1_zeroed")
        st_out = {q: sem(f"{q}_state_out") for q in ("f0", "c1", "f1")}
        outs = sem("outputs")
        fin = sem("fin_y")
        mark = {}

        block = ctx.enter_context(nc.Block())

        @block.vector
        def _(dv):
            def chain(s):
                count = [0]

                def do(ins):
                    count[0] += 1
                    ins.then_inc(s, 1)
                    dv.wait_ge(s, count[0])
                    return count[0]
                do.count = count
                return do

            do = chain(ready)
            do(dv.memset(EPSC[:], 1e-6))
            do(dv.memset(ONES[:], 1.0))
            dv.wait_ge(ld, 48)
            dv.wait_ge(mem_hi, 1)
            dv.tensor_tensor(ML[:], MR[:], MH[:].bitcast(F32), ALU.subtract).then_inc(mem_lo, 1)

            do = chain(par_vec)
            R = [AS[:, k, :] for k in range(24)]

            def cmul(out_r, out_i, ar, ai, br, bi, t1, t2, t3, t4):
                do(dv.tensor_tensor(t1, ar, br, ALU.mult))
                do(dv.tensor_tensor(t2, ai, bi, ALU.mult))
                do(dv.tensor_tensor(t3, ar, bi, ALU.mult))
                do(dv.tensor_tensor(t4, ai, br, ALU.mult))
                do(dv.tensor_tensor(out_r, t1, t2, ALU.subtract))
                do(dv.tensor_tensor(out_i, t3, t4, ALU.add))

            def exp(out, x, k, r, p):
                do(dv.tensor_scalar(k, x, 1.4426950408889634, ROUND, ALU.mult, ALU.add))
                do(dv.tensor_scalar(k, k, -ROUND, None, ALU.add))
                do(dv.scalar_tensor_tensor(out=r, in0=k, scalar=-LN2[0], in1=x, op0=ALU.mult, op1=ALU.add))
                do(dv.scalar_tensor_tensor(out=r, in0=k, scalar=-LN2[1], in1=r, op0=ALU.mult, op1=ALU.add))
                do(dv.tensor_scalar(p, r, CEXP[0], None, ALU.mult))
                for c in CEXP[1:]:
                    do(dv.scalar_tensor_tensor(out=p, in0=p, scalar=c, in1=r, op0=ALU.add, op1=ALU.mult))
                do(dv.tensor_scalar(k, k, -126.0, 127.0, ALU.max, ALU.min))
                do(dv.tensor_scalar(ASI[:], k, 127.0, 8388608.0, ALU.add, ALU.mult))
                do(dv.scalar_tensor_tensor(out=out, in0=p, scalar=1.0, in1=ASI[:].bitcast(F32), op0=ALU.add, op1=ALU.mult))

            dt, rho, th, cs, sn, k, r, z, p, sg = R[0:10]
            exp(dt, col("log_dt", 0, 16), k, r, p)
            do(dv.tensor_tensor(z, dt, col("a_re", 0, 16), ALU.mult))
            exp(rho, z, k, r, p)
            do(dv.tensor_tensor(th, dt, col("a_im", 0, 16), ALU.mult))
            do(dv.tensor_scalar(k, th, 0.3183098861837907, ROUND, ALU.mult, ALU.add))
            do(dv.tensor_scalar(k, k, -ROUND, None, ALU.add))
            do(dv.scalar_tensor_tensor(out=r, in0=k, scalar=-PI3[0], in1=th, op0=ALU.mult, op1=ALU.add))
            for c in PI3[1:]:
                do(dv.scalar_tensor_tensor(out=r, in0=k, scalar=-c, in1=r, op0=ALU.mult, op1=ALU.add))
            do(dv.tensor_scalar(sg, k, 0.5, ROUND, ALU.mult, ALU.add))
            do(dv.tensor_scalar(sg, sg, -ROUND, -2.0, ALU.add, ALU.mult))
            do(dv.tensor_tensor(sg, sg, k, ALU.add))
            do(dv.tensor_tensor(sg, sg, sg, ALU.mult))
            do(dv.tensor_scalar(sg, sg, -2.0, 1.0, ALU.mult, ALU.add))
            do(dv.tensor_tensor(z, r, r, ALU.mult))
            do(dv.tensor_scalar(p, z, CSIN[0], None, ALU.mult))
            for c in CSIN[1:]:
                do(dv.scalar_tensor_tensor(out=p, in0=p, scalar=c, in1=z, op0=ALU.add, op1=ALU.mult))
            do(dv.scalar_tensor_tensor(out=p, in0=p, scalar=1.0, in1=r, op0=ALU.add, op1=ALU.mult))
            do(dv.tensor_tensor(sn, p, sg, ALU.mult))
            do(dv.tensor_scalar(p, z, CCOS[0], None, ALU.mult))
            for c in CCOS[1:]:
                do(dv.scalar_tensor_tensor(out=p, in0=p, scalar=c, in1=z, op0=ALU.add, op1=ALU.mult))
            do(dv.scalar_tensor_tensor(out=cs, in0=p, scalar=1.0, in1=sg, op0=ALU.add, op1=ALU.mult))
            do(dv.memset(AR[:, :, 0], 1.0))
            do(dv.memset(AI[:, :, 0], 0.0))
            do(dv.tensor_tensor(AR[:, :, 1], rho, cs, ALU.mult))
            do(dv.tensor_tensor(AI[:, :, 1], rho, sn, ALU.mult))
            tt = [T[:].rearrange("p t i c -> p (t i c)") for T in (T1, T2)]
            tmp = [tt[0][:, 0:1024], tt[0][:, 1024:2048], tt[1][:, 0:1024], tt[1][:, 1024:2048]]

            def temps(w):
                return [x[:, 0:16 * w].rearrange("p (t w) -> p t w", t=16) for x in tmp]
            for w in (1, 2, 4):
                cmul(AR[:, :, w + 1:2 * w + 1], AI[:, :, w + 1:2 * w + 1], AR[:, :, 1:w + 1], AI[:, :, 1:w + 1],
                     AR[:, :, w:w + 1].to_broadcast([P, 16, w]), AI[:, :, w:w + 1].to_broadcast([P, 16, w]), *temps(w))
            do(dv.tensor_tensor(RHO8[:], rho, rho, ALU.mult))
            for _ in range(2):
                do(dv.tensor_tensor(RHO8[:], RHO8[:], RHO8[:], ALU.mult))
            for i in range(3):
                o = (ERP[:, :, 1], EIP[:, :, 1]) if i == 2 else (cs, sn)
                cmul(*o, cs, sn, cs, sn, *R[12:16])
            do(dv.memset(ERP[:, :, 0], 1.0))
            do(dv.memset(EIP[:, :, 0], 0.0))
            w = 1
            while w < NCK:
                cmul(ERP[:, :, w + 1:2 * w + 1], EIP[:, :, w + 1:2 * w + 1], ERP[:, :, 1:w + 1], EIP[:, :, 1:w + 1],
                     ERP[:, :, w:w + 1].to_broadcast([P, 16, w]), EIP[:, :, w:w + 1].to_broadcast([P, 16, w]), *temps(w))
                w *= 2
            lr, li = col("a_re", 0, 16), col("a_im", 0, 16)
            nr, den, d2, fr, fi, q1, q2 = R[10:17]
            ai = AI[:, :, 1]
            do(dv.tensor_scalar(nr, AR[:, :, 1], -1.0, None, ALU.add))
            do(dv.tensor_tensor(den, lr, lr, ALU.mult))
            do(dv.tensor_tensor(d2, li, li, ALU.mult))
            do(dv.tensor_tensor(den, den, d2, ALU.add))
            do(dv.reciprocal(den, den))
            do(dv.tensor_tensor(q1, nr, lr, ALU.mult))
            do(dv.tensor_tensor(q2, ai, li, ALU.mult))
            do(dv.tensor_tensor(fr, q1, q2, ALU.add))
            do(dv.tensor_tensor(fr, fr, den, ALU.mult))
            do(dv.tensor_tensor(q1, ai, lr, ALU.mult))
            do(dv.tensor_tensor(q2, nr, li, ALU.mult))
            do(dv.tensor_tensor(fi, q1, q2, ALU.subtract))
            do(dv.tensor_tensor(fi, fi, den, ALU.mult))
            dv.wait_ge(par_ld, 80)

            def b16(x):
                return x.unsqueeze(2).to_broadcast([P, 16, 16])
            cmul(BBR[:], BBI[:], b16(fr), b16(fi), BR[:], BI[:], *temps(16))
            do(dv.tensor_scalar(NCI[:], CI[:], -1.0, None, ALU.mult))

            def pw(x, j):
                return x[:, :, j:j + 8].unsqueeze(3).to_broadcast([P, 16, 8, 16])

            def ch(x):
                return x[:].unsqueeze(2).to_broadcast([P, 16, 8, 16])
            do(dv.tensor_tensor(PR[:], pw(AR, 0), ch(BBR), ALU.mult))
            do(dv.tensor_tensor(T1[:], pw(AI, 0), ch(BBI), ALU.mult))
            do(dv.tensor_tensor(PR[:], PR[:], T1[:], ALU.subtract))
            do(dv.tensor_tensor(PI[:], pw(AR, 0), ch(BBI), ALU.mult))
            do(dv.tensor_tensor(T1[:], pw(AI, 0), ch(BBR), ALU.mult))
            mark["P"] = do(dv.tensor_tensor(PI[:], PI[:], T1[:], ALU.add))
            do(dv.tensor_tensor(T1[:], pw(AR, 1), ch(CR), ALU.mult))
            do(dv.tensor_tensor(T3[:], pw(AI, 1), ch(CI), ALU.mult))
            do(dv.tensor_tensor(T1[:], T1[:], T3[:], ALU.subtract))
            do(dv.tensor_tensor(T2[:], pw(AI, 1), ch(CR), ALU.mult))
            do(dv.tensor_tensor(T3[:], pw(AR, 1), ch(CI), ALU.mult))
            do(dv.tensor_tensor(T2[:], T2[:], T3[:], ALU.add))
            mark["C"] = do(dv.tensor_scalar(T2[:], T2[:], -1.0, None, ALU.mult))
            dv.wait_ge(par_pe, 10)
            kr = KR[:].rearrange("p (t q h) -> p t q h", t=16, q=2)
            for q in range(2):
                do(dv.tensor_copy(kr[:, :, q, :], PS[:, q, 0:256].rearrange("p (t h) -> p t h", t=16)))
            mark["K"] = do(dv.tensor_tensor(KR[0:16, :], KR[0:16, :], DD[:], ALU.add))

            def norm_lo(q, m):
                dv.wait_ge(*n_act[q].at(f"hi{m}"))
                dv.scalar_tensor_tensor(out=XL[:, m, :], in0=X[:, m, :], scalar=col(GAIN[q], m), in1=XH[:, m, :].bitcast(F32),
                                        op0=ALU.mult, op1=ALU.subtract).then_inc(n_lo[q], 1)

            def last_adds(ph, first_tile, nxt):
                for m in range(KT + 1):
                    if m < KT:
                        dv.wait_ge(tile_done, first_tile + m)
                        dv.wait_ge(add[ph], ADDS[ph] - 2 * KT + m + 1)
                        dv.tensor_tensor(tiled(X[:, m, :]), tiled(X[:, m, :]), pset(m % 2), ALU.add).then_inc(add[ph], 1)
                    if m >= 1 and nxt != "fin":
                        norm_lo(nxt, m - 1)

            dv.wait_ge(kv_copy, 32)
            dv.wait_ge(tile_done, N0["inp"])
            for s in kv_out:
                dv.wait_ge(s, 16)
            dv.wait_ge(par_dma, 16 * 20)
            zero = chain(zeroed)
            for m in range(KT):
                norm_lo("inp", m)
            zero(dv.memset(UJ[:, :, :, NCK:NCK + 1], 0.0))
            zero(dv.memset(KB[:, 0:P], 0.0))
            zero(dv.memset(KB[:, 1312:1408], 0.0))
            zero(dv.memset(VB[:, 0, :], 0.0))
            mark["Z"] = zero(dv.memset(VB[:, 10, :], 0.0))
            for j, x in enumerate(INP):
                ps = pset(j % 2)
                if x != "VT":
                    dv.wait_ge(tile_done, T0["inp"] + j + 1)
                if j == 0:
                    dv.wait_ge(n_rs["inp"], 6)
                    dv.wait_ge(mix_ld, 96)
                if x in ("k", "q0", "q1", "q2", "q3"):
                    if x == "q1":
                        dv.wait_ge(*ivec.at("rotS_k"))
                    if x in ("q2", "q3"):
                        dv.wait_ge(*ivec.at({"q2": "rot_q0", "q3": "rot_q1"}[x]))
                    dv.tensor_tensor(tiled(QR[:, QSLOT[x], :]), ps, tiled(RSTD[:]), ALU.mult).then_inc(ivec.sem, 1)
                elif x == "v":
                    dv.tensor_tensor(tiled(VTT[:]), ps, tiled(RSTD[:]), ALU.mult).then_inc(ivec.sem, 1)
                elif x[0] == "u":
                    t = int(x[1])
                    dv.wait_ge(*(ivec.at("rotS_k") if t == 0 else ivec.at(f"u{t - 1}S")))
                    dv.tensor_tensor(tiled(LNV[:]), ps, tiled(RSTD[:]), ALU.mult).then_inc(ivec.sem, 1)
                    dv.wait_ge(*ivec.at(x))
                    dv.tensor_copy(UJ[:, t, :, 0:NCK], LNV[:, 0:SEQ].rearrange("p (c j) -> p j c", j=CK)).then_inc(ivec.sem, 1)
                    dv.tensor_copy(UJ[:, t, :, NCK + 1:CC], LNV[:, S0:TW].rearrange("p (c j) -> p j c", j=CK)).then_inc(ivec.sem, 1)
                elif x[0] == "R":
                    y = x[1:]
                    dst = LNV[:] if y == "k" else Q[:, int(y[1]), :]
                    qr = QR[:, QSLOT[y], :]
                    dv.tensor_tensor(tiled(dst), ps, tiled(SIN[:]), ALU.mult).then_inc(ivec.sem, 1)
                    dv.wait_ge(*ivec.at(y))
                    dv.tensor_tensor(qr, qr, COS[:], ALU.mult).then_inc(ivec.sem, 1)
                    dv.wait_ge(*ivec.at("cos_" + y))
                    if y == "k":
                        dv.tensor_tensor(KB[:, P:P + SEQ], LNV[:, 0:SEQ], qr[:, 0:SEQ], ALU.add).then_inc(ivec.sem, 1)
                        dv.tensor_tensor(KB[:, 1280:1312], LNV[:, S0:TW], qr[:, S0:TW], ALU.add).then_inc(ivec.sem, 1)
                    else:
                        dv.tensor_tensor(dst, dst, qr, ALU.add).then_inc(ivec.sem, 1)

            def att_tile(i, nq, kind):
                dv.wait_ge(*att_pe.at("S", i))
                for b in range(4):
                    dv.scalar_tensor_tensor(out=SB[0:nq, 2 * b:2 * b + 2, :], in0=PS[0:nq, b, :].rearrange("p (h k) -> p h k", h=2),
                                            scalar=0.125, in1=MASK[0:nq, kind, :].unsqueeze(1).to_broadcast([nq, 2, 256]),
                                            op0=ALU.mult, op1=ALU.add).then_inc(att_vec.sem, 1)
                dv.wait_ge(*att_vec.at("s3", i))
                dv.tensor_reduce(SMX[0:nq, 0:8], SB[0:nq], AX.X, ALU.max).then_inc(att_vec.sem, 1)
                dv.wait_ge(*att_vec.at("max", i))
                dv.tensor_tensor(SMX[0:nq, 0:8], SMX[0:nq, 0:8], col("sink", 0, 8)[0:nq], ALU.max).then_inc(att_vec.sem, 1)
                dv.wait_ge(*att_vec.at("maxs", i))
                dv.tensor_scalar(SMX[0:nq, 8:16], SMX[0:nq, 0:8], -1.0, None, ALU.mult).then_inc(att_vec.sem, 1)
                dv.tensor_tensor(SMX[0:nq, 40:48], col("sink", 0, 8)[0:nq], SMX[0:nq, 0:8], ALU.subtract).then_inc(att_vec.sem, 1)
                dv.wait_ge(*att_act.at("esink", i))
                dv.tensor_tensor(SMX[0:nq, 32:40], SMX[0:nq, 16:24], SMX[0:nq, 24:32], ALU.add).then_inc(att_vec.sem, 1)
                dv.wait_ge(*att_vec.at("sum", i))
                dv.reciprocal(SMX[0:nq, 48:56], SMX[0:nq, 32:40]).then_inc(att_vec.sem, 1)
                for b, nm in ((2, "PTc"), (3, "PTd")):
                    dv.wait_ge(*att_pe.at(nm, i))
                    dv.tensor_copy(PT[:, 2 * b:2 * b + 2, :, 0:nq],
                                   PS[:, 4 + b, :].rearrange("p (h k q) -> p h k q", h=2, k=2)[:, :, :, 0:nq]).then_inc(att_vec.sem, 1)
                dv.wait_ge(*att_pe.at("PV", i))
                dv.wait_ge(*att_vec.at("rec", i))
                dv.tensor_tensor(OS[0:nq, :].rearrange("p (j g d) -> p j g d", j=4, g=2), PS[0:nq, 0, :].rearrange("p (j g d) -> p j g d", j=4, g=2),
                                 SMX[0:nq, 48:56].rearrange("p (g j) -> p j g", g=2).unsqueeze(3).to_broadcast([nq, 4, 2, 64]),
                                 ALU.mult).then_inc(att_vec.sem, 1)

            att_tile(0, P, 0)
            with dv.Fori(1, 8) as i:
                att_tile(i, P, 1)
            att_tile(8, DEC, 2)

            dv.wait_ge(*att_act.at("YB", 8))
            dv.wait_ge(ssm_ld, 64)
            do = chain(ssm_vec)
            do(dv.memset(HR[:, :, 0], 0.0))
            do(dv.memset(HI[:, :, 0], 0.0))
            for k in range(32):
                dv.wait_ge(ssm_pe, k + 1)
                dv.tensor_copy((HR, HI)[k % 2][:, k // 2, 1:CC + 1], PS[:, k % 8, 0:CC]).then_inc(ssm_vec, 1)
            do.count[0] += 32
            dv.wait_ge(ssm_vec, do.count[0])
            dv.wait_ge(tm_made, 1)
            mult, plus, sub = ALU.mult, ALU.add, ALU.subtract
            for lo, w, init in ((1, NCK, None), (NCK + 2, DEC // CK, ("h0_re", "h0_im"))):
                hr, hi = HR[:, :, lo:lo + w], HI[:, :, lo:lo + w]
                er, ei = ER[:, :, 1:w + 1], EI[:, :, 1:w + 1]
                s1, s2 = S1[:, :, 0:w], S2[:, :, 0:w]
                do(dv.tensor_tensor(s1, er, hr, mult))
                do(dv.tensor_tensor(s2, ei, hi, mult))
                do(dv.tensor_tensor(s1, s1, s2, plus))
                do(dv.tensor_tensor(s2, er, hi, mult))
                do(dv.tensor_tensor(hr, ei, hr, mult))
                do(dv.tensor_tensor(s2, s2, hr, sub))
                for t in range(16):
                    for s, h, nm in ((S1, HR, 0), (S2, HI, 1)):
                        dv.tensor_tensor_scan(h[:, t, lo:lo + w], RHO8[:, t:t + 1].to_broadcast([P, w]), s[:, t, 0:w],
                                              col(init[nm], t) if init else 0.0, mult, plus).then_inc(ssm_vec, 1)
                do.count[0] += 32
                dv.wait_ge(ssm_vec, do.count[0])
                do(dv.tensor_tensor(s1, er, hr, mult))
                do(dv.tensor_tensor(s2, ei, hi, mult))
                do(dv.tensor_tensor(hi, er, hi, mult))
                do(dv.tensor_tensor(hr, ei, hr, mult))
                do(dv.tensor_tensor(hi, hi, hr, plus))
                do(dv.tensor_tensor(hr, s1, s2, sub))
            do(dv.tensor_copy(HR[:, :, NCK + 1], col("h0_re", 0, 16)))
            mark["H"] = do(dv.tensor_copy(HI[:, :, NCK + 1], col("h0_im", 0, 16)))
            for k, (h, c) in enumerate(((HR, NCK), (HI, NCK), (HR, CC), (HI, CC))):
                mark["S"] = do(dv.tensor_copy(SMALL[:, 16 * k:16 * k + 16], h[:, :, c]))

            dv.memset(GY[:, :, SEQ:S0], 0.0).then_inc(glu_vec.sem, 1)
            for j in range(4):
                dv.wait_ge(*glu_act.at(f"bh{j}"))
                dv.tensor_tensor(XL[:, 4 + j, :], Q[:, j, :], XH[:, 4 + j, :].bitcast(F32), ALU.subtract).then_inc(glu_vec.sem, 1)
            for j in range(4):
                dv.wait_ge(*glu_act.at(f"gh{j}"))
                dv.tensor_tensor(GL[:, j, :], GY[:, j, :], GH[:, j, :].bitcast(F32), ALU.subtract).then_inc(glu_vec.sem, 1)
            for j in range(4):
                dv.wait_ge(*glu_act.at(f"sig{j}"))
                dv.wait_ge(*glu_vec.at(f"gl{j}"))
                dv.tensor_tensor(GY[:, j, :], GY[:, j, :], LNV[:], ALU.mult).then_inc(glu_vec.sem, 1)
                dv.wait_ge(*glu_act.at(f"hi{j}"))
                dv.tensor_tensor(XL[:, j, :], GY[:, j, :], XH[:, j, :].bitcast(F32), ALU.subtract).then_inc(glu_vec.sem, 1)
            for g in range(3):
                for m in range(KT):
                    dv.wait_ge(tile_done, T0["out"] + 8 * g + m + 1)
                    if g:
                        dv.wait_ge(add["out"], 8 * g - 7 + m)
                    dv.tensor_tensor(tiled(X[:, m, :]), tiled(X[:, m, :]), pset(m % 2), ALU.add).then_inc(add["out"], 1)
            last_adds("out", T0["out"] + 25, "x0")

            def cross(l, prev, nxt):
                q, v, ac, te = f"x{l}", xv[l], xa[l], xp[l]
                t0 = T0[q]
                dv.memset(HH[:, :, SEQ:S0].bitcast(F32), 0.0).then_inc(xz[l], 1)
                dv.memset(HL[:, :, SEQ:S0].bitcast(F32), 0.0).then_inc(xz[l], 1)
                dv.wait_ge(xz[l], 2)

                def head(i, first):
                    for s in (0, 1):
                        dv.wait_ge(tile_done, i * 10 + (t0 + s + 1))
                        if first:
                            dv.wait_ge(n_rs[q], 6)
                        dv.tensor_tensor(tiled(XQ[:, s, :]), pset(s), tiled(RSTD[:]), ALU.mult).then_inc(v.sem, 1)
                    for k in range(12):
                        t = k
                        if t < 9:
                            nq = P if t < 8 else DEC
                            dv.wait_ge(*te.at(f"S{t}", i))
                            if t >= 2:
                                dv.wait_ge(*ac.at(f"ex{t - 2}", i))
                            dv.tensor_reduce(NX[0:nq, t % 3, 0:1], PS[0:nq, t % 2, 0:NMEM], AX.X, ALU.max).then_inc(v.sem, 1)
                            dv.wait_ge(*v.at(f"mx{t}", i))
                            dv.tensor_scalar(NX[0:nq, t % 3, 1:2], NX[0:nq, t % 3, 0:1], -1.0 / 16, None, ALU.mult).then_inc(v.sem, 1)
                        t = k - 2
                        if 0 <= t < 9:
                            nq = P if t < 8 else DEC
                            dv.wait_ge(*ac.at(f"ex{t}", i))
                            dv.reciprocal(NX[0:nq, t % 3, 3:4], NX[0:nq, t % 3, 2:3]).then_inc(v.sem, 1)
                            dv.wait_ge(*v.at(f"rc{t}", i))
                            dv.wait_ge(*te.at(f"V{t}", i))
                            dv.tensor_scalar(OX[0:nq, t % 2, :], PS[0:nq, 4 + t % 2, 0:NMEM], NX[0:nq, t % 3, 3:4], None, ALU.mult).then_inc(v.sem, 1)
                        t = k - 3
                        if 0 <= t < 9:
                            nq, c0 = (P, t * P) if t < 8 else (DEC, S0)
                            dv.wait_ge(*ac.at(f"hi{t}", i))
                            dv.tensor_tensor(HL[:, :, c0:c0 + nq], PS[:, 6 + t % 2, 0:NMEM].rearrange("p (d q) -> p d q", d=2)[:, :, 0:nq],
                                             HH[:, :, c0:c0 + nq].bitcast(F32), ALU.subtract).then_inc(v.sem, 1)
                    if isinstance(i, int) and i == HEADS - 1:
                        last_adds(q, t0 + 33, nxt)
                    elif first:
                        for m in range(KT):
                            dv.wait_ge(tile_done, t0 + 3 + m)
                            dv.tensor_tensor(tiled(X[:, m, :]), tiled(X[:, m, :]), pset(m % 2), ALU.add).then_inc(add[q], 1)
                    else:
                        for m in range(KT):
                            dv.wait_ge(tile_done, i * 10 + (t0 + 3 + m))
                            dv.wait_ge(add[q], i * 8 + (m - 7))
                            dv.tensor_tensor(tiled(X[:, m, :]), tiled(X[:, m, :]), pset(m % 2), ALU.add).then_inc(add[q], 1)

                head(0, True)
                with dv.Fori(1, HEADS - 1) as i:
                    head(i, False)
                head(HEADS - 1, False)

            def conv_taps(s, e, wname, width, sname, i, filled):
                w0, s0 = COLS[wname][0], COLS[sname][0]
                wc = COL[:, w0:w0 + 3 * width].rearrange("p (k f) -> p f k", k=3)
                sc = COL[:, s0:s0 + 2 * width].rearrange("p (k f) -> p f k", k=2)
                f = i * 2 + e
                dv.tensor_copy(FW[:, e, :], wc[:, bass.ds(f, 1), :].rearrange("p o k -> p (o k)")).then_inc(s.sem, 1)
                dv.wait_ge(*s.at(filled, i))
                dv.tensor_copy(G[:, e, S0:S0 + 2], sc[:, bass.ds(f, 1), :].rearrange("p o k -> p (o k)")).then_inc(s.sem, 1)
                dv.wait_ge(*s.at(f"st{e}", i))
                dv.tensor_scalar(TAP[:, e, :], G[:, e, 2:TW + 2], FW[:, e, 2:3], None, ALU.mult).then_inc(s.sem, 1)
                dv.wait_ge(*s.at(f"a{e}", i))
                dv.scalar_tensor_tensor(out=TAP[:, e, :], in0=G[:, e, 1:TW + 1], scalar=FW[:, e, 1:2], in1=TAP[:, e, :],
                                        op0=ALU.mult, op1=ALU.add).then_inc(s.sem, 1)
                dv.wait_ge(*s.at(f"b{e}", i))
                dv.scalar_tensor_tensor(out=TAP[:, e, :], in0=G[:, e, 0:TW], scalar=FW[:, e, 0:1], in1=TAP[:, e, :],
                                        op0=ALU.mult, op1=ALU.add).then_inc(s.sem, 1)

            def ffn(l, nxt):
                q, v, ac = f"f{l}", fv[l], fa[l]
                t0 = T0[q]
                dv.memset(G[:, :, 0:2], 0.0).then_inc(fz[l], 1)

                def gate(g, e, tile, first):
                    dv.wait_ge(tile_done, tile)
                    if first:
                        dv.wait_ge(n_rs[q], 6)
                    else:
                        dv.wait_ge(*ac.at(f"nb{e}", g - 1))
                    dv.tensor_tensor(tiled(G[:, e, 2:TW + 2]), pset(0), tiled(RSTD[:]), ALU.mult).then_inc(v.sem, 1)

                def taps(g, e):
                    conv_taps(v, e, f"cf_w{l}", FT, f"cf_s{l}", g, f"gate{e}")

                def scale(g, e):
                    dv.wait_ge(*ac.at(f"silu{e}", g))
                    dv.tensor_tensor(TAP[:, e, :], ACTV[:], RSTD[:], ALU.mult).then_inc(v.sem, 1)

                def hid(g, e, tile):
                    dv.wait_ge(tile_done, tile)
                    dv.wait_ge(*v.at(f"sm{e}", g))
                    dv.tensor_tensor(tiled(HID[:]), pset(1), tiled(TAP[:, e, :]), ALU.mult).then_inc(v.sem, 1)

                def low(g, e):
                    dv.wait_ge(*ac.at(f"hi{e}", g))
                    dv.tensor_tensor(HL[:, e, :], HID[:], HH[:, e, :].bitcast(F32), ALU.subtract).then_inc(v.sem, 1)

                def group(g, t, first):
                    gate(g, 0, t + 1, first)
                    taps(g, 0)
                    if not first:
                        for m in range(KT):
                            dv.wait_ge(tile_done, t + (2 + m))
                            if not isinstance(g, int):
                                dv.wait_ge(add[q], g * 8 + (m - 15))
                            dv.tensor_tensor(tiled(X[:, m, :]), tiled(X[:, m, :]), pset((1 + m) % 2), ALU.add).then_inc(add[q], 1)
                    o = 1 if first else 9
                    scale(g, 0)
                    hid(g, 0, t + (o + 1))
                    gate(g, 1, t + (o + 2), first)
                    low(g, 0)
                    taps(g, 1)
                    scale(g, 1)
                    hid(g, 1, t + (o + 3))
                    low(g, 1)

                dv.wait_ge(fz[l], 1)
                group(0, t0, True)
                group(1, t0 + 4, False)
                with dv.Fori(2, 11) as g:
                    group(g, g * 12 + (t0 - 8), False)
                last_adds(q, t0 + 125, nxt)

            def conv(nxt):
                q = "c1"
                t0 = T0[q]
                dv.memset(G[:, :, 0:2], 0.0).then_inc(cz, 1)
                dv.wait_ge(n_rs[q], 6)
                dv.tensor_tensor(RSTD2[:], RSTD[:], RSTD[:], ALU.mult).then_inc(cz, 1)
                dv.wait_ge(cz, 2)

                def tile(g, e, tc, tz, tb, pc, first, between=None):
                    dv.wait_ge(tile_done, tc)
                    if e == 1:
                        dv.wait_ge(*cv.at("zc0", g))
                    elif not first:
                        dv.wait_ge(*cv.at("zc1", g - 1))
                    dv.tensor_tensor(tiled(C2[:]), pset(pc[0]), tiled(RSTD2[:]), ALU.mult).then_inc(cv.sem, 1)
                    if between:
                        between()
                    dv.wait_ge(tile_done, tz)
                    dv.wait_ge(*cv.at(f"cc{e}", g))
                    if not first:
                        dv.wait_ge(*ca.at(f"nb{e}", g - 1))
                    dv.tensor_tensor(tiled(G[:, e, 2:TW + 2]), pset(pc[1]), tiled(C2[:]), ALU.mult).then_inc(cv.sem, 1)
                    conv_taps(cv, e, "cm_w", KT, "cm_s", g, f"zc{e}")
                    dv.wait_ge(*cv.at(f"c{e}", g))
                    dv.tensor_tensor(TAP[:, e, :], TAP[:, e, :], RSTD[:], ALU.mult).then_inc(cv.sem, 1)
                    dv.wait_ge(tile_done, tb)
                    dv.wait_ge(*cv.at(f"cr{e}", g))
                    dv.tensor_tensor(tiled(HID[:]), pset(pc[2]), tiled(TAP[:, e, :]), ALU.mult).then_inc(cv.sem, 1)
                    dv.wait_ge(*ca.at(f"hi{e}", g))
                    dv.tensor_tensor(HL[:, e, :], HID[:], HH[:, e, :].bitcast(F32), ALU.subtract).then_inc(cv.sem, 1)

                tile(0, 0, t0 + 1, t0 + 2, t0 + 3, (0, 1, 0), True)
                tile(0, 1, t0 + 4, t0 + 5, t0 + 6, (1, 0, 1), True)

                def group(g, t):
                    def between():
                        for m in range(KT):
                            dv.wait_ge(tile_done, t + (2 + m))
                            if not isinstance(g, int):
                                dv.wait_ge(add[q], g * 8 + (m - 15))
                            dv.tensor_tensor(tiled(X[:, m, :]), tiled(X[:, m, :]), pset((1 + m) % 2), ALU.add).then_inc(add[q], 1)
                    tile(g, 0, t + 1, t + 10, t + 11, (0, 1, 0), False, between)
                    tile(g, 1, t + 12, t + 13, t + 14, (1, 0, 1), False)

                group(1, t0 + 6)
                with dv.Fori(2, 4) as g:
                    group(g, g * 14 + (t0 - 8))
                last_adds(q, t0 + 49, nxt)

            cross(0, "out", "f0")
            ffn(0, "c1")
            conv("x1")
            cross(1, "c1", "f1")
            ffn(1, "fin")
            dv.wait_ge(n_rs["fin"], 6)
            dv.wait_ge(add["f1"], 88)
            for m in range(KT):
                dv.scalar_tensor_tensor(out=X[:, m, :], in0=X[:, m, :], scalar=col("g_fin", m), in1=RSTD[:],
                                        op0=ALU.mult, op1=ALU.mult).then_inc(fin, 1)

        @block.tensor
        def _(pe):
            def mms(out, h, l, rh, rl, start, stop):
                pe.matmul(out, h, rh, start=start, stop=False)
                pe.matmul(out, h, rl, start=False, stop=False)
                return pe.matmul(out, l, rh, start=False, stop=stop)

            def tile_a(n, s, pset_i, kt=KT, lhs=None, H=XH, L=XL, wait_lo=True):
                if wait_lo:
                    pe.wait_ge(w_lo, n + 1)
                for k in range(kt):
                    wh, wl = lhs(k) if lhs else (WH[:, s, k * P:(k + 1) * P], WL[:, s, k * P:(k + 1) * P])
                    for c in range(NCH):
                        mm = mms(PS[:, 3 * pset_i + c, 0:CW], wh, wl, chunk(H[:, k, :], c), chunk(L[:, k, :], c),
                                 k == 0, k == kt - 1)
                mm.then_inc(tile_done, 1)

            def block_b(n, s, marks, H=HH, L=HL, k0=0):
                pe.wait_ge(w_lo, n + 1)
                for o in range(4):
                    pe.wait_ge(*marks[o])
                    def lhs(k):
                        return (WH[:, s, k * 512 + o * P:k * 512 + (o + 1) * P], WL[:, s, k * 512 + o * P:k * 512 + (o + 1) * P])
                    for k in range(2):
                        wh, wl = lhs(k)
                        for c in range(NCH):
                            mm = mms(PS[:, 3 * (o % 2) + c, 0:CW], wh, wl, chunk(H[:, k0 + k, :], c), chunk(L[:, k0 + k, :], c),
                                     k == 0, k == 1)
                    mm.then_inc(tile_done, 1)

            def norm_total(q):
                pe.wait_ge(n_sum[q], KT)
                for c in range(NCH):
                    if c == 2:
                        pe.wait_ge(n_rs[q], 1)
                    pe.matmul(PS[:, 6 + c % 2, 0:CW], ONES[:], chunk(RSTD[:], c), start=True, stop=True).then_inc(n_tot[q], 1)

            pe.wait_ge(mem_lo, 1)
            pe.wait_ge(mem_hi, 1)
            for part in range(4):
                def pair(i, first=False):
                    for s in (0, 1):
                        n = i * 2 + (8 * part + s)
                        pe.wait_ge(w_lo, n + 1)
                        if not first:
                            pe.wait_ge(kv_copy, n - 1)
                        for mt in range(1 + part % 2):
                            for k in range(KT):
                                wh, wl = WH[:, s, k * P:(k + 1) * P], WL[:, s, k * P:(k + 1) * P]
                                if part % 2 == 0:
                                    mm = mms(PS[:, 3 * s, 0:NMEM], wh, wl, MH[:, k, :], ML[:, k, :], k == 0, k == KT - 1)
                                else:
                                    o = slice(mt * P, (mt + 1) * P)
                                    mm = mms(PS[:, 3 * s, o], MH[:, k, o], ML[:, k, o], wh, wl, k == 0, k == KT - 1)
                        mm.then_inc(tile_done, 1)
                if part == 0:
                    pair(0, True)
                with pe.Fori(1 if part == 0 else 0, 4) as i:
                    pair(i)
            for ri in range(2):
                if ri == 0:
                    pe.wait_ge(par_vec, mark["P"])
                for tq in range(4):
                    b = 6 + (4 * ri + tq) % 2
                    if 4 * ri + tq >= 2:
                        pe.wait_ge(par_act, 4 * ri + tq - 1)
                    for t in range(4):
                        mm = pe.transpose(PS[:, b, t * P:(t + 1) * P], (PR, PI)[ri][:, 4 * tq + t].rearrange("p i c -> p (i c)"), IDENT[:])
                    mm.then_inc(par_pe, 1)
            pe.wait_ge(kv_copy, 32)
            for q in range(2):
                for t in range(16):
                    r = slice(64 * q, 64 * q + 64)
                    o = PS[:, q, 16 * t:16 * t + 16]
                    pe.matmul(o, PR[r, t].rearrange("p i c -> p (i c)"), CR[r, t, :], start=True, stop=False, skip_group_check=True)
                    mm = pe.matmul(o, PI[r, t].rearrange("p i c -> p (i c)"), NCI[r, t, :], start=False, stop=True, skip_group_check=True)
                mm.then_inc(par_pe, 1)

            pe.wait_ge(par_vec, mark["K"])
            evac = {x: iact.at("VTb") if x == "VT" else ivec.at("sin_" + x[1:] if x[0] == "R" else x) for x in INP}
            n = N0["inp"]
            for j, x in enumerate(INP):
                s = j % 2
                if j >= 2:
                    pe.wait_ge(*evac[INP[j - 2]])
                if x == "VT":
                    pe.wait_ge(*ivec.at("v"))
                    for t in range(9):
                        w = P if t < 8 else DEC
                        c0 = t * P if t < 8 else S0
                        mm = pe.transpose(PS[0:w, 3 * s + t // 4, (t % 4) * P:(t % 4 + 1) * P], VTT[:, c0:c0 + w], IDENT[:])
                    mm.then_inc(tile_done, 1)
                elif x[0] == "R":
                    pe.wait_ge(*ivec.at(x[1:]))
                    if x == "Rk":
                        pe.wait_ge(mix_ld, 96)
                    for c in range(NCH):
                        mm = pe.matmul(PS[:, 3 * s + c, 0:CW], ROT[:], chunk(QR[:, QSLOT[x[1:]], :], c), start=True, stop=True)
                    mm.then_inc(tile_done, 1)
                else:
                    if j == 0:
                        pe.wait_ge(n_lo["inp"], KT)
                    tile_a(n, n % 2, s)
                    n += 1
                    if j == 0:
                        norm_total("inp")

            pe.wait_ge(*ivec.at("rot_q3"))

            def att_tile(i, nq, first=False):
                pe.wait_ge(*att_act.at("VS", i))
                if not first:
                    pe.wait_ge(*att_act.at("YB", i - 1))
                for g in range(2):
                    r = slice(64 * g, 64 * g + 64)
                    for j in range(4):
                        mm = pe.matmul(PS[0:nq, 2 * g + j // 2, (j % 2) * 256:(j % 2) * 256 + 256], QS[r, j, 0:nq], KS[r, :],
                                       start=True, stop=True)
                mm.then_inc(att_pe.sem, 1)
                pe.wait_ge(*att_act.at("exp7", i))
                for b in range(4):
                    for h in (2 * b, 2 * b + 1):
                        for kt in range(2):
                            mm = pe.transpose(PS[:, 4 + b, ((h % 2) * 2 + kt) * P:((h % 2) * 2 + kt) * P + nq],
                                              SB[0:nq, h, kt * P:(kt + 1) * P], IDENT[0:nq, 0:nq])
                    mm.then_inc(att_pe.sem, 1)
                pe.wait_ge(*att_vec.at("PTd", i))
                pe.wait_ge(*att_act.at("PTb", i))
                for h in range(8):
                    for kt in range(2):
                        mm = pe.matmul(PS[0:nq, 0, (h % 4) * P + (h // 4) * 64:(h % 4) * P + (h // 4) * 64 + 64], PT[:, h, kt, 0:nq], VS[:, kt, (h // 4) * 64:(h // 4) * 64 + 64],
                                       start=(kt == 0), stop=(kt == 1), skip_group_check=True)
                mm.then_inc(att_pe.sem, 1)
                pe.wait_ge(*att_vec.at("OS", i))
                for j in range(4):
                    mm = pe.transpose(PS[:, 1, j * P:j * P + nq], OS[0:nq, j * P:(j + 1) * P], IDENT[0:nq, 0:nq])
                mm.then_inc(att_pe.sem, 1)

            att_tile(0, P, True)
            with pe.Fori(1, 8) as i:
                att_tile(i, P)
            att_tile(8, DEC)

            pe.wait_ge(*att_act.at("YB", 8))
            pe.wait_ge(ssm_ld, 64)
            pe.wait_ge(ug_in, 128)
            for t in range(16):
                for ri in range(2):
                    k = 2 * t + ri
                    b = k % 8
                    if k >= 8:
                        pe.wait_ge(ssm_vec, k - 5)
                    for q in range(2):
                        mm = pe.matmul(PS[64 * q:64 * q + 64, b, 0:CC], BT[:, ri, t, 64 * q:64 * q + 64], UG[:, 2 * t + q, :],
                                       start=True, stop=True)
                    mm.then_inc(ssm_pe, 1)
            pe.wait_ge(ssm_vec, mark["H"])
            pe.wait_ge(cm_ld, 16)
            for g in range(32):
                t, q = g // 2, g % 2
                b = g % 8
                if g >= 8:
                    pe.wait_ge(ssm_act, g - 7)
                r = slice(64 * q, 64 * q + 64)
                o = PS[:, b, 0:CC]
                pe.matmul(o, TM[:, g, :], UG[:, g, :], start=True, stop=False)
                pe.matmul(o, CM[r, 0, t, :], HR[r, t, 0:CC], start=False, stop=False)
                pe.matmul(o, CM[r, 1, t, :], HI[r, t, 0:CC], start=False, stop=True).then_inc(ssm_pe, 1)
            pe.wait_ge(ssm_act, 32)

            n = N0["glu"]
            for o in range(4):
                s = o // 2
                if o == 0:
                    pe.wait_ge(*glu_vec.at("gl3"))
                if o >= 2:
                    pe.wait_ge(*glu_act.at(f"sig{o - 2}"))
                tile_a(n + s, s, o % 2, kt=4, H=GH, L=GL,
                       lhs=lambda k: (WH[:, s, k * 256 + (o % 2) * P:k * 256 + (o % 2) * P + P],
                                      WL[:, s, k * 256 + (o % 2) * P:k * 256 + (o % 2) * P + P]))
            n = N0["out"]
            pe.wait_ge(*glu_vec.at("lo3"))
            for g in range(4):
                for b in range(2):
                    marks = []
                    for o in range(4):
                        c = 8 * g + 4 * b + o
                        marks.append(glu_act.at(f"sig{2 + c}") if c < 2 else (add["out"], c - 1))
                    block_b(n, n % 2, marks, H=XH, L=XL, k0=2 * g)
                    n += 1

            def cross(l):
                q = f"x{l}"
                n = N0[q]

                def head(i, first):
                    for s in (0, 1):
                        pe.wait_ge(w_lo, i * 4 + (n + s + 1))
                        if first:
                            pe.wait_ge(add["out" if l == 0 else "c1"], 31 + s)
                            if s == 0:
                                pe.wait_ge(n_lo[q], KT)
                        else:
                            pe.wait_ge(add[q], i * 8 + (s - 1))
                        tile_a(0, s, s, wait_lo=False)
                        if first and s == 0:
                            norm_total(q)
                    pe.wait_ge(*xv[l].at("q1", i))
                    pe.wait_ge(xld[l], i * 64 + 64)
                    if first:
                        pe.wait_ge(n_rs[q], 6)
                    for k in range(12):
                        t = k
                        if t < 9:
                            nq, c0, st = (P, t * P, 0) if t < 8 else (DEC, S0, 1)
                            if t >= 2:
                                pe.wait_ge(*xa[l].at(f"ex{t - 2}", i))
                            for d in range(2):
                                mm = pe.matmul(PS[0:nq, t % 2, 0:NMEM], XQ[:, d, c0:c0 + nq], KX[:, st, d, :], start=(d == 0), stop=(d == 1))
                            mm.then_inc(xp[l].sem, 1)
                        t = k - 1
                        if 0 <= t < 9:
                            nq = P if t < 8 else DEC
                            pe.wait_ge(*xa[l].at(f"ex{t}", i))
                            if t == 8:
                                pe.nop(nofuse=True)
                            for m in range(2):
                                mm = pe.transpose(PS[:, 2 + t % 2, m * P:m * P + nq], PX[0:nq, t % 2, m * P:(m + 1) * P], IDENT[0:nq, 0:nq])
                            mm.then_inc(xp[l].sem, 1)
                        t = k - 2
                        if 0 <= t < 9:
                            nq, st = (P, 0) if t < 8 else (DEC, 1)
                            pe.wait_ge(*xa[l].at(f"pt{t}", i))
                            if t >= 2:
                                pe.wait_ge(*xv[l].at(f"ov{t - 2}", i))
                            for m in range(2):
                                mm = pe.matmul(PS[0:nq, 4 + t % 2, 0:NMEM].rearrange("p (d e) -> p d e", d=2), PXT[:, t % 2, m, 0:nq],
                                               VX[:, st, :, m, :], start=(m == 0), stop=(m == 1))
                            mm.then_inc(xp[l].sem, 1)
                        t = k - 3
                        if 0 <= t < 9:
                            nq = P if t < 8 else DEC
                            pe.wait_ge(*xv[l].at(f"ov{t}", i))
                            if t == 8:
                                pe.nop(nofuse=True)
                            for d in range(2):
                                mm = pe.transpose(PS[:, 6 + t % 2, d * P:d * P + nq], OX[0:nq, t % 2, d * P:(d + 1) * P], IDENT[0:nq, 0:nq])
                            mm.then_inc(xp[l].sem, 1)
                    pe.wait_ge(*xv[l].at("lo8", i))
                    for b in range(2):
                        marks = [xv[l].at("ov8", i) if b == 0 and o < 2 else (add[q], i * 8 + (4 * b + o - 1)) for o in range(4)]
                        block_b(i * 4 + (n + 2 + b), b, marks)

                head(0, True)
                with pe.Fori(1, HEADS) as i:
                    head(i, False)

            def a_tile(n, s, ps, free, wait_x=None, q=None):
                pe.wait_ge(w_lo, n + 1)
                pe.wait_ge(*free)
                if wait_x:
                    pe.wait_ge(n_lo[wait_x], KT)
                tile_a(0, s, ps, wait_lo=False)
                if wait_x:
                    norm_total(wait_x)

            def down(nb, s0, ready, free, p0):
                pe.wait_ge(*ready)
                for b in range(2):
                    pe.wait_ge(w_lo, nb + (b + 1))
                    for o in range(4):
                        if free(4 * b + o):
                            pe.wait_ge(*free(4 * b + o))
                        down_tile((s0 + b) % 2, o, (p0 + o) % 2)

            def ffn(l):
                q, v = f"f{l}", fv[l]
                n = N0[q]
                before = add[f"x{l}"]
                a_tile(n, 0, 0, (before, 31), wait_x=q)
                a_tile(n + 1, 1, 1, (before, 32))
                a_tile(n + 2, 0, 0, v.at("gate0"))
                a_tile(n + 3, 1, 1, v.at("hid0"))
                with pe.Fori(1, 11) as g:
                    nb = g * 6 + (n - 2)
                    a_tile(nb, 0, 0, v.at("gate1", g - 1))
                    down(nb + 1, 1, v.at("lo1", g - 1),
                         lambda j: None if j == 0 else v.at("gate0", g) if j == 1 else (add[q], g * 8 + (j - 9)), 1)
                    a_tile(nb + 3, 1, 1, (add[q], g * 8 - 1))
                    a_tile(nb + 4, 0, 0, (add[q], g * 8))
                    a_tile(nb + 5, 1, 1, v.at("hid0", g))
                down(n + 64, 0, v.at("lo1", 10),
                     lambda j: None if j < 2 else (add[q], 79 + j), 0)

            def down_tile(s, o, ps):
                for k in range(2):
                    w = slice(k * 512 + o * P, k * 512 + (o + 1) * P)
                    for c in range(NCH):
                        mm = mms(PS[:, 3 * ps + c, 0:CW], WH[:, s, w], WL[:, s, w], chunk(HH[:, k, :], c), chunk(HL[:, k, :], c),
                                 k == 0, k == 1)
                mm.then_inc(tile_done, 1)

            def conv():
                q, n = "c1", N0["c1"]
                a_tile(n, 0, 0, (add["f0"], 87), wait_x=q)
                a_tile(n + 1, 1, 1, (add["f0"], 88))
                for b, x in enumerate(("cc0", "zc0", "hid0", "cc1")):
                    a_tile(n + 2 + b, b % 2, b % 2, cv.at(x))
                with pe.Fori(1, 4) as g:
                    nb = g * 8 + (n - 2)
                    a_tile(nb, 0, 0, cv.at("zc1", g - 1))
                    down(nb + 1, 1, cv.at("lo1", g - 1),
                         lambda j: None if j == 0 else cv.at("cc0", g) if j == 1 else (add[q], g * 8 + (j - 9)), 1)
                    a_tile(nb + 3, 1, 1, (add[q], g * 8 - 1))
                    a_tile(nb + 4, 0, 0, (add[q], g * 8))
                    for b, x in enumerate(("zc0", "hid0", "cc1")):
                        a_tile(nb + (5 + b), (1 + b) % 2, (1 + b) % 2, cv.at(x, g))
                down(n + 30, 0, cv.at("lo1", 3),
                     lambda j: None if j < 2 else (add[q], 23 + j), 0)

            cross(0)
            ffn(0)
            conv()
            cross(1)
            ffn(1)
            norm_total("fin")

        @block.sync
        def _(sp):
            sp.dma_start(MR[:], a["memT"]).then_inc(ld, 16)
            sp.dma_start(COL[:], a["cols"]).then_inc(ld, 16)
            sp.dma_start(IDENT[:], a["ident"]).then_inc(ld, 16)
            for n in (0, 1):
                sp.dma_start(WR[:, n, :], a["w"][n]).then_inc(w_raw[n], 16)
            with sp.Fori(1, NBLOCKS // 2) as i:
                for s in (0, 1):
                    sp.wait_ge(w_lo, i * 2 + (s - 1))
                    sp.dma_start(WR[:, s, :], a["w"][bass.ds(i * 2 + s, 1)].rearrange("o p n -> (o p) n")).then_inc(w_raw[s], 16)
            for m in range(KT):
                sp.wait_ge(fin, m + 1)
                sp.dma_start(a["y"][:, m, :], X[:, m, :]).then_inc(outs, 16)
            sp.wait_ge(outs, 16 * KT)

        @block.gpsimd
        def _(pool):
            def lo_block(n, s):
                pool.wait_ge(w_hi, n + 1)
                pool.tensor_tensor(WL[:, s, :], WR[:, s, :], WH[:, s, :].bitcast(F32), ALU.subtract).then_inc(w_lo, 1)

            def sum_squares(q, m):
                pool.wait_ge(*n_act[q].at(f"sq{m}"))
                sq = QR[:, m % 2, :] if q == "inp" else SQ[:, m % 2, :]
                if m == 0:
                    pool.tensor_copy(RSTD[:], sq).then_inc(n_sum[q], 1)
                else:
                    pool.wait_ge(n_sum[q], m)
                    pool.tensor_tensor(RSTD[:], RSTD[:], sq, ALU.add).then_inc(n_sum[q], 1)

            done = [0]

            def blocks(upto):
                lo, hi = done[0] // 2, upto // 2
                with pool.Fori(lo, hi) as i:
                    for s in (0, 1):
                        lo_block(i * 2 + s, s)
                done[0] = upto

            blocks(N0["inp"] + 2)
            for m in range(KT):
                sum_squares("inp", m)
            for ph, nxt in (("out", "x0"), ("x0", "f0"), ("f0", "c1"), ("c1", "x1"), ("x1", "f1"), ("f1", "fin")):
                start = N0[nxt] if nxt != "fin" else NBLOCKS
                blocks(start)
                for b in range(2):
                    for m in range(4):
                        sum_squares(nxt, 4 * b + m)
                    if nxt != "fin":
                        lo_block(start + b, b)
                done[0] = start + 2

        @block.scalar
        def _(act):
            def hi_block(n, s):
                act.wait_ge(w_raw[s], (n - s) * 8 + 16)
                act.activation(WH[:, s, :], WR[:, s, :], ACT.Copy).then_inc(w_hi, 1)

            def step(n, s, tiles):
                act.wait_ge(tile_done, tiles)
                hi_block(n + 2, s)

            def norm_tile(q, m, x_final):
                act.wait_ge(*x_final)
                if m >= 2:
                    act.wait_ge(n_sum[q], m - 1)
                sq = QR[:, m % 2, :] if q == "inp" else SQ[:, m % 2, :]
                act.activation(sq, X[:, m, :], ACT.Square).then_inc(n_act[q].sem, 1)
                if q != "fin":
                    act.activation(XH[:, m, :], X[:, m, :], ACT.Copy, scale=col(GAIN[q], m)).then_inc(n_act[q].sem, 1)

            def rstd(q):
                for c in range(NCH):
                    act.wait_ge(n_tot[q], c + 1)
                    act.activation(chunk(LNV[:], c), PS[:, 6 + c % 2, 0:CW], ACT.Ln, bias=EPSC[:], scale=1.0 / D).then_inc(n_rs[q], 1)
                act.wait_ge(n_rs[q], 3)
                for c in range(NCH):
                    act.activation(chunk(RSTD[:], c), chunk(LNV[:], c), ACT.Exp, scale=-0.5).then_inc(n_rs[q], 1)

            act.wait_ge(ld, 48)
            act.activation(MH[:], MR[:], ACT.Copy).then_inc(mem_hi, 1)
            hi_block(0, 0)
            hi_block(1, 1)
            for t, nm in ((BR, "b_re"), (BI, "b_im"), (CR, "c_re"), (CI, "c_im"), (DD, "d_diag")):
                act.dma_start(t[:], a[nm]).then_inc(par_ld, 16)
            act.dma_start(X[:], a["x"]).then_inc(x_ld, 16)
            for part in range(4):
                if part >= 2:
                    act.wait_ge(kv_out[part - 2], 16)
                with act.Fori(0, 4) as i:
                    for s in (0, 1):
                        n = i * 2 + (8 * part + s)
                        step(n, s, n + 1)
                        act.activation(KVS[:, part % 2, bass.ds(i * 2 + s, 1), :].rearrange("p o m -> p (o m)"),
                                       PS[:, 3 * s, 0:NMEM], ACT.Copy).then_inc(kv_copy, 1)
                act.wait_ge(kv_copy, 8 * part + 8)
                act.dma_start(a["memkv"][part], KVS[:, part % 2].rearrange("p b m -> p (b m)")).then_inc(kv_out[part], 16)
            for k in range(8):
                act.wait_ge(par_pe, k + 1)
                act.activation(BTP[:, k // 4, 4 * (k % 4):4 * (k % 4) + 4, :].rearrange("p t c -> p (t c)"),
                               PS[:, 6 + k % 2, :], ACT.Copy).then_inc(par_act, 1)
            act.wait_ge(par_act, 8)
            act.dma_start(a["bt"], BTP[:]).then_inc(par_dma, 16)
            act.wait_ge(par_vec, mark["K"])
            act.dma_start(a["er"], ERP[:]).then_inc(par_dma, 16)
            act.dma_start(a["ei"], EIP[:]).then_inc(par_dma, 16)
            act.dma_start(a["cm"][:, 0], T1[:].rearrange("p t j h -> p (t j h)")).then_inc(par_dma, 16)
            act.dma_start(a["cm"][:, 1], T2[:].rearrange("p t j h -> p (t j h)")).then_inc(par_dma, 16)
            for j in range(8):
                r = 16 * (7 - j)
                act.dma_start(a["tm"][r:P, j, :], KR[0:P - r, :]).then_inc(par_dma, 16)
                if r:
                    act.dma_start(a["tm"][0:r, j, :], a["zeros"][0:r, :]).then_inc(par_dma, 16)
            act.wait_ge(par_dma, 16 * 20)
            for s in kv_out:
                act.wait_ge(s, 16)

            for t, nm in ((COS[:], "cos"), (SIN[:], "sin"), (ROT[:], "rot"), (MASK[:], "mask")):
                act.dma_start(t, a[nm]).then_inc(mix_ld, 16)
            act.dma_start(KB[:, 1152:1280], a["past_k"]).then_inc(mix_ld, 16)
            act.dma_start(VB[:, 9, :], a["past_v"]).then_inc(mix_ld, 16)
            act.wait_ge(ready, 2)
            for m in range(KT):
                norm_tile("inp", m, (x_ld, 16))
            n = N0["inp"]
            for j, x in enumerate(INP):
                if x in INP_BLOCKS:
                    step(n, n % 2, T0["inp"] + j + 1)
                    n += 1
                if j == 0:
                    rstd("inp")
                if x == "VT":
                    s = j % 2
                    act.wait_ge(tile_done, T0["inp"] + j + 1)
                    act.wait_ge(zeroed, mark["Z"])
                    act.activation(VB[:, 1:9, :].rearrange("p (b s) c -> p b (s c)", b=2), PS[:, 3 * s:3 * s + 2, :], ACT.Copy).then_inc(iact.sem, 1)
                    act.activation(VB[0:DEC, 10, :], PS[0:DEC, 3 * s + 2, 0:P], ACT.Copy).then_inc(iact.sem, 1)
                if x == "q1":
                    act.wait_ge(*ivec.at("u3S"))
                    act.dma_start(a["uj"].rearrange("(t g) c j k -> (g c) t (j k)", g=8), UJ[:].rearrange("p t j c -> p t (j c)")).then_inc(uj_out, 16)
            act.wait_ge(*ivec.at("rot_q3"))
            act.wait_ge(*iact.at("VTb"))
            act.dma_start(a["k_new"][:, 0:P], KB[:, 1024:1152]).then_inc(small_out, 16)
            act.dma_start(a["k_new"][:, P:P + DEC], KB[:, 1280:1312]).then_inc(small_out, 16)
            act.dma_start(a["v_new"][:, 0:P], VTT[:, SEQ - P:SEQ]).then_inc(small_out, 16)
            act.dma_start(a["v_new"][:, P:P + DEC], VTT[:, S0:TW]).then_inc(small_out, 16)
            act.wait_ge(uj_out, 16)
            act.wait_ge(tile_done, T0["glu"])
            for j in range(CK):
                act.dma_start(UG[16 * (7 - j):16 * (7 - j) + 16, :, :],
                              a["uj"].rearrange("g c j k -> j c g k")[j]).then_inc(ug_in, 16)

            def att_tile(i, nq, qc, kc, vb, first=False):
                if not first:
                    act.wait_ge(*att_act.at("YB", i - 1))
                    act.nop(nofuse=True)
                act.activation(QS[:, :, 0:nq], qc, ACT.Copy).then_inc(att_act.sem, 1)
                act.activation(KS[:], kc, ACT.Copy).then_inc(att_act.sem, 1)
                act.activation(VS[:], vb, ACT.Copy).then_inc(att_act.sem, 1)
                act.wait_ge(*att_vec.at("ds", i))
                for h in range(8):
                    act.activation(SB[0:nq, h, :], SB[0:nq, h, :], ACT.Exp, bias=SMX[0:nq, 8 + h:9 + h],
                                   accum_out=SMX[0:nq, 16 + h:17 + h]).then_inc(att_act.sem, 1)
                act.activation(SMX[0:nq, 24:32], SMX[0:nq, 40:48], ACT.Exp).then_inc(att_act.sem, 1)
                for b, nm in enumerate(("PTa", "PTb")):
                    act.wait_ge(*att_pe.at(nm, i))
                    act.activation(PT[:, 2 * b:2 * b + 2, :, 0:nq], PS[:, 4 + b, :].rearrange("p (h k q) -> p h k q", h=2, k=2)[:, :, :, 0:nq],
                                   ACT.Copy).then_inc(att_act.sem, 1)
                act.wait_ge(*att_pe.at("OT", i))
                act.nop(nofuse=True)
                act.activation(qc, PS[:, 1, :].rearrange("p (j q) -> p j q", j=4)[:, :, 0:nq], ACT.Copy).then_inc(att_act.sem, 1)

            att_tile(0, P, Q[:, :, 0:P], KB[:, 0:256], VB[:, 0:2, :], True)
            with act.Fori(1, 8) as i:
                att_tile(i, P, Q[:, :, bass.ds(i * P, P)], KB[:, bass.ds(i * P, 256)], VB[:, bass.ds(i, 2), :])
            att_tile(8, DEC, Q[:, :, S0:TW], KB[:, 1152:1408], VB[:, 9:11, :])

            act.wait_ge(*att_act.at("YB", 8))
            act.wait_ge(small_out, 64)
            for t, nm in ((BT, "bt"), (ER, "er"), (EI, "ei"), (TMR, "tm")):
                act.dma_start(t[:], a[nm]).then_inc(ssm_ld, 16)
            act.wait_ge(ssm_ld, 64)
            act.activation(TM[:].rearrange("p g (j h) -> p j g h", j=CK), TMR[:].rearrange("p j (g h) -> p j g h", g=32),
                           ACT.Copy).then_inc(tm_made, 1)
            act.wait_ge(ssm_pe, 32)
            act.dma_start(CM[:].rearrange("p r t m -> p r (t m)"), a["cm"]).then_inc(cm_ld, 16)
            for g in range(32):
                act.wait_ge(ssm_pe, 33 + g)
                act.activation(UG[:, g, :], PS[:, g % 8, 0:CC], ACT.Copy).then_inc(ssm_act, 1)
            act.wait_ge(ssm_act, 32)
            for j in range(CK):
                act.dma_start(a["yj"].rearrange("g c j k -> j c g k")[j], UG[16 * j:16 * j + 16, :, :]).then_inc(y_out, 16)
            act.wait_ge(ssm_vec, mark["S"])
            act.dma_start(a["ssm_new"], SMALL[:]).then_inc(small_out, 16)
            act.wait_ge(y_out, 16 * CK)
            act.dma_start(UJ[:].rearrange("p t j c -> p t (j c)"), a["yj"].rearrange("(t g) c j k -> (g c) t (j k)", g=8)).then_inc(y_in, 16)
            for j in range(4):
                act.activation(XH[:, 4 + j, :], Q[:, j, :], ACT.Copy).then_inc(glu_act.sem, 1)
            act.wait_ge(*glu_vec.at("bl3"))
            act.wait_ge(y_in, 16)
            for j in range(4):
                act.activation(GY[:, j, 0:SEQ].rearrange("p (c j) -> p c j", j=CK), UJ[:, j, :, 0:NCK].rearrange("p j c -> p c j"),
                               ACT.Gelu_apprx_tanh).then_inc(glu_act.sem, 1)
                act.activation(GY[:, j, S0:TW].rearrange("p (c j) -> p c j", j=CK), UJ[:, j, :, NCK + 1:CC].rearrange("p j c -> p c j"),
                               ACT.Gelu_apprx_tanh).then_inc(glu_act.sem, 1)
                act.wait_ge(*glu_act.at(f"gs{j}"))
                act.activation(GH[:, j, :], GY[:, j, :], ACT.Copy).then_inc(glu_act.sem, 1)
            n = N0["glu"]
            for o in range(4):
                act.wait_ge(tile_done, T0["glu"] + o + 1)
                if o:
                    act.wait_ge(*glu_vec.at(f"mul{o - 1}"))
                act.activation(tiled(LNV[:]), pset(o % 2), ACT.Sigmoid).then_inc(glu_act.sem, 1)
                if o % 2:
                    step(n + o // 2, o // 2, T0["glu"] + o + 1)
                act.wait_ge(*glu_vec.at(f"mul{o}"))
                act.activation(XH[:, o, :], GY[:, o, :], ACT.Copy).then_inc(glu_act.sem, 1)

            def last_norm(ph, n, t, nxt, whole=None):
                for b in range(2):
                    for m in range(4 * b, 4 * b + 4):
                        if whole and m == 6:
                            act.wait_ge(tile_done, whole)
                        norm_tile(nxt, m, (add[ph], ADDS[ph] - KT + m + 1))
                    if nxt != "fin":
                        step(n + b, b, t + 4 * b + 4)

            n, t = N0["out"], T0["out"]
            for b in range(6):
                step(n + b, b % 2, t + 4 * b + 4)
            last_norm("out", n + 6, t + 24, "x0", whole=T0["x0"])

            def cross(l, nxt):
                q, v, ac, te = f"x{l}", xv[l], xa[l], xp[l]
                n, t0 = N0[q], T0[q]

                def loads(h):
                    for st, src in ((0, "memkv"), (1, "smemkv")):
                        act.dma_start(KX[:, st].rearrange("p d m -> p (d m)"), a[src][2 * l][:, bass.ds(h * 512, 512)]).then_inc(xld[l], 16)
                        act.dma_start(VX[:, st].rearrange("p d m e -> p (d m e)"), a[src][2 * l + 1][:, bass.ds(h * 512, 512)]).then_inc(xld[l], 16)

                def head(i, first=False, last=False):
                    for s in (0, 1):
                        step(i * 4 + (n + s), s, i * 10 + (t0 + s + 1))
                        if first and s == 0:
                            rstd(q)
                    for k in range(12):
                        t = k
                        if t < 9:
                            nq = P if t < 8 else DEC
                            act.wait_ge(*v.at(f"nm{t}", i))
                            if t >= 2:
                                act.wait_ge(*te.at(f"T{t - 2}", i))
                            act.activation(PX[0:nq, t % 2, :], PS[0:nq, t % 2, 0:NMEM], ACT.Exp, bias=NX[0:nq, t % 3, 1:2], scale=1.0 / 16,
                                           accum_out=NX[0:nq, t % 3, 2:3]).then_inc(ac.sem, 1)
                        t = k - 1
                        if 0 <= t < 9:
                            nq = P if t < 8 else DEC
                            act.wait_ge(*te.at(f"T{t}", i))
                            act.activation(PXT[:, t % 2, :, 0:nq], PS[:, 2 + t % 2, 0:NMEM].rearrange("p (m q) -> p m q", m=2)[:, :, 0:nq],
                                           ACT.Copy).then_inc(ac.sem, 1)
                        t = k - 3
                        if 0 <= t < 9:
                            nq, c0 = (P, t * P) if t < 8 else (DEC, S0)
                            act.wait_ge(*te.at(f"O{t}", i))
                            act.activation(HH[:, :, c0:c0 + nq], PS[:, 6 + t % 2, 0:NMEM].rearrange("p (d q) -> p d q", d=2)[:, :, 0:nq],
                                           ACT.Copy).then_inc(ac.sem, 1)
                    if not last:
                        loads(i + 1)
                        for b in range(2):
                            step(i * 4 + (n + 2 + b), b, i * 10 + (t0 + 6 + 4 * b))
                    else:
                        last_norm(q, n + 14, t0 + 32, nxt)

                loads(0)
                head(0, first=True)
                with act.Fori(1, HEADS - 1) as i:
                    head(i)
                head(HEADS - 1, last=True)

            def new_states(s, g, e):
                act.activation(STF[:, 0:2, bass.ds(g * 2 + e, 1)].rearrange("p s o -> p (s o)"), G[:, e, SEQ:SEQ + 2], ACT.Copy).then_inc(s.sem, 1)
                act.activation(STF[:, 2:4, bass.ds(g * 2 + e, 1)].rearrange("p s o -> p (s o)"), G[:, e, TW:TW + 2], ACT.Copy).then_inc(s.sem, 1)

            def ffn(l, nxt):
                q, v, ac = f"f{l}", fv[l], fa[l]
                n, t0 = N0[q], T0[q]

                def gated(g, e):
                    act.wait_ge(*v.at(f"c{e}", g))
                    if e == 1:
                        act.wait_ge(*v.at("sm0", g))
                    elif not (isinstance(g, int) and g == 0):
                        act.wait_ge(*v.at("sm1", g - 1))
                    act.activation(ACTV[:], TAP[:, e, :], ACT.Silu).then_inc(ac.sem, 1)
                    new_states(ac, g, e)

                def high(g, e):
                    act.wait_ge(*v.at(f"hid{e}", g))
                    act.activation(HH[:, e, :], HID[:], ACT.Copy).then_inc(ac.sem, 1)

                def group(g, nb, t, first=False):
                    step(nb, 0, t + 1)
                    if first:
                        rstd(q)
                    o, b0 = (1, 1) if first else (9, 3)
                    gated(g, 0)
                    if not first:
                        for b in range(2):
                            step(nb + (1 + b), (1 + b) % 2, t + (5 + 4 * b))
                    step(nb + b0, b0 % 2, t + (o + 1))
                    high(g, 0)
                    step(nb + (b0 + 1), (b0 + 1) % 2, t + (o + 2))
                    gated(g, 1)
                    step(nb + (b0 + 2), (b0 + 2) % 2, t + (o + 3))
                    high(g, 1)

                group(0, n, t0, True)
                with act.Fori(1, 11) as g:
                    group(g, g * 6 + (n - 2), g * 12 + (t0 - 8))
                act.wait_ge(*ac.at("nb1", 10))
                act.dma_start(a[f"st_f{l}"], STF[:]).then_inc(st_out[q], 16)
                last_norm(q, n + 64, t0 + 124, nxt)
                act.wait_ge(st_out[q], 16)

            def conv(nxt):
                n, t0 = N0["c1"], T0["c1"]

                def high(g, e):
                    act.wait_ge(*cv.at(f"zc{e}", g))
                    act.nop(nofuse=True)
                    new_states(ca, g, e)
                    act.wait_ge(*cv.at(f"hid{e}", g))
                    act.activation(HH[:, e, :], HID[:], ACT.Copy).then_inc(ca.sem, 1)

                def group(g, nb, t, first=False):
                    step(nb, 0, t + 1)
                    if first:
                        rstd("c1")
                    o, b0 = (1, 1) if first else (9, 3)
                    if not first:
                        for b in range(2):
                            step(nb + (1 + b), (1 + b) % 2, t + (5 + 4 * b))
                    step(nb + b0, b0 % 2, t + (o + 1))
                    step(nb + (b0 + 1), (b0 + 1) % 2, t + (o + 2))
                    high(g, 0)
                    for b in (2, 3, 4):
                        step(nb + (b0 + b), (b0 + b) % 2, t + (o + b + 1))
                    high(g, 1)

                group(0, n, t0, True)
                with act.Fori(1, 4) as g:
                    group(g, g * 8 + (n - 2), g * 14 + (t0 - 8))
                act.wait_ge(*ca.at("hi1", 3))
                act.dma_start(a["st_c1"], STF[:, :, 0:KT]).then_inc(st_out["c1"], 16)
                last_norm("c1", n + 30, t0 + 48, nxt)
                act.wait_ge(st_out["c1"], 16)

            cross(0, "f0")
            ffn(0, "c1")
            conv("x1")
            cross(1, "f1")
            ffn(1, "fin")
            rstd("fin")
            act.wait_ge(small_out, 80)




def _layout(i):
    f = {k: np.asarray(v) for k, v in i.items()}

    def kblocks(w):
        k, n = w.shape
        return w.reshape(KT, P, n // P, P).transpose(2, 1, 0, 3).reshape(n // P, P, BLK)

    def rows2(w):
        n = w.shape[0]
        return w.reshape(n // 256, 2, P, 2, 512).transpose(0, 3, 2, 1, 4).reshape(-1, P, BLK)

    pair = np.array([h * 64 + d for j in range(4) for h in (j, j + 4) for d in range(64)])
    we = f["w_in_even"][0]
    u, q, k, v = we[:, :512], we[:, 512:1024][:, pair], we[:, 1024:1152], we[:, 1152:1280]
    inp = {"k": kblocks(k)[0], "v": kblocks(v)[0]}
    inp.update({f"u{t}": kblocks(u)[t] for t in range(4)})
    inp.update({f"q{t}": kblocks(q)[t] for t in range(4)})
    wg = f["w_glu"][0].reshape(4, P, 2, 256).transpose(2, 1, 0, 3).reshape(2, P, BLK)
    wo = f["w_out_even"][0]
    wo = np.concatenate([wo[:512], wo[512:][pair]])
    blocks = []
    for l in (0, 1):
        blocks += list(kblocks(f["xattn_wkv"][l]))
    blocks += [inp[x] for x in INP_BLOCKS] + list(wg) + list(rows2(wo))

    def skewed(a_of, na, down, groups):
        down = list(rows2(down))
        for g in range(groups):
            aa = a_of(g)
            blocks.append(aa[0])
            if g:
                blocks.extend(down[2 * g - 2:2 * g])
            blocks.extend(aa[1:])
        blocks.extend(down[-2:])

    for l in (0, 1):
        if l == 1:
            w = kblocks(f["w_in_odd"][0])
            skewed(lambda g: [w[c * KT + 2 * g + e] for e in (0, 1) for c in (1, 2, 0)], 6, f["w_out_odd"][0], 4)
        wq, wx = kblocks(f["xattn_wq"][l]), rows2(f["xattn_wo"][l])
        for h in range(HEADS):
            blocks += [wq[2 * h], wq[2 * h + 1], wx[2 * h], wx[2 * h + 1]]
        w = kblocks(f["ffn_w_up"][l])
        skewed(lambda g: [w[c * FT + 2 * g + e] for e in (0, 1) for c in (0, 1)], 4, f["ffn_w_down"][l], 11)
    w = np.stack(blocks)
    assert w.shape == (NBLOCKS, P, BLK)

    def feat(x):
        return x.reshape(x.shape[0], -1, P).transpose(2, 1, 0)

    cols = np.zeros((P, NCOL), np.float32)

    def put(name, x):
        c, n = COLS[name]
        cols[:, c:c + n] = x.reshape(P, n)
    for nm, key in (("mix", "norm_mix"), ("x", "norm_xattn"), ("f", "norm_ffn")):
        for l in (0, 1):
            put(f"g_{nm}{l}", f[key][l].reshape(KT, P).T)
    put("g_fin", f["norm_final"].reshape(KT, P).T)
    put("cm_w", f["conv_mix_w"][0].reshape(3 * KT, P).T)
    put("cm_s", f["state_conv_mix"][0, 0].reshape(2 * KT, P).T)
    for l in (0, 1):
        put(f"cf_w{l}", f["ffn_conv_w"][l].reshape(3 * FT, P).T)
        put(f"cf_s{l}", f["state_conv_ffn"][l, 0].reshape(2 * FT, P).T)
    put("sink", np.broadcast_to(f["attn_sinks"][0], (P, 8)))
    for nm, key in (("a_re", "ssm_a_re"), ("a_im", "ssm_a_im"), ("log_dt", "ssm_log_dt")):
        put(nm, f[key][0].reshape(16, P).T)
    put("h0_re", f["state_ssm_re"][0, 0].reshape(16, P).T)
    put("h0_im", f["state_ssm_im"][0, 0].reshape(16, P).T)

    x = np.zeros((P, KT, TW), np.float32)
    x[:, :, :SEQ] = feat(f["x_prompt"][0])
    x[:, :, S0:] = feat(f["x_sample"][0])
    smem = []
    for l in (0, 1):
        smem.append(feat(f["cache_mem_k"][l, 0].reshape(NMEM, D)).reshape(P, 2048))
        smem.append(f["cache_mem_v"][l, 0].reshape(2, P, KT, P).transpose(1, 2, 0, 3).reshape(P, 2048))

    def state(x):
        return x.reshape(16, P, -1).transpose(1, 0, 2)

    def cstate(x):
        return x.reshape(16, 2, 16, 64).transpose(1, 3, 0, 2).reshape(P, 16, 16)
    dd = np.zeros((16, 32, 16), np.float32)
    dd[np.arange(16), :, np.arange(16)] = f["ssm_d"][0].T

    inv = np.float32(10000.0) ** (-np.arange(32, dtype=np.float32) * np.float32(2.0) / np.float32(64))
    pos = np.zeros(TW, np.float32)
    pos[:SEQ], pos[S0:] = np.arange(SEQ), 512 + np.arange(DEC)
    ang = (pos[None, :] * inv[:, None]).astype(np.float32)
    rot = np.zeros((P, P), np.float32)
    for b in (0, 64):
        for m in range(32):
            rot[b + 32 + m, b + m] = -1.0
            rot[b + m, b + 32 + m] = 1.0
    mask = np.full((P, 3, 256), NEG, np.float32)
    mask[:64, 0, 128:192] = 0
    mask[64:, 0, 128:256] = 0
    mask[:64, 1, 0:192] = 0
    mask[64:, 1, 64:256] = 0
    mask[:, 2, 0:160] = 0
    return {
        "w": w, "cols": cols, "x": x, "memT": np.ascontiguousarray(feat(f["mem_prompt"][0])), "smemkv": np.stack(smem),
        "past_k": f["cache_win_k"][0, 0].reshape(128, P).T, "past_v": f["cache_win_v"][0, 0].reshape(128, P),
        "b_re": state(f["ssm_b_re"][0]), "b_im": state(f["ssm_b_im"][0]),
        "c_re": cstate(f["ssm_c_re"][0]), "c_im": cstate(f["ssm_c_im"][0]), "d_diag": dd.reshape(16, 512),
        "ident": np.eye(P, dtype=np.float32), "zeros": np.zeros((P, 512), np.float32), "rot": rot, "mask": mask,
        "cos": np.tile(np.cos(ang.astype(np.float64)).astype(np.float32), (4, 1)),
        "sin": np.tile(np.sin(ang.astype(np.float64)).astype(np.float32), (4, 1)),
    }


_OUTS = {"y": (P, KT, TW), "memkv": (4, P, 2048), "k_new": (P, P + DEC), "v_new": (P, P + DEC), "ssm_new": (P, 64),
         "st_f0": (P, 4, FT), "st_f1": (P, 4, FT), "st_c1": (P, 4, KT)}
_SCRATCH = {"uj": (32, 16, CK, CC), "yj": (32, 16, CK, CC), "bt": (P, 2, 16, P), "er": (P, 16, NCK + 1), "ei": (P, 16, NCK + 1),
            "cm": (P, 2, 2048), "tm": (P, CK, 512)}


def kernel(**inputs):
    import concourse.bacc as _bacc
    from concourse.bass_utils import run_bass_kernel_spmd as _run

    nc = _bacc.Bacc("TRN2", target_bir_lowering=False, num_devices=1)
    arrays = {f"in_{k}": np.ascontiguousarray(v) for k, v in _layout(inputs).items()}
    a = {k[3:]: nc.dram_tensor(k, v.shape, F32, kind="ExternalInput").ap() for k, v in arrays.items()}
    for k, s in _OUTS.items():
        a[k] = nc.dram_tensor(f"out_{k}", s, F32, kind="ExternalOutput").ap()
    for k, s in _SCRATCH.items():
        a[k] = nc.dram_tensor(f"scratch_{k}", s, F32, kind="Internal").ap()
    build(nc, a)
    r = _run(nc, [arrays], core_ids=[0]).results[0]
    o = {k: np.asarray(r[f"out_{k}"]) for k in _OUTS}

    def tokens(x):
        return np.ascontiguousarray(x.transpose(2, 1, 0)).reshape(x.shape[2], -1)
    y = tokens(o["y"])
    yp, ys = y[None, :SEQ], y[None, S0:]
    kw, vw = o["k_new"].T, o["v_new"].T
    ssm = [o["ssm_new"][:, 16 * k:16 * k + 16].T.reshape(1, 1, 32, 64) for k in range(4)]
    conv = {q: o[q].transpose(1, 2, 0).reshape(4, -1) for q in ("st_f0", "st_f1", "st_c1")}
    cf = np.stack([conv["st_f0"], conv["st_f1"]])
    mk = np.stack([tokens(o["memkv"][2 * l].reshape(P, KT, NMEM)) for l in (0, 1)])
    mv = np.stack([o["memkv"][2 * l + 1].reshape(P, KT, 2, P).transpose(2, 0, 1, 3).reshape(NMEM, D) for l in (0, 1)])
    out = (yp, ys, kw[:P].reshape(1, 1, P, 2, 64), vw[:P].reshape(1, 1, P, 2, 64), ssm[0], ssm[1],
           conv["st_c1"][None, None, 0:2], cf[:, None, 0:2], mk.reshape(2, 1, NMEM, HEADS, 256), mv.reshape(2, 1, NMEM, HEADS, 256),
           kw[P:].reshape(1, 1, DEC, 2, 64), vw[P:].reshape(1, 1, DEC, 2, 64), ssm[2], ssm[3],
           conv["st_c1"][None, None, 2:4], cf[:, None, 2:4])
    return tuple(np.ascontiguousarray(x) for x in out)
```

```python
from contextlib import ExitStack

import numpy as np
import concourse.bass as bass
from concourse import mybir

F32, F32R, I32 = mybir.dt.float32, mybir.dt.float32r, mybir.dt.int32
ALU = mybir.AluOpType
ACT = mybir.ActivationFunctionType
AX = mybir.AxisListType

P = 128
D, KT = 1024, 8
SEQ, DEC = 1024, 32
NCH, CW = 3, 354
TW = NCH * CW
S0 = TW - DEC
F_FF, FT = 2816, 22
NMEM = 256
HEADS = 4
CK, NCK = 8, SEQ // 8
CC = NCK + 1 + DEC // CK
NEG = -1e30
BLK = 1024
VALUE_BANKS = ((4, 5), (0, 3))

PHASES = [("kv", 32, 32), ("inp", 10, 16), ("outb", 4, 16), ("glu", 2, 4), ("outa", 4, 16), ("x0", 16, 40), ("f0", 66, 132),
          ("c1", 32, 56), ("x1", 16, 40), ("f1", 66, 132)]
N0, T0 = {}, {}
_n = _t = 0
for _name, _b, _tl in PHASES:
    N0[_name], T0[_name] = _n, _t
    _n, _t = _n + _b, _t + _tl
NBLOCKS, NTILES = _n, _t
NEXT = {a[0]: b[0] for a, b in zip(PHASES, PHASES[1:])}

COLS = {}
_c = 0
for _name, _w in [("g_mix0", 8), ("g_x0", 8), ("g_f0", 8), ("g_mix1", 8), ("g_x1", 8), ("g_f1", 8), ("g_fin", 8),
                  ("cm_w", 24), ("cm_s", 16), ("cf_w0", 66), ("cf_s0", 44), ("cf_w1", 66), ("cf_s1", 44),
                  ("sink", 8), ("a_re", 16), ("a_im", 16), ("log_dt", 16), ("h0_re", 16), ("h0_im", 16)]:
    COLS[_name] = (_c, _w)
    _c += _w
NCOL = _c

INP = ["k", "v", "Rk", "u0", "VT", "u1", "u2", "u3", "q0", "q1", "Rq0", "q2", "Rq1", "q3", "Rq2", "Rq3"]
INP_BLOCKS = [x for x in INP if x[0] != "R" and x != "VT"]


class Steps:

    def __init__(self, sem, names):
        self.sem, self.n = sem, len(names)
        self.k = {x: i + 1 for i, x in enumerate(names)}

    def at(self, name, i=0):
        return self.sem, i * self.n + self.k[name]



GAIN = {"inp": "g_mix0", "x0": "g_x0", "f0": "g_f0", "c1": "g_mix1", "x1": "g_x1", "f1": "g_f1", "fin": "g_fin"}
QSLOT = {"k": 0, "q0": 1, "q1": 0, "q2": 1, "q3": 0}
ADDS = {"out": 32, "x0": 32, "f0": 88, "c1": 32, "x1": 32, "f1": 88}
CEXP = [1.0 / 5040, 1.0 / 720, 1.0 / 120, 1.0 / 24, 1.0 / 6, 0.5, 1.0]
CSIN = [1.0 / 6227020800, -1.0 / 39916800, 1.0 / 362880, -1.0 / 5040, 1.0 / 120, -1.0 / 6]
CCOS = [-1.0 / 87178291200, 1.0 / 479001600, -1.0 / 3628800, 1.0 / 40320, -1.0 / 720, 1.0 / 24, -0.5]
ROUND = 12582912.0
LN2 = (0.693359375, -2.12194440e-4)
PI3 = (3.140625, 9.67502593994140625e-4, 1.5099579909783764e-7)


def build(nc, a):
    with ExitStack() as ctx:
        cursor = [16512]

        def place(name, shape, dt=F32, offset=None):
            size = (4 * int(np.prod(shape[1:])) + 31) // 32 * 32
            if offset is None:
                offset = cursor[0]
                cursor[0] += size
            return nc.alloc_sbuf_tensor_at(name, shape, dt, offset=(offset + 31) // 32 * 32)

        def region(start, limit):
            start = (start + 31) // 32 * 32

            pos = [start]

            def put(name, shape, dt=F32):
                t = place(name, shape, dt, offset=pos[0])
                pos[0] += (4 * int(np.prod(shape[1:])) + 31) // 32 * 32
                assert pos[0] <= limit, (name, pos[0] - limit)
                return t
            return put

        def sem(name):
            return ctx.enter_context(nc.semaphore(name))

        X = place("X", [P, KT, TW])
        xh_off = cursor[0]
        XH = place("XH", [P, KT, TW], F32R)
        XL = place("XL", [P, KT, TW], F32R)
        x_end = cursor[0]
        WR = place("WR", [P, 2, BLK])
        wh_off = cursor[0]
        WH = place("WH", [P, 2, BLK], F32R)
        WL = place("WL", [P, 2, BLK], F32R)
        hh_off = cursor[0]
        HH = place("HH", [P, 2, TW], F32R)
        HL = place("HL", [P, 2, TW], F32R)
        hh_end = cursor[0]
        rstd_off = cursor[0]
        RSTD = place("RSTD", [P, TW])
        LNV = place("LNV", [P, TW])
        COL = place("COL", [P, NCOL])
        IDENT = place("IDENT", [P, P])
        ONES = place("ONES", [P, P])
        EPSC = place("EPSC", [P, 1])
        RHO8 = place("RHO8", [P, 16])
        SMALL = place("SMALL", [P, 64])
        arena, end = cursor[0], 229344

        put = region(arena, end)
        MR = put("MR", [P, KT, NMEM])
        MH = put("MH", [P, KT, NMEM], F32R)
        ML = put("ML", [P, KT, NMEM], F32R)
        KVS = put("KVS", [P, 2, KT, NMEM])
        WX = place("WX", [P, 2, BLK], offset=arena)
        WHX = put("WHX", [P, 2, BLK], F32R)
        WLX = [put("WLX0", [P, BLK], F32R), place("WLX1", [P, BLK], F32R, offset=rstd_off + 4 * TW)]
        put = region(xh_off, x_end)
        PR, PI = put("PR", [P, 16, 8, 16]), put("PI", [P, 16, 8, 16])
        T1, T2 = put("T1", [P, 16, 8, 16]), put("T2", [P, 16, 8, 16])
        T3 = place("T3", [P, 16, 8, 16], offset=xh_off + 4 * 4 * 2048)
        BTP = put("BTP", [P, 2, 16, P])
        KR = put("KR", [P, 512])
        BR, BI = put("BR", [P, 16, 16]), put("BI", [P, 16, 16])
        BBR, BBI = put("BBR", [P, 16, 16]), put("BBI", [P, 16, 16])
        CR, CI = put("CR", [P, 16, 16]), put("CI", [P, 16, 16])
        CRD, NCID = put("CRD", [P, 16, 32]), put("NCID", [P, 16, 32])
        DD = put("DD", [16, 512])
        AR, AI = put("AR", [P, 16, 9]), put("AI", [P, 16, 9])
        AS = put("AS", [P, 24, 16])
        ASI = put("ASI", [P, 16], I32)
        put = region(hh_off, hh_end)
        ERP, EIP = put("ERP", [P, 16, NCK + 1]), put("EIP", [P, 16, NCK + 1])

        put = region(arena, end)
        UJ = put("UJ", [P, 4, CK, CC])
        Q = put("Q", [P, 4, TW])
        KB = put("KB", [P, 1408])
        VB = put("VB", [P, 11, P])
        SMX = put("SMX", [P, 2, 64])
        MASK = put("MASK", [P, 3, 256])
        ROT = put("ROT", [P, P])
        VTT = put("VTT", [P, TW])
        QS = put("QS", [P, 4, P])
        OS = put("OS", [P, 512])
        put = region(hh_off, hh_end)
        COS, SIN = put("COS", [P, TW]), put("SIN", [P, TW])
        QR = put("QR", [P, 2, TW])
        UG = place("UG", [P, 32, CC], offset=arena)
        SB = place("SB", [P, 2, 8, 256], offset=wh_off)
        PT = place("PT", [P, 8, 2, P], offset=rstd_off)
        put = region(xh_off, x_end)
        BT = put("BT", [P, 2, 16, P])
        ER, EI = put("ER", [P, 16, NCK + 1]), put("EI", [P, 16, NCK + 1])
        HR, HI = put("HR", [P, 16, CC + 1]), put("HI", [P, 16, CC + 1])
        TM = put("TM", [P, 32, P])
        KS = put("KS", [P, 256])
        CM = place("CM", [P, 2, 16, P], offset=xh_off)
        TMR = place("TMR", [P, CK, 512], offset=hh_off)
        put = region(hh_off, hh_end)
        S1, S2 = put("S1", [P, 16, NCK + DEC // CK]), put("S2", [P, 16, NCK + DEC // CK])
        GY = place("GY", [P, 4, TW], offset=hh_off)
        put = region(arena + 4 * 4 * CK * CC, end)
        GH, GL = put("GH", [P, 4, TW], F32R), put("GL", [P, 4, TW], F32R)

        put = region(arena, end)
        SQ = put("SQ", [P, 2, TW])
        XQ = put("XQ", [P, 2, TW])
        KX = put("KX", [P, 2, 2, NMEM])
        VX = put("VX", [P, 2, 2, 2, P])
        PX, PXT, OX = put("PX", [P, 2, NMEM]), put("PXT", [P, 2, 2, P]), put("OX", [P, 2, NMEM])
        NX = put("NX", [P, 3, 4])
        put = region(arena + (2 * 4 * TW + 31) // 32 * 32, end)
        G = put("G", [P, 2, TW + 2])
        TAP = put("TAP", [P, 2, TW])
        ACTV, HID = put("ACTV", [P, TW]), put("HID", [P, TW])
        C2, RSTD2 = put("C2", [P, TW]), put("RSTD2", [P, TW])
        STF = put("STF", [P, 4, FT])
        FW = put("FW", [P, 2, 3])

        PS = ctx.enter_context(nc.psum_tensor("PS", [P, 8, 512], F32))

        def pset(s):
            return PS[:, 3 * s:3 * s + 3, 0:CW]

        def col(name, j=0, w=1):
            c = COLS[name][0] + j
            return COL[:, c:c + w]

        def kv_slot(s):
            return (WR[:, s, :], WH[:, s, :], WL[:, s, :]) if s < 2 else (WX[:, s - 2, :], WHX[:, s - 2, :], WLX[s - 2][:])

        def tiled(x):
            return x.rearrange("p (c w) -> p c w", c=NCH)

        def chunk(x, c):
            return x[:, c * CW:(c + 1) * CW]

        ld = sem("first_loads")
        w_raw = [sem("w_raw_even"), sem("w_raw_odd")]
        kv_raw = [sem(f"kv_raw{x}") for x in range(4)]
        w_hi, w_lo = sem("w_hi"), sem("w_lo")
        tile_done = sem("tile_done")
        kv_copy, kv_out = sem("kv_copy"), [sem(f"kv_out{x}") for x in range(4)]
        mem_hi, mem_lo = sem("mem_hi"), sem("mem_lo")
        par_kr = sem("par_impulse")
        par_ld, par_vec, par_pe, par_dma, par_act = (sem("par_" + x) for x in ("loads", "vec", "pe", "dma", "act"))
        x_ld, ready = sem("x_load"), sem("constants_ready")
        NORMS = ["inp", "x0", "f0", "c1", "x1", "f1", "fin"]
        n_act, n_sum, n_lo, n_tot, n_rs = {}, {}, {}, {}, {}
        for q in NORMS:
            n_act[q] = Steps(sem(f"norm_{q}_act"), [s + str(m) for m in range(KT) for s in (["sq", "hi"] if q != "fin" else ["sq"])])
            n_sum[q] = sem(f"norm_{q}_sum")
            n_lo[q] = sem(f"norm_{q}_lo")
            n_tot[q] = sem(f"norm_{q}_total")
            n_rs[q] = sem(f"norm_{q}_rstd")
        add = {q: sem(f"add_{q}") for q in ADDS}
        names = []
        for x in INP:
            if x == "Rk":
                names += ["sin_k", "cos_k", "rot_k", "rotS_k"]
            elif x[0] == "R":
                names += [s + x[1:] for s in ("sin_", "cos_", "rot_")]
            elif x[0] == "u":
                names += [x, x + "P", x + "S"]
            elif x != "VT":
                names += [x]
        ivec = Steps(sem("inp_vec"), names)
        iact = Steps(sem("inp_act"), ["VTa", "VTb"])
        zeroed, tm_made = sem("mixer_zeroed"), sem("tm_made")
        mix_ld, uj_out, ug_in = sem("mix_loads"), sem("u_to_dram"), sem("u_by_group")
        aa_act = Steps(sem("scores_act"), ["QS", "KS"] + [f"exp{h}" for h in range(8)] + ["esink"])
        aa_vec = Steps(sem("scores_vec"), ["s0", "s1", "s2", "s3", "max", "maxs", "neg", "ds"])
        aa_pe = Steps(sem("scores_pe"), ["S"])
        ab_act = Steps(sem("values_act"), ["PTa", "PTb", "YB"])
        ab_vec = Steps(sem("values_vec"), ["sum", "rec", "PTc", "PTd", "OS"])
        ab_pe = Steps(sem("values_pe"), ["PTa", "PTb", "PTc", "PTd", "PV", "OT"])
        ssm_ld, cm_ld = sem("ssm_loads"), sem("ssm_cm_load")
        ssm_v, ssm_copy = sem("ssm_v"), sem("ssm_v_copied")
        ssm_rot, ssm_scan = sem("ssm_rotation"), sem("ssm_scan")
        ssm_y, ssm_act = sem("ssm_y"), sem("ssm_y_copied")
        y_out, y_in, small_out = sem("y_to_dram"), sem("y_back"), sem("new_state_out")
        four = range(4)
        glu_act = Steps(sem("glu_act"), [f"bh{j}" for j in four] + [s + str(j) for j in four for s in ("gp", "gs", "gh")]
                        + [s + str(j) for j in four for s in ("sig", "hi")])
        glu_vec = Steps(sem("glu_vec"), ["z"] + [f"bl{j}" for j in four] + [f"gl{j}" for j in four]
                        + [s + str(j) for j in four for s in ("mul", "lo")])
        xv, xa, xp, xld, xz = {}, {}, {}, {}, {}
        for l in (0, 1):
            xv[l] = Steps(sem(f"x{l}_vec"), ["q0", "q1"] + [f"{s}{t}" for k in range(12) for s, t in (
                ("mx", k), ("nm", k), ("rc", k - 2), ("ov", k - 2), ("lo", k - 3)) if 0 <= t < 9])
            xa[l] = Steps(sem(f"x{l}_act"), [f"{s}{t}" for k in range(12) for s, t in (
                ("ex", k), ("pt", k - 1), ("hi", k - 3)) if 0 <= t < 9])
            xp[l] = Steps(sem(f"x{l}_pe"), [f"{s}{t}" for k in range(12) for s, t in (
                ("S", k), ("T", k - 1), ("V", k - 2), ("O", k - 3)) if 0 <= t < 9])
            xld[l], xz[l] = sem(f"x{l}_kv_loads"), sem(f"x{l}_zeroed")
        fv, fa, fz = {}, {}, {}
        for l in (0, 1):
            fv[l] = Steps(sem(f"f{l}_vec"), ["gate0", "w0", "st0", "a0", "b0", "c0", "sm0", "hid0", "gate1", "lo0", "w1", "st1",
                                             "a1", "b1", "c1", "sm1", "hid1", "lo1"])
            fa[l] = Steps(sem(f"f{l}_act"), [s + str(e) for e in (0, 1) for s in ("silu", "na", "nb", "hi")])
            fz[l] = sem(f"f{l}_zeroed")
        cv = Steps(sem("c1_vec"), [s + str(e) for e in (0, 1) for s in ("cc", "zc", "w", "st", "a", "b", "c", "cr", "hid", "lo")])
        ca = Steps(sem("c1_act"), [s + str(e) for e in (0, 1) for s in ("na", "nb", "hi")])
        cz = sem("c1_zeroed")
        st_out = {q: sem(f"{q}_state_out") for q in ("f0", "c1", "f1")}
        outs = sem("outputs")
        fin = sem("fin_y")
        mark = {"H": 26, "S": 30}

        block = ctx.enter_context(nc.Block())

        @block.vector
        def _(dv):
            def chain(s):
                count = [0]

                def do(ins):
                    count[0] += 1
                    ins.then_inc(s, 1)
                    dv.wait_ge(s, count[0])
                    return count[0]
                do.count = count
                return do

            do = chain(ready)
            do(dv.memset(EPSC[:], 1e-6))
            do(dv.memset(ONES[:], 1.0))
            dv.wait_ge(ld, 48)
            dv.wait_ge(mem_hi, 1)
            dv.tensor_tensor(ML[:], MR[:], MH[:].bitcast(F32), ALU.subtract).then_inc(mem_lo, 1)

            do = chain(par_vec)
            R = [AS[:, k, :] for k in range(24)]

            def cmul(out_r, out_i, ar, ai, br, bi, t1, t2, t3, t4):
                do(dv.tensor_tensor(t1, ar, br, ALU.mult))
                do(dv.tensor_tensor(t2, ai, bi, ALU.mult))
                do(dv.tensor_tensor(t3, ar, bi, ALU.mult))
                do(dv.tensor_tensor(t4, ai, br, ALU.mult))
                do(dv.tensor_tensor(out_r, t1, t2, ALU.subtract))
                do(dv.tensor_tensor(out_i, t3, t4, ALU.add))

            def exp(out, x, k, r, p):
                do(dv.tensor_scalar(k, x, 1.4426950408889634, ROUND, ALU.mult, ALU.add))
                do(dv.tensor_scalar(k, k, -ROUND, None, ALU.add))
                do(dv.scalar_tensor_tensor(out=r, in0=k, scalar=-LN2[0], in1=x, op0=ALU.mult, op1=ALU.add))
                do(dv.scalar_tensor_tensor(out=r, in0=k, scalar=-LN2[1], in1=r, op0=ALU.mult, op1=ALU.add))
                do(dv.tensor_scalar(p, r, CEXP[0], None, ALU.mult))
                for c in CEXP[1:]:
                    do(dv.scalar_tensor_tensor(out=p, in0=p, scalar=c, in1=r, op0=ALU.add, op1=ALU.mult))
                do(dv.tensor_scalar(k, k, -126.0, 127.0, ALU.max, ALU.min))
                do(dv.tensor_scalar(ASI[:], k, 127.0, 8388608.0, ALU.add, ALU.mult))
                do(dv.scalar_tensor_tensor(out=out, in0=p, scalar=1.0, in1=ASI[:].bitcast(F32), op0=ALU.add, op1=ALU.mult))

            dt, rho, th, cs, sn, k, r, z, p, sg = R[0:10]
            exp(dt, col("log_dt", 0, 16), k, r, p)
            do(dv.tensor_tensor(z, dt, col("a_re", 0, 16), ALU.mult))
            exp(rho, z, k, r, p)
            do(dv.tensor_tensor(th, dt, col("a_im", 0, 16), ALU.mult))
            do(dv.tensor_scalar(k, th, 0.3183098861837907, ROUND, ALU.mult, ALU.add))
            do(dv.tensor_scalar(k, k, -ROUND, None, ALU.add))
            do(dv.scalar_tensor_tensor(out=r, in0=k, scalar=-PI3[0], in1=th, op0=ALU.mult, op1=ALU.add))
            for c in PI3[1:]:
                do(dv.scalar_tensor_tensor(out=r, in0=k, scalar=-c, in1=r, op0=ALU.mult, op1=ALU.add))
            do(dv.tensor_scalar(sg, k, 0.5, ROUND, ALU.mult, ALU.add))
            do(dv.tensor_scalar(sg, sg, -ROUND, -2.0, ALU.add, ALU.mult))
            do(dv.tensor_tensor(sg, sg, k, ALU.add))
            do(dv.tensor_tensor(sg, sg, sg, ALU.mult))
            do(dv.tensor_scalar(sg, sg, -2.0, 1.0, ALU.mult, ALU.add))
            do(dv.tensor_tensor(z, r, r, ALU.mult))
            do(dv.tensor_scalar(p, z, CSIN[0], None, ALU.mult))
            for c in CSIN[1:]:
                do(dv.scalar_tensor_tensor(out=p, in0=p, scalar=c, in1=z, op0=ALU.add, op1=ALU.mult))
            do(dv.scalar_tensor_tensor(out=p, in0=p, scalar=1.0, in1=r, op0=ALU.add, op1=ALU.mult))
            do(dv.tensor_tensor(sn, p, sg, ALU.mult))
            do(dv.tensor_scalar(p, z, CCOS[0], None, ALU.mult))
            for c in CCOS[1:]:
                do(dv.scalar_tensor_tensor(out=p, in0=p, scalar=c, in1=z, op0=ALU.add, op1=ALU.mult))
            do(dv.scalar_tensor_tensor(out=cs, in0=p, scalar=1.0, in1=sg, op0=ALU.add, op1=ALU.mult))
            do(dv.memset(AR[:, :, 0], 1.0))
            do(dv.memset(AI[:, :, 0], 0.0))
            do(dv.tensor_tensor(AR[:, :, 1], rho, cs, ALU.mult))
            do(dv.tensor_tensor(AI[:, :, 1], rho, sn, ALU.mult))
            tt = [T[:].rearrange("p t i c -> p (t i c)") for T in (T1, T2)]
            tmp = [tt[0][:, 0:1024], tt[0][:, 1024:2048], tt[1][:, 0:1024], tt[1][:, 1024:2048]]

            def temps(w):
                return [x[:, 0:16 * w].rearrange("p (t w) -> p t w", t=16) for x in tmp]
            for w in (1, 2, 4):
                cmul(AR[:, :, w + 1:2 * w + 1], AI[:, :, w + 1:2 * w + 1], AR[:, :, 1:w + 1], AI[:, :, 1:w + 1],
                     AR[:, :, w:w + 1].to_broadcast([P, 16, w]), AI[:, :, w:w + 1].to_broadcast([P, 16, w]), *temps(w))
            do(dv.tensor_tensor(RHO8[:], rho, rho, ALU.mult))
            for _ in range(2):
                do(dv.tensor_tensor(RHO8[:], RHO8[:], RHO8[:], ALU.mult))
            for i in range(3):
                o = (ERP[:, :, 1], EIP[:, :, 1]) if i == 2 else (cs, sn)
                cmul(*o, cs, sn, cs, sn, *R[12:16])
            do(dv.memset(ERP[:, :, 0], 1.0))
            do(dv.memset(EIP[:, :, 0], 0.0))
            w = 1
            while w < NCK:
                cmul(ERP[:, :, w + 1:2 * w + 1], EIP[:, :, w + 1:2 * w + 1], ERP[:, :, 1:w + 1], EIP[:, :, 1:w + 1],
                     ERP[:, :, w:w + 1].to_broadcast([P, 16, w]), EIP[:, :, w:w + 1].to_broadcast([P, 16, w]), *temps(w))
                w *= 2
            lr, li = col("a_re", 0, 16), col("a_im", 0, 16)
            nr, den, d2, fr, fi, q1, q2 = R[10:17]
            ai = AI[:, :, 1]
            do(dv.tensor_scalar(nr, AR[:, :, 1], -1.0, None, ALU.add))
            do(dv.tensor_tensor(den, lr, lr, ALU.mult))
            do(dv.tensor_tensor(d2, li, li, ALU.mult))
            do(dv.tensor_tensor(den, den, d2, ALU.add))
            do(dv.reciprocal(den, den))
            do(dv.tensor_tensor(q1, nr, lr, ALU.mult))
            do(dv.tensor_tensor(q2, ai, li, ALU.mult))
            do(dv.tensor_tensor(fr, q1, q2, ALU.add))
            do(dv.tensor_tensor(fr, fr, den, ALU.mult))
            do(dv.tensor_tensor(q1, ai, lr, ALU.mult))
            do(dv.tensor_tensor(q2, nr, li, ALU.mult))
            do(dv.tensor_tensor(fi, q1, q2, ALU.subtract))
            do(dv.tensor_tensor(fi, fi, den, ALU.mult))
            dv.wait_ge(par_ld, 80)

            def b16(x):
                return x.unsqueeze(2).to_broadcast([P, 16, 16])
            cmul(BBR[:], BBI[:], b16(fr), b16(fi), BR[:], BI[:], *temps(16))
            do(dv.memset(CRD[:], 0.0))
            do(dv.memset(NCID[:], 0.0))
            for q in range(2):
                r, c = slice(64 * q, 64 * q + 64), slice(16 * q, 16 * q + 16)
                do(dv.tensor_copy(CRD[r, :, c], CR[r]))
                do(dv.tensor_scalar(NCID[r, :, c], CI[r], -1.0, None, ALU.mult))

            def pw(x, j):
                return x[:, :, j:j + 8].unsqueeze(3).to_broadcast([P, 16, 8, 16])

            def ch(x):
                return x[:].unsqueeze(2).to_broadcast([P, 16, 8, 16])
            do(dv.tensor_tensor(PR[:], pw(AR, 0), ch(BBR), ALU.mult))
            do(dv.tensor_tensor(T1[:], pw(AI, 0), ch(BBI), ALU.mult))
            do(dv.tensor_tensor(PR[:], PR[:], T1[:], ALU.subtract))
            do(dv.tensor_tensor(PI[:], pw(AR, 0), ch(BBI), ALU.mult))
            do(dv.tensor_tensor(T1[:], pw(AI, 0), ch(BBR), ALU.mult))
            mark["P"] = do(dv.tensor_tensor(PI[:], PI[:], T1[:], ALU.add))
            do(dv.tensor_tensor(T1[:], pw(AR, 1), ch(CR), ALU.mult))
            do(dv.tensor_tensor(T3[:], pw(AI, 1), ch(CI), ALU.mult))
            do(dv.tensor_tensor(T1[:], T1[:], T3[:], ALU.subtract))
            do(dv.tensor_tensor(T2[:], pw(AI, 1), ch(CR), ALU.mult))
            do(dv.tensor_tensor(T3[:], pw(AR, 1), ch(CI), ALU.mult))
            do(dv.tensor_tensor(T2[:], T2[:], T3[:], ALU.add))
            mark["C"] = do(dv.tensor_scalar(T2[:], T2[:], -1.0, None, ALU.mult))
            dv.wait_ge(par_kr, 1)
            do(dv.tensor_copy(KR[:], PS[:, 1, :]))
            mark["K"] = do(dv.tensor_tensor(KR[0:16, :], KR[0:16, :], DD[:], ALU.add))

            def norm_lo(q, m):
                dv.wait_ge(*n_act[q].at(f"hi{m}"))
                dv.scalar_tensor_tensor(out=XL[:, m, :], in0=X[:, m, :], scalar=col(GAIN[q], m), in1=XH[:, m, :].bitcast(F32),
                                        op0=ALU.mult, op1=ALU.subtract).then_inc(n_lo[q], 1)

            def last_adds(ph, first_tile, nxt):
                for m in range(KT + 1):
                    if m < KT:
                        dv.wait_ge(tile_done, first_tile + m)
                        dv.wait_ge(add[ph], ADDS[ph] - 2 * KT + m + 1)
                        dv.tensor_tensor(tiled(X[:, m, :]), tiled(X[:, m, :]), pset(m % 2), ALU.add).then_inc(add[ph], 1)
                    if m >= 1 and nxt != "fin":
                        norm_lo(nxt, m - 1)

            dv.wait_ge(par_dma, 16 * 20)
            zero = chain(zeroed)
            for m in range(KT):
                norm_lo("inp", m)
            dv.wait_ge(kv_copy, 32)
            dv.wait_ge(tile_done, N0["inp"])
            for s in kv_out:
                dv.wait_ge(s, 16)
            zero(dv.memset(UJ[:, :, :, NCK:NCK + 1], 0.0))
            zero(dv.memset(KB[:, 0:P], 0.0))
            zero(dv.memset(KB[:, 1312:1408], 0.0))
            zero(dv.memset(VB[:, 0, :], 0.0))
            mark["Z"] = zero(dv.memset(VB[:, 10, :], 0.0))
            for j, x in enumerate(INP):
                ps = pset(j % 2)
                if x != "VT":
                    dv.wait_ge(tile_done, T0["inp"] + j + 1)
                if j == 0:
                    dv.wait_ge(n_rs["inp"], 6)
                    dv.wait_ge(mix_ld, 96)
                if x in ("k", "q0", "q1", "q2", "q3"):
                    if x == "q1":
                        dv.wait_ge(*ivec.at("rotS_k"))
                    if x in ("q2", "q3"):
                        dv.wait_ge(*ivec.at({"q2": "rot_q0", "q3": "rot_q1"}[x]))
                    dv.tensor_tensor(tiled(QR[:, QSLOT[x], :]), ps, tiled(RSTD[:]), ALU.mult).then_inc(ivec.sem, 1)
                elif x == "v":
                    dv.tensor_tensor(tiled(VTT[:]), ps, tiled(RSTD[:]), ALU.mult).then_inc(ivec.sem, 1)
                elif x[0] == "u":
                    t = int(x[1])
                    dv.wait_ge(*(ivec.at("rotS_k") if t == 0 else ivec.at(f"u{t - 1}S")))
                    dv.tensor_tensor(tiled(LNV[:]), ps, tiled(RSTD[:]), ALU.mult).then_inc(ivec.sem, 1)
                    dv.wait_ge(*ivec.at(x))
                    dv.tensor_copy(UJ[:, t, :, 0:NCK], LNV[:, 0:SEQ].rearrange("p (c j) -> p j c", j=CK)).then_inc(ivec.sem, 1)
                    dv.tensor_copy(UJ[:, t, :, NCK + 1:CC], LNV[:, S0:TW].rearrange("p (c j) -> p j c", j=CK)).then_inc(ivec.sem, 1)
                elif x[0] == "R":
                    y = x[1:]
                    dst = LNV[:] if y == "k" else Q[:, int(y[1]), :]
                    qr = QR[:, QSLOT[y], :]
                    dv.tensor_tensor(tiled(dst), ps, tiled(SIN[:]), ALU.mult).then_inc(ivec.sem, 1)
                    dv.wait_ge(*ivec.at(y))
                    dv.tensor_tensor(qr, qr, COS[:], ALU.mult).then_inc(ivec.sem, 1)
                    dv.wait_ge(*ivec.at("cos_" + y))
                    if y == "k":
                        dv.tensor_tensor(KB[:, P:P + SEQ], LNV[:, 0:SEQ], qr[:, 0:SEQ], ALU.add).then_inc(ivec.sem, 1)
                        dv.tensor_tensor(KB[:, 1280:1312], LNV[:, S0:TW], qr[:, S0:TW], ALU.add).then_inc(ivec.sem, 1)
                    else:
                        dv.tensor_tensor(dst, dst, qr, ALU.add).then_inc(ivec.sem, 1)

            def att(k, s, nq=P, kind=1, values=True, scores=True):
                j, z, nj = k - 1, 1 - s, P
                if scores:
                    dv.wait_ge(*aa_pe.at("S", k))
                    if not (isinstance(k, int) and k < 2):
                        dv.wait_ge(*ab_pe.at("PTd", k - 2))
                    for b in range(4):
                        dv.scalar_tensor_tensor(out=SB[0:nq, s, 2 * b:2 * b + 2, :], in0=PS[0:nq, b, :].rearrange("p (h k) -> p h k", h=2),
                                                scalar=0.125, in1=MASK[0:nq, kind, :].unsqueeze(1).to_broadcast([nq, 2, 256]),
                                                op0=ALU.mult, op1=ALU.add).then_inc(aa_vec.sem, 1)
                if values:
                    nj = P if scores else DEC
                    dv.wait_ge(*aa_act.at("esink", j))
                    dv.tensor_tensor(SMX[0:nj, z, 32:40], SMX[0:nj, z, 16:24], SMX[0:nj, z, 24:32], ALU.add).then_inc(ab_vec.sem, 1)
                    dv.wait_ge(*ab_vec.at("sum", j))
                    dv.reciprocal(SMX[0:nj, z, 48:56], SMX[0:nj, z, 32:40]).then_inc(ab_vec.sem, 1)
                    for b, nm in ((2, "PTc"), (3, "PTd")):
                        dv.wait_ge(*ab_pe.at(nm, j))
                        dv.tensor_copy(PT[:, 2 * b:2 * b + 2, :, 0:nj],
                                       PS[:, 2 + b, :].rearrange("p (h k q) -> p h k q", h=2, k=2)[:, :, :, 0:nj]).then_inc(ab_vec.sem, 1)
                if scores:
                    dv.wait_ge(*aa_vec.at("s3", k))
                    dv.tensor_reduce(SMX[0:nq, s, 0:8], SB[0:nq, s], AX.X, ALU.max).then_inc(aa_vec.sem, 1)
                    dv.wait_ge(*aa_vec.at("max", k))
                    dv.tensor_tensor(SMX[0:nq, s, 0:8], SMX[0:nq, s, 0:8], col("sink", 0, 8)[0:nq], ALU.max).then_inc(aa_vec.sem, 1)
                    dv.wait_ge(*aa_vec.at("maxs", k))
                    dv.tensor_scalar(SMX[0:nq, s, 8:16], SMX[0:nq, s, 0:8], -1.0, None, ALU.mult).then_inc(aa_vec.sem, 1)
                    dv.tensor_tensor(SMX[0:nq, s, 40:48], col("sink", 0, 8)[0:nq], SMX[0:nq, s, 0:8], ALU.subtract).then_inc(aa_vec.sem, 1)
                if values:
                    dv.wait_ge(*ab_pe.at("PV", j))
                    dv.wait_ge(*ab_vec.at("rec", j))
                    dv.tensor_tensor(OS[0:nj, :].rearrange("p (j g d) -> p j g d", j=4, g=2), PS[0:nj, 6, :].rearrange("p (j g d) -> p j g d", j=4, g=2),
                                     SMX[0:nj, z, 48:56].rearrange("p (g j) -> p j g", g=2).unsqueeze(3).to_broadcast([nj, 4, 2, 64]),
                                     ALU.mult).then_inc(ab_vec.sem, 1)

            att(0, 0, kind=0, values=False)
            att(1, 1)
            dv.memset(HR[:, :, 0], 0.0).then_inc(ssm_scan, 1)
            dv.memset(HI[:, :, 0], 0.0).then_inc(ssm_scan, 1)
            for k in range(32):
                dv.wait_ge(ssm_v, k + 1)
                dv.tensor_copy((HR, HI)[k % 2][:, k // 2, 1:CC + 1], PS[:, 4 + k % 4, 0:CC]).then_inc(ssm_copy, 1)
            with dv.Fori(1, 3) as i:
                att(i * 2, 0)
                att(i * 2 + 1, 1)
            dv.wait_ge(ssm_rot, 12)
            for lo, w, init in ((1, NCK, None), (NCK + 2, DEC // CK, ("h0_re", "h0_im"))):
                for t in range(16):
                    for s, h, nm in ((S1, HR, 0), (S2, HI, 1)):
                        dv.tensor_tensor_scan(h[:, t, lo:lo + w], RHO8[:, t:t + 1].to_broadcast([P, w]), s[:, t, 0 if init is None else NCK:][:, 0:w],
                                              col(init[nm], t) if init else 0.0, ALU.mult, ALU.add).then_inc(ssm_scan, 1)
            att(6, 0)
            att(7, 1)
            att(8, 0, nq=DEC, kind=2)
            att(9, 1, scores=False)

            dv.wait_ge(*ab_act.at("YB", 8))
            dv.wait_ge(ssm_rot, mark["S"])
            dv.memset(GY[:, :, SEQ:S0], 0.0).then_inc(glu_vec.sem, 1)
            for j in range(4):
                dv.wait_ge(*glu_act.at(f"bh{j}"))
                dv.tensor_tensor(XL[:, j, :], Q[:, j, :], XH[:, j, :].bitcast(F32), ALU.subtract).then_inc(glu_vec.sem, 1)

            def out_add(c, tile):
                m = c % KT
                dv.wait_ge(tile_done, tile)
                if c >= KT:
                    dv.wait_ge(add["out"], c - KT + 1)
                dv.tensor_tensor(tiled(X[:, m, :]), tiled(X[:, m, :]), pset(m % 2), ALU.add).then_inc(add["out"], 1)

            for c in range(16):
                out_add(c, T0["outb"] + c + 1)
                if c in (8, 10, 12, 14):
                    j = (c - 8) // 2
                    dv.wait_ge(*glu_act.at(f"gh{j}"))
                    dv.tensor_tensor(GL[:, j, :], GY[:, j, :], GH[:, j, :].bitcast(F32), ALU.subtract).then_inc(glu_vec.sem, 1)
            for j in range(4):
                dv.wait_ge(*glu_act.at(f"sig{j}"))
                dv.wait_ge(*glu_vec.at(f"gl{j}"))
                dv.tensor_tensor(GY[:, j, :], GY[:, j, :], LNV[:], ALU.mult).then_inc(glu_vec.sem, 1)
                dv.wait_ge(*glu_act.at(f"hi{j}"))
                dv.tensor_tensor(XL[:, 4 + j, :], GY[:, j, :], XH[:, 4 + j, :].bitcast(F32), ALU.subtract).then_inc(glu_vec.sem, 1)
            for c in range(16, 24):
                out_add(c, T0["outa"] + c - 15)
            last_adds("out", T0["outa"] + 9, "x0")

            def cross(l, prev, nxt):
                q, v, ac, te = f"x{l}", xv[l], xa[l], xp[l]
                t0 = T0[q]
                dv.memset(HH[:, :, SEQ:S0].bitcast(F32), 0.0).then_inc(xz[l], 1)
                dv.memset(HL[:, :, SEQ:S0].bitcast(F32), 0.0).then_inc(xz[l], 1)
                dv.wait_ge(xz[l], 2)

                def head(i, first):
                    for s in (0, 1):
                        dv.wait_ge(tile_done, i * 10 + (t0 + s + 1))
                        if first:
                            dv.wait_ge(n_rs[q], 6)
                        dv.tensor_tensor(tiled(XQ[:, s, :]), pset(s), tiled(RSTD[:]), ALU.mult).then_inc(v.sem, 1)
                    for k in range(12):
                        t = k
                        if t < 9:
                            nq = P if t < 8 else DEC
                            dv.wait_ge(*te.at(f"S{t}", i))
                            if t >= 2:
                                dv.wait_ge(*ac.at(f"ex{t - 2}", i))
                            dv.tensor_reduce(NX[0:nq, t % 3, 0:1], PS[0:nq, t % 2, 0:NMEM], AX.X, ALU.max).then_inc(v.sem, 1)
                            dv.wait_ge(*v.at(f"mx{t}", i))
                            dv.tensor_scalar(NX[0:nq, t % 3, 1:2], NX[0:nq, t % 3, 0:1], -1.0 / 16, None, ALU.mult).then_inc(v.sem, 1)
                        t = k - 2
                        if 0 <= t < 9:
                            nq = P if t < 8 else DEC
                            dv.wait_ge(*ac.at(f"ex{t}", i))
                            dv.reciprocal(NX[0:nq, t % 3, 3:4], NX[0:nq, t % 3, 2:3]).then_inc(v.sem, 1)
                            dv.wait_ge(*v.at(f"rc{t}", i))
                            dv.wait_ge(*te.at(f"V{t}", i))
                            dv.tensor_scalar(OX[0:nq, t % 2, :], PS[0:nq, 4 + t % 2, 0:NMEM], NX[0:nq, t % 3, 3:4], None, ALU.mult).then_inc(v.sem, 1)
                        t = k - 3
                        if 0 <= t < 9:
                            nq, c0 = (P, t * P) if t < 8 else (DEC, S0)
                            dv.wait_ge(*ac.at(f"hi{t}", i))
                            dv.tensor_tensor(HL[:, :, c0:c0 + nq], PS[:, 6 + t % 2, 0:NMEM].rearrange("p (d q) -> p d q", d=2)[:, :, 0:nq],
                                             HH[:, :, c0:c0 + nq].bitcast(F32), ALU.subtract).then_inc(v.sem, 1)
                    if isinstance(i, int) and i == HEADS - 1:
                        last_adds(q, t0 + 33, nxt)
                    elif first:
                        for m in range(KT):
                            dv.wait_ge(tile_done, t0 + 3 + m)
                            dv.tensor_tensor(tiled(X[:, m, :]), tiled(X[:, m, :]), pset(m % 2), ALU.add).then_inc(add[q], 1)
                    else:
                        for m in range(KT):
                            dv.wait_ge(tile_done, i * 10 + (t0 + 3 + m))
                            dv.wait_ge(add[q], i * 8 + (m - 7))
                            dv.tensor_tensor(tiled(X[:, m, :]), tiled(X[:, m, :]), pset(m % 2), ALU.add).then_inc(add[q], 1)

                head(0, True)
                with dv.Fori(1, HEADS - 1) as i:
                    head(i, False)
                head(HEADS - 1, False)

            def conv_taps(s, e, wname, width, sname, i, filled):
                w0, s0 = COLS[wname][0], COLS[sname][0]
                wc = COL[:, w0:w0 + 3 * width].rearrange("p (k f) -> p f k", k=3)
                sc = COL[:, s0:s0 + 2 * width].rearrange("p (k f) -> p f k", k=2)
                f = i * 2 + e
                dv.tensor_copy(FW[:, e, :], wc[:, bass.ds(f, 1), :].rearrange("p o k -> p (o k)")).then_inc(s.sem, 1)
                dv.wait_ge(*s.at(filled, i))
                dv.tensor_copy(G[:, e, S0:S0 + 2], sc[:, bass.ds(f, 1), :].rearrange("p o k -> p (o k)")).then_inc(s.sem, 1)
                dv.wait_ge(*s.at(f"st{e}", i))
                dv.tensor_scalar(TAP[:, e, :], G[:, e, 2:TW + 2], FW[:, e, 2:3], None, ALU.mult).then_inc(s.sem, 1)
                dv.wait_ge(*s.at(f"a{e}", i))
                dv.scalar_tensor_tensor(out=TAP[:, e, :], in0=G[:, e, 1:TW + 1], scalar=FW[:, e, 1:2], in1=TAP[:, e, :],
                                        op0=ALU.mult, op1=ALU.add).then_inc(s.sem, 1)
                dv.wait_ge(*s.at(f"b{e}", i))
                dv.scalar_tensor_tensor(out=TAP[:, e, :], in0=G[:, e, 0:TW], scalar=FW[:, e, 0:1], in1=TAP[:, e, :],
                                        op0=ALU.mult, op1=ALU.add).then_inc(s.sem, 1)

            def ffn(l, nxt):
                q, v, ac = f"f{l}", fv[l], fa[l]
                t0 = T0[q]
                dv.memset(G[:, :, 0:2], 0.0).then_inc(fz[l], 1)

                def gate(g, e, tile, first):
                    dv.wait_ge(tile_done, tile)
                    if first:
                        dv.wait_ge(n_rs[q], 6)
                    else:
                        dv.wait_ge(*ac.at(f"nb{e}", g - 1))
                    dv.tensor_tensor(tiled(G[:, e, 2:TW + 2]), pset(0), tiled(RSTD[:]), ALU.mult).then_inc(v.sem, 1)

                def taps(g, e):
                    conv_taps(v, e, f"cf_w{l}", FT, f"cf_s{l}", g, f"gate{e}")

                def scale(g, e):
                    dv.wait_ge(*ac.at(f"silu{e}", g))
                    dv.tensor_tensor(TAP[:, e, :], ACTV[:], RSTD[:], ALU.mult).then_inc(v.sem, 1)

                def hid(g, e, tile):
                    dv.wait_ge(tile_done, tile)
                    dv.wait_ge(*v.at(f"sm{e}", g))
                    dv.tensor_tensor(tiled(HID[:]), pset(1), tiled(TAP[:, e, :]), ALU.mult).then_inc(v.sem, 1)

                def low(g, e):
                    dv.wait_ge(*ac.at(f"hi{e}", g))
                    dv.tensor_tensor(HL[:, e, :], HID[:], HH[:, e, :].bitcast(F32), ALU.subtract).then_inc(v.sem, 1)

                def group(g, t, first):
                    gate(g, 0, t + 1, first)
                    taps(g, 0)
                    if not first:
                        for m in range(KT):
                            dv.wait_ge(tile_done, t + (2 + m))
                            if not isinstance(g, int):
                                dv.wait_ge(add[q], g * 8 + (m - 15))
                            dv.tensor_tensor(tiled(X[:, m, :]), tiled(X[:, m, :]), pset((1 + m) % 2), ALU.add).then_inc(add[q], 1)
                    o = 1 if first else 9
                    scale(g, 0)
                    hid(g, 0, t + (o + 1))
                    gate(g, 1, t + (o + 2), first)
                    low(g, 0)
                    taps(g, 1)
                    scale(g, 1)
                    hid(g, 1, t + (o + 3))
                    low(g, 1)

                dv.wait_ge(fz[l], 1)
                group(0, t0, True)
                group(1, t0 + 4, False)
                with dv.Fori(2, 11) as g:
                    group(g, g * 12 + (t0 - 8), False)
                last_adds(q, t0 + 125, nxt)

            def conv(nxt):
                q = "c1"
                t0 = T0[q]
                dv.memset(G[:, :, 0:2], 0.0).then_inc(cz, 1)
                dv.wait_ge(n_rs[q], 6)
                dv.tensor_tensor(RSTD2[:], RSTD[:], RSTD[:], ALU.mult).then_inc(cz, 1)
                dv.wait_ge(cz, 2)

                def tile(g, e, tc, tz, tb, pc, first, between=None):
                    dv.wait_ge(tile_done, tc)
                    if e == 1:
                        dv.wait_ge(*cv.at("zc0", g))
                    elif not first:
                        dv.wait_ge(*cv.at("zc1", g - 1))
                    dv.tensor_tensor(tiled(C2[:]), pset(pc[0]), tiled(RSTD2[:]), ALU.mult).then_inc(cv.sem, 1)
                    if between:
                        between()
                    dv.wait_ge(tile_done, tz)
                    dv.wait_ge(*cv.at(f"cc{e}", g))
                    if not first:
                        dv.wait_ge(*ca.at(f"nb{e}", g - 1))
                    dv.tensor_tensor(tiled(G[:, e, 2:TW + 2]), pset(pc[1]), tiled(C2[:]), ALU.mult).then_inc(cv.sem, 1)
                    conv_taps(cv, e, "cm_w", KT, "cm_s", g, f"zc{e}")
                    dv.wait_ge(*cv.at(f"c{e}", g))
                    dv.tensor_tensor(TAP[:, e, :], TAP[:, e, :], RSTD[:], ALU.mult).then_inc(cv.sem, 1)
                    dv.wait_ge(tile_done, tb)
                    dv.wait_ge(*cv.at(f"cr{e}", g))
                    dv.tensor_tensor(tiled(HID[:]), pset(pc[2]), tiled(TAP[:, e, :]), ALU.mult).then_inc(cv.sem, 1)
                    dv.wait_ge(*ca.at(f"hi{e}", g))
                    dv.tensor_tensor(HL[:, e, :], HID[:], HH[:, e, :].bitcast(F32), ALU.subtract).then_inc(cv.sem, 1)

                tile(0, 0, t0 + 1, t0 + 2, t0 + 3, (0, 1, 0), True)
                tile(0, 1, t0 + 4, t0 + 5, t0 + 6, (1, 0, 1), True)

                def group(g, t):
                    def between():
                        for m in range(KT):
                            dv.wait_ge(tile_done, t + (2 + m))
                            if not isinstance(g, int):
                                dv.wait_ge(add[q], g * 8 + (m - 15))
                            dv.tensor_tensor(tiled(X[:, m, :]), tiled(X[:, m, :]), pset((1 + m) % 2), ALU.add).then_inc(add[q], 1)
                    tile(g, 0, t + 1, t + 10, t + 11, (0, 1, 0), False, between)
                    tile(g, 1, t + 12, t + 13, t + 14, (1, 0, 1), False)

                group(1, t0 + 6)
                with dv.Fori(2, 4) as g:
                    group(g, g * 14 + (t0 - 8))
                last_adds(q, t0 + 49, nxt)

            cross(0, "out", "f0")
            ffn(0, "c1")
            conv("x1")
            cross(1, "c1", "f1")
            ffn(1, "fin")
            dv.wait_ge(n_rs["fin"], 6)
            dv.wait_ge(add["f1"], 88)
            for m in range(KT):
                dv.scalar_tensor_tensor(out=X[:, m, :], in0=X[:, m, :], scalar=col("g_fin", m), in1=RSTD[:],
                                        op0=ALU.mult, op1=ALU.mult).then_inc(fin, 1)

        @block.tensor
        def _(pe):
            def mms(out, h, l, rh, rl, start, stop):
                pe.matmul(out, h, rh, start=start, stop=False)
                pe.matmul(out, h, rl, start=False, stop=False)
                return pe.matmul(out, l, rh, start=False, stop=stop)

            def tile_a(n, s, pset_i, kt=KT, lhs=None, H=XH, L=XL, wait_lo=True, split=None):
                if wait_lo:
                    pe.wait_ge(w_lo, n + 1)
                for k in range(kt):
                    if split:
                        pe.wait_ge(n_lo[split], k + 1)
                    wh, wl = lhs(k) if lhs else (WH[:, s, k * P:(k + 1) * P], WL[:, s, k * P:(k + 1) * P])
                    for c in range(NCH):
                        mm = mms(PS[:, 3 * pset_i + c, 0:CW], wh, wl, chunk(H[:, k, :], c), chunk(L[:, k, :], c),
                                 k == 0, k == kt - 1)
                mm.then_inc(tile_done, 1)

            def block_b(n, s, marks, H=HH, L=HL, k0=0):
                pe.wait_ge(w_lo, n + 1)
                for o in range(4):
                    pe.wait_ge(*marks[o])
                    def lhs(k):
                        return (WH[:, s, k * 512 + o * P:k * 512 + (o + 1) * P], WL[:, s, k * 512 + o * P:k * 512 + (o + 1) * P])
                    for k in range(2):
                        wh, wl = lhs(k)
                        for c in range(NCH):
                            mm = mms(PS[:, 3 * (o % 2) + c, 0:CW], wh, wl, chunk(H[:, k0 + k, :], c), chunk(L[:, k0 + k, :], c),
                                     k == 0, k == 1)
                    mm.then_inc(tile_done, 1)

            def norm_total(q):
                pe.wait_ge(n_sum[q], KT)
                for c in range(NCH):
                    if c == 2:
                        pe.wait_ge(n_rs[q], 1)
                    pe.matmul(PS[:, 6 + c % 2, 0:CW], ONES[:], chunk(RSTD[:], c), start=True, stop=True).then_inc(n_tot[q], 1)

            pe.wait_ge(mem_lo, 1)
            pe.wait_ge(mem_hi, 1)
            def impulses():
                pe.wait_ge(par_vec, mark["P"])
                for t in range(16):
                    o = PS[:, 1, 32 * t:32 * t + 32]
                    pe.matmul(o, PR[:, t].rearrange("p i c -> p (i c)"), CRD[:, t, :], start=True, stop=False, skip_group_check=True)
                    mm = pe.matmul(o, PI[:, t].rearrange("p i c -> p (i c)"), NCID[:, t, :], start=False, stop=True, skip_group_check=True)
                mm.then_inc(par_kr, 1)

            def transposes():
                pe.wait_ge(par_vec, mark["C"])
                for ri in range(2):
                    for tq in range(4):
                        b = 6 + (4 * ri + tq) % 2
                        if 4 * ri + tq >= 2:
                            pe.wait_ge(par_act, 4 * ri + tq - 1)
                        for t in range(4):
                            mm = pe.transpose(PS[:, b, t * P:(t + 1) * P], (PR, PI)[ri][:, 4 * tq + t].rearrange("p i c -> p (i c)"), IDENT[:])
                        mm.then_inc(par_pe, 1)

            def quad(part, q, first=False):
                for s in range(4):
                    pe.wait_ge(w_lo, q * 4 + (s + 1))
                    _, h, l = kv_slot(s)
                    if part % 2 == 0:
                        if not (first and s < 2):
                            pe.wait_ge(kv_copy, q * 4 + (s - 1))
                        for k in range(KT):
                            w = slice(k * P, (k + 1) * P)
                            mm = mms(PS[:, 3 * (s % 2), 0:NMEM], h[:, w], l[:, w], MH[:, k, :], ML[:, k, :], k == 0, k == KT - 1)
                    else:
                        if s % 2 == 0:
                            pe.wait_ge(kv_copy, q * 4 + (s - 2))
                        for mt in range(2):
                            o = slice(mt * P, (mt + 1) * P)
                            for j in range(4):
                                k, w = 4 * (s % 2) + j, slice(j * 256, (j + 1) * 256)
                                mm = mms(PS[:, VALUE_BANKS[s // 2][mt], 0:256], MH[:, k, o], ML[:, k, o], h[:, w], l[:, w],
                                         k == 0, k == KT - 1)
                    mm.then_inc(tile_done, 1)

            quad(0, 0, True)
            quad(0, 1)
            for part in (1, 2):
                with pe.Fori(2 * part, 2 * part + 2) as q:
                    quad(part, q)
            impulses()
            quad(3, 6)
            transposes()
            quad(3, 7)
            pe.wait_ge(par_vec, mark["K"])
            pe.wait_ge(kv_copy, 32)
            evac = {x: iact.at("VTb") if x == "VT" else ivec.at("sin_" + x[1:] if x[0] == "R" else x) for x in INP}
            n = N0["inp"]
            for j, x in enumerate(INP):
                s = j % 2
                if j >= 2:
                    pe.wait_ge(*evac[INP[j - 2]])
                if x == "VT":
                    pe.wait_ge(*ivec.at("v"))
                    for t in range(9):
                        w = P if t < 8 else DEC
                        c0 = t * P if t < 8 else S0
                        mm = pe.transpose(PS[0:w, 3 * s + t // 4, (t % 4) * P:(t % 4 + 1) * P], VTT[:, c0:c0 + w], IDENT[:])
                    mm.then_inc(tile_done, 1)
                elif x[0] == "R":
                    pe.wait_ge(*ivec.at(x[1:]))
                    if x == "Rk":
                        pe.wait_ge(mix_ld, 96)
                    for c in range(NCH):
                        mm = pe.matmul(PS[:, 3 * s + c, 0:CW], ROT[:], chunk(QR[:, QSLOT[x[1:]], :], c), start=True, stop=True)
                    mm.then_inc(tile_done, 1)
                else:
                    tile_a(n, n % 2, s, split="inp" if j == 0 else None)
                    n += 1
                    if j == 0:
                        norm_total("inp")

            pe.wait_ge(*ivec.at("rot_q3"))

            def att(k, s, nq=P, values=True, scores=True, vb=None):
                j, z, nj = k - 1, 1 - s, P if scores else DEC
                if scores:
                    pe.wait_ge(*aa_act.at("KS", k))
                    if not (isinstance(k, int) and k == 0):
                        pe.wait_ge(*aa_vec.at("s3", j))
                    for g in range(2):
                        r = slice(64 * g, 64 * g + 64)
                        for h in range(4):
                            mm = pe.matmul(PS[0:nq, 2 * g + h // 2, (h % 2) * 256:(h % 2) * 256 + 256], QS[r, h, 0:nq], KS[r],
                                           start=True, stop=True)
                    mm.then_inc(aa_pe.sem, 1)
                if not values:
                    return
                pe.wait_ge(*aa_act.at("exp7", j))
                for b in range(4):
                    if b >= 2:
                        pe.wait_ge(*ab_act.at(("PTa", "PTb")[b - 2], j))
                        pe.nop(nofuse=True)
                    for h in (2 * b, 2 * b + 1):
                        for kt in range(2):
                            mm = pe.transpose(PS[:, 4 + b % 2, ((h % 2) * 2 + kt) * P:((h % 2) * 2 + kt) * P + nj],
                                              SB[0:nj, z, h, kt * P:(kt + 1) * P], IDENT[0:nj, 0:nj])
                    mm.then_inc(ab_pe.sem, 1)
                pe.wait_ge(*ab_vec.at("PTd", j))
                for h in range(8):
                    for kt in range(2):
                        o = (h % 4) * P + (h // 4) * 64
                        mm = pe.matmul(PS[0:nj, 6, o:o + 64], PT[:, h, kt, 0:nj], vb(kt, slice((h // 4) * 64, (h // 4) * 64 + 64)),
                                       start=(kt == 0), stop=(kt == 1), skip_group_check=True)
                mm.then_inc(ab_pe.sem, 1)
                pe.wait_ge(*ab_vec.at("OS", j))
                if not (isinstance(k, int) and k == 1):
                    pe.wait_ge(*ab_act.at("YB", k - 2))
                pe.nop(nofuse=True)
                for c in range(4):
                    mm = pe.transpose(PS[:, 7, c * P:c * P + nj], OS[0:nj, c * P:(c + 1) * P], IDENT[0:nj, 0:nj])
                mm.then_inc(ab_pe.sem, 1)

            def values(k):
                if isinstance(k, int):
                    return lambda kt, d: VB[:, k + kt, d]
                return lambda kt, d: VB[:, bass.ds(k + kt, 1), d].rearrange("p o d -> p (o d)")

            att(0, 0, values=False)
            att(1, 1, vb=values(0))
            pe.wait_ge(ssm_ld, 64)
            pe.wait_ge(ug_in, 128)
            pe.wait_ge(*ab_act.at("YB", 0))
            for t in range(16):
                for ri in range(2):
                    k = 2 * t + ri
                    if k >= 4:
                        pe.wait_ge(ssm_copy, k - 3)
                    for q in range(2):
                        mm = pe.matmul(PS[64 * q:64 * q + 64, 4 + k % 4, 0:CC], BT[:, ri, t, 64 * q:64 * q + 64], UG[:, 2 * t + q, :],
                                       start=True, stop=True)
                    mm.then_inc(ssm_v, 1)
            pe.wait_ge(ssm_copy, 32)
            with pe.Fori(1, 3) as i:
                att(i * 2, 0, vb=values(i * 2 - 1))
                att(i * 2 + 1, 1, vb=values(i * 2))
            att(6, 0, vb=values(5))
            att(7, 1, vb=values(6))
            att(8, 0, nq=DEC, vb=values(7))
            att(9, 1, scores=False, vb=values(9))
            pe.wait_ge(ssm_rot, mark["H"])
            pe.wait_ge(cm_ld, 16)
            pe.wait_ge(tm_made, 1)
            pe.wait_ge(*ab_act.at("YB", 8))
            for g in range(32):
                t, q = g // 2, g % 2
                b = g % 8
                if g >= 8:
                    pe.wait_ge(ssm_act, g - 7)
                r = slice(64 * q, 64 * q + 64)
                o = PS[:, b, 0:CC]
                pe.matmul(o, TM[:, g, :], UG[:, g, :], start=True, stop=False)
                pe.matmul(o, CM[r, 0, t, :], HR[r, t, 0:CC], start=False, stop=False)
                pe.matmul(o, CM[r, 1, t, :], HI[r, t, 0:CC], start=False, stop=True).then_inc(ssm_y, 1)
            pe.wait_ge(ssm_act, 32)

            pe.wait_ge(*glu_vec.at("bl3"))
            n = N0["outb"]
            for b in range(4):
                block_b(n + b, b % 2, [(add["out"], max(4 * b + o - 1, 1)) if 4 * b + o >= 2 else (ssm_act, 32) for o in range(4)],
                        H=XH, L=XL, k0=2 * (b // 2))
            n = N0["glu"]
            for o in range(4):
                s = o // 2
                if o == 0:
                    pe.wait_ge(*glu_vec.at("gl3"))
                if o < 2:
                    pe.wait_ge(add["out"], 15 + o)
                else:
                    pe.wait_ge(*glu_act.at(f"sig{o - 2}"))
                tile_a(n + s, s, o % 2, kt=4, H=GH, L=GL,
                       lhs=lambda k: (WH[:, s, k * 256 + (o % 2) * P:k * 256 + (o % 2) * P + P],
                                      WL[:, s, k * 256 + (o % 2) * P:k * 256 + (o % 2) * P + P]))
            n = N0["outa"]
            pe.wait_ge(*glu_vec.at("lo3"))
            for b in range(4):
                block_b(n + b, b % 2, [(add["out"], 16 + 4 * b + o - 1) if 4 * b + o >= 2 else glu_act.at(f"sig{2 + o}") for o in range(4)],
                        H=XH, L=XL, k0=4 + 2 * (b // 2))

            def cross(l):
                q = f"x{l}"
                n = N0[q]

                def head(i, first):
                    for s in (0, 1):
                        pe.wait_ge(w_lo, i * 4 + (n + s + 1))
                        if first:
                            pe.wait_ge(add["out" if l == 0 else "c1"], 31 + s)
                        else:
                            pe.wait_ge(add[q], i * 8 + (s - 1))
                        tile_a(0, s, s, wait_lo=False, split=q if first and s == 0 else None)
                        if first and s == 0:
                            norm_total(q)
                    pe.wait_ge(*xv[l].at("q1", i))
                    pe.wait_ge(xld[l], i * 64 + 64)
                    if first:
                        pe.wait_ge(n_rs[q], 6)
                    for k in range(12):
                        t = k
                        if t < 9:
                            nq, c0, st = (P, t * P, 0) if t < 8 else (DEC, S0, 1)
                            if t >= 2:
                                pe.wait_ge(*xa[l].at(f"ex{t - 2}", i))
                            for d in range(2):
                                mm = pe.matmul(PS[0:nq, t % 2, 0:NMEM], XQ[:, d, c0:c0 + nq], KX[:, st, d, :], start=(d == 0), stop=(d == 1))
                            mm.then_inc(xp[l].sem, 1)
                        t = k - 1
                        if 0 <= t < 9:
                            nq = P if t < 8 else DEC
                            pe.wait_ge(*xa[l].at(f"ex{t}", i))
                            if t == 8:
                                pe.nop(nofuse=True)
                            for m in range(2):
                                mm = pe.transpose(PS[:, 2 + t % 2, m * P:m * P + nq], PX[0:nq, t % 2, m * P:(m + 1) * P], IDENT[0:nq, 0:nq])
                            mm.then_inc(xp[l].sem, 1)
                        t = k - 2
                        if 0 <= t < 9:
                            nq, st = (P, 0) if t < 8 else (DEC, 1)
                            pe.wait_ge(*xa[l].at(f"pt{t}", i))
                            if t >= 2:
                                pe.wait_ge(*xv[l].at(f"ov{t - 2}", i))
                            for m in range(2):
                                mm = pe.matmul(PS[0:nq, 4 + t % 2, 0:NMEM].rearrange("p (d e) -> p d e", d=2), PXT[:, t % 2, m, 0:nq],
                                               VX[:, st, :, m, :], start=(m == 0), stop=(m == 1))
                            mm.then_inc(xp[l].sem, 1)
                        t = k - 3
                        if 0 <= t < 9:
                            nq = P if t < 8 else DEC
                            pe.wait_ge(*xv[l].at(f"ov{t}", i))
                            if t == 8:
                                pe.nop(nofuse=True)
                            for d in range(2):
                                mm = pe.transpose(PS[:, 6 + t % 2, d * P:d * P + nq], OX[0:nq, t % 2, d * P:(d + 1) * P], IDENT[0:nq, 0:nq])
                            mm.then_inc(xp[l].sem, 1)
                    pe.wait_ge(*xv[l].at("lo8", i))
                    for b in range(2):
                        marks = [xv[l].at("ov8", i) if b == 0 and o < 2 else (add[q], i * 8 + (4 * b + o - 1)) for o in range(4)]
                        block_b(i * 4 + (n + 2 + b), b, marks)

                head(0, True)
                with pe.Fori(1, HEADS) as i:
                    head(i, False)

            def a_tile(n, s, ps, free, wait_x=None, q=None):
                pe.wait_ge(w_lo, n + 1)
                pe.wait_ge(*free)
                tile_a(0, s, ps, wait_lo=False, split=wait_x)
                if wait_x:
                    norm_total(wait_x)

            def down(nb, s0, ready, free, p0):
                pe.wait_ge(*ready)
                for b in range(2):
                    pe.wait_ge(w_lo, nb + (b + 1))
                    for o in range(4):
                        if free(4 * b + o):
                            pe.wait_ge(*free(4 * b + o))
                        down_tile((s0 + b) % 2, o, (p0 + o) % 2)

            def ffn(l):
                q, v = f"f{l}", fv[l]
                n = N0[q]
                before = add[f"x{l}"]
                a_tile(n, 0, 0, (before, 31), wait_x=q)
                a_tile(n + 1, 1, 1, (before, 32))
                a_tile(n + 2, 0, 0, v.at("gate0"))
                a_tile(n + 3, 1, 1, v.at("hid0"))
                with pe.Fori(1, 11) as g:
                    nb = g * 6 + (n - 2)
                    a_tile(nb, 0, 0, v.at("gate1", g - 1))
                    down(nb + 1, 1, v.at("lo1", g - 1),
                         lambda j: None if j == 0 else v.at("gate0", g) if j == 1 else (add[q], g * 8 + (j - 9)), 1)
                    a_tile(nb + 3, 1, 1, (add[q], g * 8 - 1))
                    a_tile(nb + 4, 0, 0, (add[q], g * 8))
                    a_tile(nb + 5, 1, 1, v.at("hid0", g))
                down(n + 64, 0, v.at("lo1", 10),
                     lambda j: None if j < 2 else (add[q], 79 + j), 0)

            def down_tile(s, o, ps):
                for k in range(2):
                    w = slice(k * 512 + o * P, k * 512 + (o + 1) * P)
                    for c in range(NCH):
                        mm = mms(PS[:, 3 * ps + c, 0:CW], WH[:, s, w], WL[:, s, w], chunk(HH[:, k, :], c), chunk(HL[:, k, :], c),
                                 k == 0, k == 1)
                mm.then_inc(tile_done, 1)

            def conv():
                q, n = "c1", N0["c1"]
                a_tile(n, 0, 0, (add["f0"], 87), wait_x=q)
                a_tile(n + 1, 1, 1, (add["f0"], 88))
                for b, x in enumerate(("cc0", "zc0", "hid0", "cc1")):
                    a_tile(n + 2 + b, b % 2, b % 2, cv.at(x))
                with pe.Fori(1, 4) as g:
                    nb = g * 8 + (n - 2)
                    a_tile(nb, 0, 0, cv.at("zc1", g - 1))
                    down(nb + 1, 1, cv.at("lo1", g - 1),
                         lambda j: None if j == 0 else cv.at("cc0", g) if j == 1 else (add[q], g * 8 + (j - 9)), 1)
                    a_tile(nb + 3, 1, 1, (add[q], g * 8 - 1))
                    a_tile(nb + 4, 0, 0, (add[q], g * 8))
                    for b, x in enumerate(("zc0", "hid0", "cc1")):
                        a_tile(nb + (5 + b), (1 + b) % 2, (1 + b) % 2, cv.at(x, g))
                down(n + 30, 0, cv.at("lo1", 3),
                     lambda j: None if j < 2 else (add[q], 23 + j), 0)

            cross(0)
            ffn(0)
            conv()
            cross(1)
            ffn(1)
            norm_total("fin")

        @block.sync
        def _(sp):
            sp.dma_start(MR[:], a["memT"]).then_inc(ld, 16)
            sp.dma_start(COL[:], a["cols"]).then_inc(ld, 16)
            sp.dma_start(IDENT[:], a["ident"]).then_inc(ld, 16)

            def block_at(n):
                return a["w"][bass.ds(n, 1)].rearrange("o p n -> (o p) n")

            for s in range(4):
                if s == 2:
                    sp.wait_ge(mem_lo, 1)
                sp.dma_start(kv_slot(s)[0], a["w"][s]).then_inc(kv_raw[s], 16)
            with sp.Fori(1, N0["inp"] // 4) as i:
                for s in range(4):
                    sp.wait_ge(w_lo, i * 4 + (s - 3))
                    sp.dma_start(kv_slot(s)[0], block_at(i * 4 + s)).then_inc(kv_raw[s], 16)
            for s in (0, 1):
                sp.wait_ge(w_lo, N0["inp"] - 3 + s)
                sp.dma_start(WR[:, s, :], a["w"][N0["inp"] + s]).then_inc(w_raw[s], 16)
            with sp.Fori(N0["inp"] // 2 + 1, NBLOCKS // 2) as i:
                for s in (0, 1):
                    sp.wait_ge(w_lo, i * 2 + (s - 1))
                    sp.dma_start(WR[:, s, :], block_at(i * 2 + s)).then_inc(w_raw[s], 16)
            for m in range(KT):
                sp.wait_ge(fin, m + 1)
                sp.dma_start(a["y"][:, m, :], X[:, m, :]).then_inc(outs, 16)
            sp.wait_ge(outs, 16 * KT)

        @block.gpsimd
        def _(pool):
            def lo_block(n, s):
                pool.wait_ge(w_hi, n + 1)
                pool.tensor_tensor(WL[:, s, :], WR[:, s, :], WH[:, s, :].bitcast(F32), ALU.subtract).then_inc(w_lo, 1)

            def sum_squares(q, m):
                pool.wait_ge(*n_act[q].at(f"sq{m}"))
                sq = QR[:, m % 2, :] if q == "inp" else SQ[:, m % 2, :]
                if m == 0:
                    pool.tensor_copy(RSTD[:], sq).then_inc(n_sum[q], 1)
                else:
                    pool.wait_ge(n_sum[q], m)
                    pool.tensor_tensor(RSTD[:], RSTD[:], sq, ALU.add).then_inc(n_sum[q], 1)

            done = [0]

            def blocks(upto):
                lo, hi = done[0] // 2, upto // 2
                with pool.Fori(lo, hi) as i:
                    for s in (0, 1):
                        lo_block(i * 2 + s, s)
                done[0] = upto

            with pool.Fori(0, N0["inp"] // 4) as i:
                for s in range(4):
                    pool.wait_ge(w_hi, i * 4 + (s + 1))
                    raw, h, l = kv_slot(s)
                    pool.tensor_tensor(l, raw, h.bitcast(F32), ALU.subtract).then_inc(w_lo, 1)
            for m in range(KT):
                sum_squares("inp", m)
                if m == 1:
                    done[0] = N0["inp"]
                    blocks(N0["inp"] + 2)
            blocks(N0["outb"])

            def do(ins):
                rot[0] += 1
                ins.then_inc(ssm_rot, 1)
                pool.wait_ge(ssm_rot, rot[0])
            rot = [0]
            segments = ((1, NCK, 0), (NCK + 2, DEC // CK, NCK))
            pool.wait_ge(tm_made, 1)
            pool.wait_ge(ssm_copy, 32)
            for lo, w, so in segments:
                hr, hi = HR[:, :, lo:lo + w], HI[:, :, lo:lo + w]
                er, ei = ER[:, :, 1:w + 1], EI[:, :, 1:w + 1]
                s1, s2 = S1[:, :, so:so + w], S2[:, :, so:so + w]
                do(pool.tensor_tensor(s1, er, hr, ALU.mult))
                do(pool.tensor_tensor(s2, ei, hi, ALU.mult))
                do(pool.tensor_tensor(s1, s1, s2, ALU.add))
                do(pool.tensor_tensor(s2, er, hi, ALU.mult))
                do(pool.tensor_tensor(hr, ei, hr, ALU.mult))
                do(pool.tensor_tensor(s2, s2, hr, ALU.subtract))
            pool.wait_ge(ssm_scan, 66)
            for lo, w, so in segments:
                hr, hi = HR[:, :, lo:lo + w], HI[:, :, lo:lo + w]
                er, ei = ER[:, :, 1:w + 1], EI[:, :, 1:w + 1]
                s1, s2 = S1[:, :, so:so + w], S2[:, :, so:so + w]
                do(pool.tensor_tensor(s1, er, hr, ALU.mult))
                do(pool.tensor_tensor(s2, ei, hi, ALU.mult))
                do(pool.tensor_tensor(hi, er, hi, ALU.mult))
                do(pool.tensor_tensor(hr, ei, hr, ALU.mult))
                do(pool.tensor_tensor(hi, hi, hr, ALU.add))
                do(pool.tensor_tensor(hr, s1, s2, ALU.subtract))
            do(pool.tensor_copy(HR[:, :, NCK + 1], col("h0_re", 0, 16)))
            do(pool.tensor_copy(HI[:, :, NCK + 1], col("h0_im", 0, 16)))
            for k, (h, c) in enumerate(((HR, NCK), (HI, NCK), (HR, CC), (HI, CC))):
                do(pool.tensor_copy(SMALL[:, 16 * k:16 * k + 16], h[:, :, c]))
            assert rot[0] == mark["S"]
            for ph, nxt in (("out", "x0"), ("x0", "f0"), ("f0", "c1"), ("c1", "x1"), ("x1", "f1"), ("f1", "fin")):
                start = N0[nxt] if nxt != "fin" else NBLOCKS
                blocks(start)
                for b in range(2):
                    for m in range(4):
                        sum_squares(nxt, 4 * b + m)
                    if nxt != "fin":
                        lo_block(start + b, b)
                done[0] = start + 2

        @block.scalar
        def _(act):
            def hi_block(n, s):
                act.wait_ge(w_raw[s], (n - s) * 8 + (16 - 8 * N0["inp"]))
                act.activation(WH[:, s, :], WR[:, s, :], ACT.Copy).then_inc(w_hi, 1)

            def step(n, s, tiles):
                act.wait_ge(tile_done, tiles)
                hi_block(n + 2, s)

            def norm_tile(q, m, x_final):
                act.wait_ge(*x_final)
                if m >= 2:
                    act.wait_ge(n_sum[q], m - 1)
                sq = QR[:, m % 2, :] if q == "inp" else SQ[:, m % 2, :]
                act.activation(sq, X[:, m, :], ACT.Square).then_inc(n_act[q].sem, 1)
                if q != "fin":
                    act.activation(XH[:, m, :], X[:, m, :], ACT.Copy, scale=col(GAIN[q], m)).then_inc(n_act[q].sem, 1)

            def rstd(q):
                for c in range(NCH):
                    act.wait_ge(n_tot[q], c + 1)
                    act.activation(chunk(LNV[:], c), PS[:, 6 + c % 2, 0:CW], ACT.Ln, bias=EPSC[:], scale=1.0 / D).then_inc(n_rs[q], 1)
                act.wait_ge(n_rs[q], 3)
                for c in range(NCH):
                    act.activation(chunk(RSTD[:], c), chunk(LNV[:], c), ACT.Exp, scale=-0.5).then_inc(n_rs[q], 1)

            act.wait_ge(ld, 48)
            act.activation(MH[:], MR[:], ACT.Copy).then_inc(mem_hi, 1)

            def kv_hi(s, q):
                act.wait_ge(kv_raw[s], q * 16 + 16)
                raw, h, _ = kv_slot(s)
                act.activation(h, raw, ACT.Copy).then_inc(w_hi, 1)

            def kv_block(part, q, s):
                act.wait_ge(tile_done, q * 4 + (s + 1))
                if not (isinstance(q, int) and q == 7):
                    kv_hi(s, q + 1)
                elif s < 2:
                    hi_block(N0["inp"] + s, s)
                if part % 2 == 0:
                    act.activation(KVS[:, part % 2, bass.ds(q * 4 + (s - 8 * part), 1), :].rearrange("p o m -> p (o m)"),
                                   PS[:, 3 * (s % 2), 0:NMEM], ACT.Copy).then_inc(kv_copy, 1)
                elif s % 2:
                    for mt in range(2):
                        act.activation(KVS[:, part % 2, bass.ds(q * 4 + (s - 1 - 8 * part), 2), mt * P:(mt + 1) * P],
                                       PS[:, VALUE_BANKS[s // 2][mt], 0:256].rearrange("p (b c) -> p b c", b=2), ACT.Copy).then_inc(kv_copy, 1)

            def parameters():
                act.wait_ge(par_vec, mark["C"])
                act.dma_start(a["er"], ERP[:]).then_inc(par_dma, 16)
                act.dma_start(a["ei"], EIP[:]).then_inc(par_dma, 16)
                act.dma_start(a["cm"][:, 0], T1[:].rearrange("p t j h -> p (t j h)")).then_inc(par_dma, 16)
                act.dma_start(a["cm"][:, 1], T2[:].rearrange("p t j h -> p (t j h)")).then_inc(par_dma, 16)
                for k in range(8):
                    act.wait_ge(par_pe, k + 1)
                    act.activation(BTP[:, k // 4, 4 * (k % 4):4 * (k % 4) + 4, :].rearrange("p t c -> p (t c)"),
                                   PS[:, 6 + k % 2, :], ACT.Copy).then_inc(par_act, 1)
                act.wait_ge(par_act, 8)
                act.dma_start(a["bt"], BTP[:]).then_inc(par_dma, 16)
                act.wait_ge(par_vec, mark["K"])
                for j in range(8):
                    r = 16 * (7 - j)
                    act.dma_start(a["tm"][r:P, j, :], KR[0:P - r, :]).then_inc(par_dma, 16)
                    if r:
                        act.dma_start(a["tm"][0:r, j, :], a["zeros"][0:r, :]).then_inc(par_dma, 16)

            for s in range(4):
                kv_hi(s, 0)
            for t, nm in ((BR, "b_re"), (BI, "b_im"), (CR, "c_re"), (CI, "c_im"), (DD, "d_diag")):
                act.dma_start(t[:], a[nm]).then_inc(par_ld, 16)
            for part in range(4):
                if part >= 2:
                    act.wait_ge(kv_out[part - 2], 16)
                if part < 3:
                    with act.Fori(2 * part, 2 * part + 2) as q:
                        for s in range(4):
                            kv_block(part, q, s)
                            if part < 2 and s % 2:
                                m = bass.ds(q * 2 + s // 2, 1)
                                act.dma_start(X[:, m, :], a["x"][:, m, :]).then_inc(x_ld, 16)
                else:
                    for s in range(4):
                        kv_block(3, 6, s)
                    parameters()
                    act.wait_ge(ready, 2)
                    for s in range(4):
                        kv_block(3, 7, s)
                        if s == 1:
                            act.wait_ge(par_dma, 16 * 20)
                        if s % 2:
                            for m in (s - 1, s):
                                norm_tile("inp", m, (x_ld, 16 * KT))
                act.wait_ge(kv_copy, 8 * part + 8)
                act.dma_start(a["memkv"][part], KVS[:, part % 2].rearrange("p b m -> p (b m)")).then_inc(kv_out[part], 16)

            act.dma_start(COS[:], a["cos"]).then_inc(mix_ld, 16)
            act.dma_start(SIN[:], a["sin"]).then_inc(mix_ld, 16)
            for m in range(4, KT):
                norm_tile("inp", m, (x_ld, 16 * KT))
            for s in kv_out:
                act.wait_ge(s, 16)
            act.dma_start(ROT[:], a["rot"]).then_inc(mix_ld, 16)
            act.dma_start(MASK[:], a["mask"]).then_inc(mix_ld, 16)
            act.dma_start(KB[:, 1152:1280], a["past_k"]).then_inc(mix_ld, 16)
            act.dma_start(VB[:, 9, :], a["past_v"]).then_inc(mix_ld, 16)
            n = N0["inp"]
            for j, x in enumerate(INP):
                if x in INP_BLOCKS:
                    if n < N0["outb"] - 2:
                        step(n, n % 2, T0["inp"] + j + 1)
                    n += 1
                if j == 0:
                    rstd("inp")
                if x == "VT":
                    s = j % 2
                    act.wait_ge(tile_done, T0["inp"] + j + 1)
                    act.wait_ge(zeroed, mark["Z"])
                    act.activation(VB[:, 1:9, :].rearrange("p (b s) c -> p b (s c)", b=2), PS[:, 3 * s:3 * s + 2, :], ACT.Copy).then_inc(iact.sem, 1)
                    act.activation(VB[0:DEC, 10, :], PS[0:DEC, 3 * s + 2, 0:P], ACT.Copy).then_inc(iact.sem, 1)
                if x == "q1":
                    act.wait_ge(*ivec.at("u3S"))
                    act.dma_start(a["uj"].rearrange("(t g) c j k -> (g c) t (j k)", g=8), UJ[:].rearrange("p t j c -> p t (j c)")).then_inc(uj_out, 16)
                if x == "q2":
                    act.wait_ge(uj_out, 16)
                    for r in range(CK):
                        act.dma_start(UG[16 * (7 - r):16 * (7 - r) + 16, :, :],
                                      a["uj"].rearrange("g c j k -> j c g k")[r]).then_inc(ug_in, 16)
            act.wait_ge(*ivec.at("rot_q3"))
            act.wait_ge(*iact.at("VTb"))
            act.dma_start(a["k_new"][:, 0:P], KB[:, 1024:1152]).then_inc(small_out, 16)
            act.dma_start(a["k_new"][:, P:P + DEC], KB[:, 1280:1312]).then_inc(small_out, 16)
            act.dma_start(a["v_new"][:, 0:P], VTT[:, SEQ - P:SEQ]).then_inc(small_out, 16)
            act.dma_start(a["v_new"][:, P:P + DEC], VTT[:, S0:TW]).then_inc(small_out, 16)
            act.wait_ge(tile_done, T0["outb"])
            for t, nm in ((BT, "bt"), (ER, "er"), (EI, "ei"), (TMR, "tm")):
                act.dma_start(t[:], a[nm]).then_inc(ssm_ld, 16)

            def queries(k, nq=P):
                cols = slice(S0, TW) if isinstance(k, int) and k == 8 else slice(k * P, k * P + P) if isinstance(k, int) else bass.ds(k * P, P)
                return Q[:, :, cols]

            def stage(k, nq=P):
                if not (isinstance(k, int) and k == 0):
                    act.wait_ge(*aa_pe.at("S", k - 1))
                    act.nop(nofuse=True)
                act.activation(QS[:, :, 0:nq], queries(k), ACT.Copy).then_inc(aa_act.sem, 1)
                act.activation(KS[:], KB[:, 1152:1408] if nq < P else KB[:, k * P:k * P + 256] if isinstance(k, int) else KB[:, bass.ds(k * P, 256)],
                               ACT.Copy).then_inc(aa_act.sem, 1)

            def att(k, s, nq=P, values=True, scores=True, then=P):
                j, z, nj = k - 1, 1 - s, P if scores else DEC
                if values:
                    for b, nm in enumerate(("PTa", "PTb")):
                        act.wait_ge(*ab_pe.at(nm, j))
                        act.activation(PT[:, 2 * b:2 * b + 2, :, 0:nj], PS[:, 4 + b, :].rearrange("p (h k q) -> p h k q", h=2, k=2)[:, :, :, 0:nj],
                                       ACT.Copy).then_inc(ab_act.sem, 1)
                if then:
                    stage(k + 1, then)
                if scores:
                    act.wait_ge(*aa_vec.at("ds", k))
                    for h in range(8):
                        act.activation(SB[0:nq, s, h, :], SB[0:nq, s, h, :], ACT.Exp, bias=SMX[0:nq, s, 8 + h:9 + h],
                                       accum_out=SMX[0:nq, s, 16 + h:17 + h]).then_inc(aa_act.sem, 1)
                    act.activation(SMX[0:nq, s, 24:32], SMX[0:nq, s, 40:48], ACT.Exp).then_inc(aa_act.sem, 1)
                if values:
                    act.wait_ge(*ab_pe.at("OT", j))
                    act.nop(nofuse=True)
                    act.activation(Q[:, :, S0:TW] if not scores else queries(j), PS[:, 7, :].rearrange("p (j q) -> p j q", j=4)[:, :, 0:nj],
                                   ACT.Copy).then_inc(ab_act.sem, 1)

            stage(0)
            att(0, 0, values=False)
            att(1, 1)
            act.wait_ge(ssm_ld, 64)
            act.activation(TM[:].rearrange("p g (j h) -> p j g h", j=CK), TMR[:].rearrange("p j (g h) -> p j g h", g=32),
                           ACT.Copy).then_inc(tm_made, 1)
            act.wait_ge(ssm_v, 32)
            act.dma_start(CM[:].rearrange("p r t m -> p r (t m)"), a["cm"]).then_inc(cm_ld, 16)
            with act.Fori(1, 3) as i:
                att(i * 2, 0)
                att(i * 2 + 1, 1)
            att(6, 0)
            att(7, 1, then=DEC)
            att(8, 0, nq=DEC, then=0)
            att(9, 1, scores=False, then=0)
            act.wait_ge(small_out, 64)
            act.wait_ge(*ab_pe.at("PTd", 8))
            for s in (0, 1):
                hi_block(N0["outb"] + s, s)

            for g in range(32):
                act.wait_ge(ssm_y, 1 + g)
                act.activation(UG[:, g, :], PS[:, g % 8, 0:CC], ACT.Copy).then_inc(ssm_act, 1)
            act.wait_ge(ssm_act, 32)
            for j in range(CK):
                act.dma_start(a["yj"].rearrange("g c j k -> j c g k")[j], UG[16 * j:16 * j + 16, :, :]).then_inc(y_out, 16)
            act.wait_ge(ssm_rot, mark["S"])
            for j in range(4):
                act.activation(XH[:, j, :], Q[:, j, :], ACT.Copy).then_inc(glu_act.sem, 1)
            act.dma_start(a["ssm_new"], SMALL[:]).then_inc(small_out, 16)
            act.wait_ge(y_out, 16 * CK)
            act.dma_start(UJ[:].rearrange("p t j c -> p t (j c)"), a["yj"].rearrange("(t g) c j k -> (g c) t (j k)", g=8)).then_inc(y_in, 16)
            act.wait_ge(*glu_vec.at("bl3"))
            act.wait_ge(y_in, 16)
            n = N0["outb"]
            for j in range(4):
                act.activation(GY[:, j, 0:SEQ].rearrange("p (c j) -> p c j", j=CK), UJ[:, j, :, 0:NCK].rearrange("p j c -> p c j"),
                               ACT.Gelu_apprx_tanh).then_inc(glu_act.sem, 1)
                act.activation(GY[:, j, S0:TW].rearrange("p (c j) -> p c j", j=CK), UJ[:, j, :, NCK + 1:CC].rearrange("p j c -> p c j"),
                               ACT.Gelu_apprx_tanh).then_inc(glu_act.sem, 1)
                act.wait_ge(*glu_act.at(f"gs{j}"))
                act.activation(GH[:, j, :], GY[:, j, :], ACT.Copy).then_inc(glu_act.sem, 1)
                if j % 2:
                    step(n + j // 2, j // 2, T0["outb"] + 4 * (j // 2) + 4)
            for b in (2, 3):
                step(n + b, b % 2, T0["outb"] + 4 * b + 4)
            n = N0["glu"]
            for o in range(4):
                act.wait_ge(tile_done, T0["glu"] + o + 1)
                if o:
                    act.wait_ge(*glu_vec.at(f"mul{o - 1}"))
                act.activation(tiled(LNV[:]), pset(o % 2), ACT.Sigmoid).then_inc(glu_act.sem, 1)
                if o % 2:
                    step(n + o // 2, o // 2, T0["glu"] + o + 1)
                act.wait_ge(*glu_vec.at(f"mul{o}"))
                act.activation(XH[:, 4 + o, :], GY[:, o, :], ACT.Copy).then_inc(glu_act.sem, 1)

            def last_norm(ph, n, t, nxt, whole=None):
                for b in range(2):
                    for m in range(4 * b, 4 * b + 4):
                        if whole and m == 6:
                            act.wait_ge(tile_done, whole)
                        norm_tile(nxt, m, (add[ph], ADDS[ph] - KT + m + 1))
                    if nxt != "fin":
                        step(n + b, b, t + 4 * b + 4)

            n, t = N0["outa"], T0["outa"]
            for b in range(2):
                step(n + b, b % 2, t + 4 * b + 4)
            last_norm("out", n + 2, t + 8, "x0", whole=T0["x0"])

            def cross(l, nxt):
                q, v, ac, te = f"x{l}", xv[l], xa[l], xp[l]
                n, t0 = N0[q], T0[q]

                def loads(h):
                    for st, src in ((0, "memkv"), (1, "smemkv")):
                        act.dma_start(KX[:, st].rearrange("p d m -> p (d m)"), a[src][2 * l][:, bass.ds(h * 512, 512)]).then_inc(xld[l], 16)
                        act.dma_start(VX[:, st].rearrange("p d m e -> p (d m e)"), a[src][2 * l + 1][:, bass.ds(h * 512, 512)]).then_inc(xld[l], 16)

                def head(i, first=False, last=False):
                    for s in (0, 1):
                        step(i * 4 + (n + s), s, i * 10 + (t0 + s + 1))
                        if first and s == 0:
                            rstd(q)
                    for k in range(12):
                        t = k
                        if t < 9:
                            nq = P if t < 8 else DEC
                            act.wait_ge(*v.at(f"nm{t}", i))
                            if t >= 2:
                                act.wait_ge(*te.at(f"T{t - 2}", i))
                            act.activation(PX[0:nq, t % 2, :], PS[0:nq, t % 2, 0:NMEM], ACT.Exp, bias=NX[0:nq, t % 3, 1:2], scale=1.0 / 16,
                                           accum_out=NX[0:nq, t % 3, 2:3]).then_inc(ac.sem, 1)
                        t = k - 1
                        if 0 <= t < 9:
                            nq = P if t < 8 else DEC
                            act.wait_ge(*te.at(f"T{t}", i))
                            act.activation(PXT[:, t % 2, :, 0:nq], PS[:, 2 + t % 2, 0:NMEM].rearrange("p (m q) -> p m q", m=2)[:, :, 0:nq],
                                           ACT.Copy).then_inc(ac.sem, 1)
                        t = k - 3
                        if 0 <= t < 9:
                            nq, c0 = (P, t * P) if t < 8 else (DEC, S0)
                            act.wait_ge(*te.at(f"O{t}", i))
                            act.activation(HH[:, :, c0:c0 + nq], PS[:, 6 + t % 2, 0:NMEM].rearrange("p (d q) -> p d q", d=2)[:, :, 0:nq],
                                           ACT.Copy).then_inc(ac.sem, 1)
                    if not last:
                        loads(i + 1)
                        for b in range(2):
                            step(i * 4 + (n + 2 + b), b, i * 10 + (t0 + 6 + 4 * b))
                    else:
                        last_norm(q, n + 14, t0 + 32, nxt)

                loads(0)
                head(0, first=True)
                with act.Fori(1, HEADS - 1) as i:
                    head(i)
                head(HEADS - 1, last=True)

            def new_states(s, g, e):
                act.activation(STF[:, 0:2, bass.ds(g * 2 + e, 1)].rearrange("p s o -> p (s o)"), G[:, e, SEQ:SEQ + 2], ACT.Copy).then_inc(s.sem, 1)
                act.activation(STF[:, 2:4, bass.ds(g * 2 + e, 1)].rearrange("p s o -> p (s o)"), G[:, e, TW:TW + 2], ACT.Copy).then_inc(s.sem, 1)

            def ffn(l, nxt):
                q, v, ac = f"f{l}", fv[l], fa[l]
                n, t0 = N0[q], T0[q]

                def gated(g, e):
                    act.wait_ge(*v.at(f"c{e}", g))
                    if e == 1:
                        act.wait_ge(*v.at("sm0", g))
                    elif not (isinstance(g, int) and g == 0):
                        act.wait_ge(*v.at("sm1", g - 1))
                    act.activation(ACTV[:], TAP[:, e, :], ACT.Silu).then_inc(ac.sem, 1)
                    new_states(ac, g, e)

                def high(g, e):
                    act.wait_ge(*v.at(f"hid{e}", g))
                    act.activation(HH[:, e, :], HID[:], ACT.Copy).then_inc(ac.sem, 1)

                def group(g, nb, t, first=False):
                    step(nb, 0, t + 1)
                    if first:
                        rstd(q)
                    o, b0 = (1, 1) if first else (9, 3)
                    gated(g, 0)
                    if not first:
                        for b in range(2):
                            step(nb + (1 + b), (1 + b) % 2, t + (5 + 4 * b))
                    step(nb + b0, b0 % 2, t + (o + 1))
                    high(g, 0)
                    step(nb + (b0 + 1), (b0 + 1) % 2, t + (o + 2))
                    gated(g, 1)
                    step(nb + (b0 + 2), (b0 + 2) % 2, t + (o + 3))
                    high(g, 1)

                group(0, n, t0, True)
                with act.Fori(1, 11) as g:
                    group(g, g * 6 + (n - 2), g * 12 + (t0 - 8))
                act.wait_ge(*ac.at("nb1", 10))
                act.dma_start(a[f"st_f{l}"], STF[:]).then_inc(st_out[q], 16)
                last_norm(q, n + 64, t0 + 124, nxt)
                act.wait_ge(st_out[q], 16)

            def conv(nxt):
                n, t0 = N0["c1"], T0["c1"]

                def high(g, e):
                    act.wait_ge(*cv.at(f"zc{e}", g))
                    act.nop(nofuse=True)
                    new_states(ca, g, e)
                    act.wait_ge(*cv.at(f"hid{e}", g))
                    act.activation(HH[:, e, :], HID[:], ACT.Copy).then_inc(ca.sem, 1)

                def group(g, nb, t, first=False):
                    step(nb, 0, t + 1)
                    if first:
                        rstd("c1")
                    o, b0 = (1, 1) if first else (9, 3)
                    if not first:
                        for b in range(2):
                            step(nb + (1 + b), (1 + b) % 2, t + (5 + 4 * b))
                    step(nb + b0, b0 % 2, t + (o + 1))
                    step(nb + (b0 + 1), (b0 + 1) % 2, t + (o + 2))
                    high(g, 0)
                    for b in (2, 3, 4):
                        step(nb + (b0 + b), (b0 + b) % 2, t + (o + b + 1))
                    high(g, 1)

                group(0, n, t0, True)
                with act.Fori(1, 4) as g:
                    group(g, g * 8 + (n - 2), g * 14 + (t0 - 8))
                act.wait_ge(*ca.at("hi1", 3))
                act.dma_start(a["st_c1"], STF[:, :, 0:KT]).then_inc(st_out["c1"], 16)
                last_norm("c1", n + 30, t0 + 48, nxt)
                act.wait_ge(st_out["c1"], 16)

            cross(0, "f0")
            ffn(0, "c1")
            conv("x1")
            cross(1, "f1")
            ffn(1, "fin")
            rstd("fin")
            act.wait_ge(small_out, 80)




def _layout(i):
    f = {k: np.asarray(v) for k, v in i.items()}

    def kblocks(w):
        k, n = w.shape
        return w.reshape(KT, P, n // P, P).transpose(2, 1, 0, 3).reshape(n // P, P, BLK)

    def rows2(w):
        n = w.shape[0]
        return w.reshape(n // 256, 2, P, 2, 512).transpose(0, 3, 2, 1, 4).reshape(-1, P, BLK)

    pair = np.array([h * 64 + d for j in range(4) for h in (j, j + 4) for d in range(64)])
    we = f["w_in_even"][0]
    u, q, k, v = we[:, :512], we[:, 512:1024][:, pair], we[:, 1024:1152], we[:, 1152:1280]
    inp = {"k": kblocks(k)[0], "v": kblocks(v)[0]}
    inp.update({f"u{t}": kblocks(u)[t] for t in range(4)})
    inp.update({f"q{t}": kblocks(q)[t] for t in range(4)})
    wg = f["w_glu"][0].reshape(4, P, 2, 256).transpose(2, 1, 0, 3).reshape(2, P, BLK)
    wo = f["w_out_even"][0]
    wo = np.concatenate([wo[:512], wo[512:][pair]])
    blocks = []
    for l in (0, 1):
        wkv = f["xattn_wkv"][l]
        blocks += list(kblocks(wkv[:, :D]))
        blocks += list(wkv[:, D:].reshape(2, 4, P, 4, 256).transpose(3, 0, 2, 1, 4).reshape(8, P, BLK))
    wo = list(rows2(wo))
    blocks += [inp[x] for x in INP_BLOCKS] + wo[4:] + list(wg) + wo[:4]

    def skewed(a_of, na, down, groups):
        down = list(rows2(down))
        for g in range(groups):
            aa = a_of(g)
            blocks.append(aa[0])
            if g:
                blocks.extend(down[2 * g - 2:2 * g])
            blocks.extend(aa[1:])
        blocks.extend(down[-2:])

    for l in (0, 1):
        if l == 1:
            w = kblocks(f["w_in_odd"][0])
            skewed(lambda g: [w[c * KT + 2 * g + e] for e in (0, 1) for c in (1, 2, 0)], 6, f["w_out_odd"][0], 4)
        wq, wx = kblocks(f["xattn_wq"][l]), rows2(f["xattn_wo"][l])
        for h in range(HEADS):
            blocks += [wq[2 * h], wq[2 * h + 1], wx[2 * h], wx[2 * h + 1]]
        w = kblocks(f["ffn_w_up"][l])
        skewed(lambda g: [w[c * FT + 2 * g + e] for e in (0, 1) for c in (0, 1)], 4, f["ffn_w_down"][l], 11)
    w = np.stack(blocks)
    assert w.shape == (NBLOCKS, P, BLK)

    def feat(x):
        return x.reshape(x.shape[0], -1, P).transpose(2, 1, 0)

    cols = np.zeros((P, NCOL), np.float32)

    def put(name, x):
        c, n = COLS[name]
        cols[:, c:c + n] = x.reshape(P, n)
    for nm, key in (("mix", "norm_mix"), ("x", "norm_xattn"), ("f", "norm_ffn")):
        for l in (0, 1):
            put(f"g_{nm}{l}", f[key][l].reshape(KT, P).T)
    put("g_fin", f["norm_final"].reshape(KT, P).T)
    put("cm_w", f["conv_mix_w"][0].reshape(3 * KT, P).T)
    put("cm_s", f["state_conv_mix"][0, 0].reshape(2 * KT, P).T)
    for l in (0, 1):
        put(f"cf_w{l}", f["ffn_conv_w"][l].reshape(3 * FT, P).T)
        put(f"cf_s{l}", f["state_conv_ffn"][l, 0].reshape(2 * FT, P).T)
    put("sink", np.broadcast_to(f["attn_sinks"][0], (P, 8)))
    for nm, key in (("a_re", "ssm_a_re"), ("a_im", "ssm_a_im"), ("log_dt", "ssm_log_dt")):
        put(nm, f[key][0].reshape(16, P).T)
    put("h0_re", f["state_ssm_re"][0, 0].reshape(16, P).T)
    put("h0_im", f["state_ssm_im"][0, 0].reshape(16, P).T)

    x = np.zeros((P, KT, TW), np.float32)
    x[:, :, :SEQ] = feat(f["x_prompt"][0])
    x[:, :, S0:] = feat(f["x_sample"][0])
    smem = []
    for l in (0, 1):
        smem.append(feat(f["cache_mem_k"][l, 0].reshape(NMEM, D)).reshape(P, 2048))
        smem.append(f["cache_mem_v"][l, 0].reshape(2, P, KT, P).transpose(1, 2, 0, 3).reshape(P, 2048))

    def state(x):
        return x.reshape(16, P, -1).transpose(1, 0, 2)

    def cstate(x):
        return x.reshape(16, 2, 16, 64).transpose(1, 3, 0, 2).reshape(P, 16, 16)
    dd = np.zeros((16, 32, 16), np.float32)
    dd[np.arange(16), :, np.arange(16)] = f["ssm_d"][0].T

    inv = np.float32(10000.0) ** (-np.arange(32, dtype=np.float32) * np.float32(2.0) / np.float32(64))
    pos = np.zeros(TW, np.float32)
    pos[:SEQ], pos[S0:] = np.arange(SEQ), 512 + np.arange(DEC)
    ang = (pos[None, :] * inv[:, None]).astype(np.float32)
    rot = np.zeros((P, P), np.float32)
    for b in (0, 64):
        for m in range(32):
            rot[b + 32 + m, b + m] = -1.0
            rot[b + m, b + 32 + m] = 1.0
    mask = np.full((P, 3, 256), NEG, np.float32)
    mask[:64, 0, 128:192] = 0
    mask[64:, 0, 128:256] = 0
    mask[:64, 1, 0:192] = 0
    mask[64:, 1, 64:256] = 0
    mask[:, 2, 0:160] = 0
    return {
        "w": w, "cols": cols, "x": x, "memT": np.ascontiguousarray(feat(f["mem_prompt"][0])), "smemkv": np.stack(smem),
        "past_k": f["cache_win_k"][0, 0].reshape(128, P).T, "past_v": f["cache_win_v"][0, 0].reshape(128, P),
        "b_re": state(f["ssm_b_re"][0]), "b_im": state(f["ssm_b_im"][0]),
        "c_re": cstate(f["ssm_c_re"][0]), "c_im": cstate(f["ssm_c_im"][0]), "d_diag": dd.reshape(16, 512),
        "ident": np.eye(P, dtype=np.float32), "zeros": np.zeros((P, 512), np.float32), "rot": rot, "mask": mask,
        "cos": np.tile(np.cos(ang.astype(np.float64)).astype(np.float32), (4, 1)),
        "sin": np.tile(np.sin(ang.astype(np.float64)).astype(np.float32), (4, 1)),
    }


_OUTS = {"y": (P, KT, TW), "memkv": (4, P, 2048), "k_new": (P, P + DEC), "v_new": (P, P + DEC), "ssm_new": (P, 64),
         "st_f0": (P, 4, FT), "st_f1": (P, 4, FT), "st_c1": (P, 4, KT)}
_SCRATCH = {"uj": (32, 16, CK, CC), "yj": (32, 16, CK, CC), "bt": (P, 2, 16, P), "er": (P, 16, NCK + 1), "ei": (P, 16, NCK + 1),
            "cm": (P, 2, 2048), "tm": (P, CK, 512)}


def kernel(**inputs):
    import concourse.bacc as _bacc
    from concourse.bass_utils import run_bass_kernel_spmd as _run

    nc = _bacc.Bacc("TRN2", target_bir_lowering=False, num_devices=1)
    arrays = {f"in_{k}": np.ascontiguousarray(v) for k, v in _layout(inputs).items()}
    a = {k[3:]: nc.dram_tensor(k, v.shape, F32, kind="ExternalInput").ap() for k, v in arrays.items()}
    for k, s in _OUTS.items():
        a[k] = nc.dram_tensor(f"out_{k}", s, F32, kind="ExternalOutput").ap()
    for k, s in _SCRATCH.items():
        a[k] = nc.dram_tensor(f"scratch_{k}", s, F32, kind="Internal").ap()
    build(nc, a)
    r = _run(nc, [arrays], core_ids=[0]).results[0]
    o = {k: np.asarray(r[f"out_{k}"]) for k in _OUTS}

    def tokens(x):
        return np.ascontiguousarray(x.transpose(2, 1, 0)).reshape(x.shape[2], -1)
    y = tokens(o["y"])
    yp, ys = y[None, :SEQ], y[None, S0:]
    kw, vw = o["k_new"].T, o["v_new"].T
    ssm = [o["ssm_new"][:, 16 * k:16 * k + 16].T.reshape(1, 1, 32, 64) for k in range(4)]
    conv = {q: o[q].transpose(1, 2, 0).reshape(4, -1) for q in ("st_f0", "st_f1", "st_c1")}
    cf = np.stack([conv["st_f0"], conv["st_f1"]])
    mk = np.stack([tokens(o["memkv"][2 * l].reshape(P, KT, NMEM)) for l in (0, 1)])
    mv = np.stack([o["memkv"][2 * l + 1].reshape(P, KT, 2, P).transpose(2, 0, 1, 3).reshape(NMEM, D) for l in (0, 1)])
    out = (yp, ys, kw[:P].reshape(1, 1, P, 2, 64), vw[:P].reshape(1, 1, P, 2, 64), ssm[0], ssm[1],
           conv["st_c1"][None, None, 0:2], cf[:, None, 0:2], mk.reshape(2, 1, NMEM, HEADS, 256), mv.reshape(2, 1, NMEM, HEADS, 256),
           kw[P:].reshape(1, 1, DEC, 2, 64), vw[P:].reshape(1, 1, DEC, 2, 64), ssm[2], ssm[3],
           conv["st_c1"][None, None, 2:4], cf[:, None, 2:4])
    return tuple(np.ascontiguousarray(x) for x in out)
```

```python
from contextlib import ExitStack

import numpy as np
import concourse.bass as bass
from concourse import mybir

F32, F32R, I32 = mybir.dt.float32, mybir.dt.float32r, mybir.dt.int32
ALU = mybir.AluOpType
ACT = mybir.ActivationFunctionType
AX = mybir.AxisListType

P = 128
D, KT = 1024, 8
SEQ, DEC = 1024, 32
NCH, CW = 3, 354
TW = NCH * CW
S0 = TW - DEC
F_FF, FT = 2816, 22
NMEM = 256
HEADS = 4
CK, NCK = 8, SEQ // 8
CC = NCK + 1 + DEC // CK
NEG = -1e30
BLK = 1024
VALUE_BANKS = ((4, 5), (0, 3))

PHASES = [("kv", 32, 32), ("inp", 10, 16), ("outb", 4, 16), ("glu", 2, 4), ("outa", 4, 16), ("x0", 16, 40), ("f0", 66, 132),
          ("c1", 32, 56), ("x1", 16, 40), ("f1", 66, 132)]
N0, T0 = {}, {}
_n = _t = 0
for _name, _b, _tl in PHASES:
    N0[_name], T0[_name] = _n, _t
    _n, _t = _n + _b, _t + _tl
NBLOCKS, NTILES = _n, _t
NEXT = {a[0]: b[0] for a, b in zip(PHASES, PHASES[1:])}

COLS = {}
_c = 0
for _name, _w in [("g_mix0", 8), ("g_x0", 8), ("g_f0", 8), ("g_mix1", 8), ("g_x1", 8), ("g_f1", 8), ("g_fin", 8),
                  ("cm_w", 24), ("cm_s", 16), ("cf_w0", 66), ("cf_s0", 44), ("cf_w1", 66), ("cf_s1", 44),
                  ("sink", 8), ("a_re", 16), ("a_im", 16), ("log_dt", 16), ("h0_re", 16), ("h0_im", 16)]:
    COLS[_name] = (_c, _w)
    _c += _w
NCOL = _c

INP = ["k", "v", "Rk", "q0", "VT", "q1", "Rq0", "q2", "Rq1", "q3", "Rq2", "u0", "Rq3", "u1", "u2", "u3"]
INP_BLOCKS = [x for x in INP if x[0] != "R" and x != "VT"]


class Steps:

    def __init__(self, sem, names):
        self.sem, self.n = sem, len(names)
        self.k = {x: i + 1 for i, x in enumerate(names)}

    def at(self, name, i=0):
        return self.sem, i * self.n + self.k[name]



GAIN = {"inp": "g_mix0", "x0": "g_x0", "f0": "g_f0", "c1": "g_mix1", "x1": "g_x1", "f1": "g_f1", "fin": "g_fin"}
QSLOT = {"k": 0, "q0": 1, "q1": 0, "q2": 1, "q3": 0}
ADDS = {"out": 32, "x0": 32, "f0": 88, "c1": 32, "x1": 32, "f1": 88}
CEXP = [1.0 / 5040, 1.0 / 720, 1.0 / 120, 1.0 / 24, 1.0 / 6, 0.5, 1.0]
CSIN = [1.0 / 6227020800, -1.0 / 39916800, 1.0 / 362880, -1.0 / 5040, 1.0 / 120, -1.0 / 6]
CCOS = [-1.0 / 87178291200, 1.0 / 479001600, -1.0 / 3628800, 1.0 / 40320, -1.0 / 720, 1.0 / 24, -0.5]
ROUND = 12582912.0
LN2 = (0.693359375, -2.12194440e-4)
PI3 = (3.140625, 9.67502593994140625e-4, 1.5099579909783764e-7)


def build(nc, a):
    with ExitStack() as ctx:
        cursor = [16512]

        def place(name, shape, dt=F32, offset=None):
            size = (4 * int(np.prod(shape[1:])) + 31) // 32 * 32
            if offset is None:
                offset = cursor[0]
                cursor[0] += size
            return nc.alloc_sbuf_tensor_at(name, shape, dt, offset=(offset + 31) // 32 * 32)

        def region(start, limit):
            start = (start + 31) // 32 * 32

            pos = [start]

            def put(name, shape, dt=F32):
                t = place(name, shape, dt, offset=pos[0])
                pos[0] += (4 * int(np.prod(shape[1:])) + 31) // 32 * 32
                assert pos[0] <= limit, (name, pos[0] - limit)
                return t
            return put

        def sem(name):
            return ctx.enter_context(nc.semaphore(name))

        X = place("X", [P, KT, TW])
        xh_off = cursor[0]
        XH = place("XH", [P, KT, TW], F32R)
        XL = place("XL", [P, KT, TW], F32R)
        x_end = cursor[0]
        WR = place("WR", [P, 2, BLK])
        wh_off = cursor[0]
        WH = place("WH", [P, 2, BLK], F32R)
        WL = place("WL", [P, 2, BLK], F32R)
        hh_off = cursor[0]
        HH = place("HH", [P, 2, TW], F32R)
        HL = place("HL", [P, 2, TW], F32R)
        hh_end = cursor[0]
        rstd_off = cursor[0]
        RSTD = place("RSTD", [P, TW])
        LNV = place("LNV", [P, TW])
        COL = place("COL", [P, NCOL])
        IDENT = place("IDENT", [P, P])
        ONES = place("ONES", [P, P])
        EPSC = place("EPSC", [P, 1])
        RHO8 = place("RHO8", [P, 16])
        SMALL = place("SMALL", [P, 64])
        arena, end = cursor[0], 229344

        put = region(arena, end)
        MR = put("MR", [P, KT, NMEM])
        MH = put("MH", [P, KT, NMEM], F32R)
        ML = put("ML", [P, KT, NMEM], F32R)
        KVS = put("KVS", [P, 2, KT, NMEM])
        WX = place("WX", [P, 2, BLK], offset=arena)
        WHX = put("WHX", [P, 2, BLK], F32R)
        SQT = put("SQT", [P, TW // 2])
        WLX = [put("WLX0", [P, BLK], F32R), place("WLX1", [P, BLK], F32R, offset=rstd_off + 4 * TW)]
        put = region(xh_off, x_end)
        PR, PI = put("PR", [P, 16, 8, 16]), put("PI", [P, 16, 8, 16])
        T1, T2 = put("T1", [P, 16, 8, 16]), put("T2", [P, 16, 8, 16])
        T3 = place("T3", [P, 16, 8, 16], offset=xh_off + 4 * 4 * 16 * P)
        BTP = put("BTP", [P, 2, 16, P])
        KR = put("KR", [P, 512])
        BR, BI = put("BR", [P, 16, 16]), put("BI", [P, 16, 16])
        BBR, BBI = put("BBR", [P, 16, 16]), put("BBI", [P, 16, 16])
        CR, CI = put("CR", [P, 16, 16]), put("CI", [P, 16, 16])
        CRD, NCID = put("CRD", [P, 16, 32]), put("NCID", [P, 16, 32])
        DD = put("DD", [16, 512])
        AR, AI = put("AR", [P, 16, 9]), put("AI", [P, 16, 9])
        AS = put("AS", [P, 24, 16])
        ASI = put("ASI", [P, 16], I32)
        put = region(hh_off, hh_end)
        ERP, EIP = put("ERP", [P, 16, NCK + 1]), put("EIP", [P, 16, NCK + 1])

        put = region(arena, end)
        UJ = put("UJ", [P, 4, CK, CC])
        Q = put("Q", [P, 4, TW])
        KB = put("KB", [P, 1408])
        VB = put("VB", [P, 11, P])
        SMX = put("SMX", [P, 2, 64])
        MASK = put("MASK", [P, 3, 256])
        ROT = put("ROT", [P, P])
        vtt_off = arena + 4 * (4 * CK * CC + 4 * TW + 2 * 1408 + 2 * 64 + 3 * 256 + P)
        VTT = put("VTT", [P, TW])
        KS = place("KS", [P, 512], offset=vtt_off)
        QS = put("QS", [P, 4, P])
        OS = put("OS", [P, 512])
        put = region(hh_off, hh_end)
        COS, SIN = put("COS", [P, TW]), put("SIN", [P, TW])
        QR = put("QR", [P, 2, TW])
        UG = place("UG", [P, 32, CC], offset=arena)
        SB = place("SB", [P, 2, 8, 256], offset=wh_off)
        PT = place("PT", [P, 8, 2, P], offset=rstd_off)
        put = region(xh_off, x_end)
        BT = put("BT", [P, 2, 16, P])
        ER, EI = put("ER", [P, 16, NCK + 1]), put("EI", [P, 16, NCK + 1])
        HR, HI = put("HR", [P, 16, CC + 1]), put("HI", [P, 16, CC + 1])
        TM = put("TM", [P, 32, P])
        CM = [place("CM0", [P, 32, P], offset=xh_off), place("CM1", [P, 32, P], offset=xh_off + 4 * 32 * P)]
        TMR = place("TMR", [P, CK, 512], offset=hh_off)
        put = region(hh_off, hh_end)
        S1, S2 = put("S1", [P, 16, NCK + DEC // CK]), put("S2", [P, 16, NCK + DEC // CK])
        GY = place("GY", [P, 4, TW], offset=hh_off)
        put = region(arena + 4 * 4 * CK * CC, end)
        GH, GL = put("GH", [P, 4, TW], F32R), put("GL", [P, 4, TW], F32R)

        put = region(arena, end)
        SQ = put("SQ", [P, 2, TW])
        XQ = place("XQ", [P, 2, TW], offset=arena)
        XQH, XQL = put("XQH", [P, 2, TW], F32R), put("XQL", [P, 2, TW], F32R)
        KX = put("KX", [P, 2, 2, NMEM])
        KXH, KXL = put("KXH", [P, 2, 2, NMEM], F32R), put("KXL", [P, 2, 2, NMEM], F32R)
        VX = put("VX", [P, 2, 2, 2, P])
        VXH, VXL = put("VXH", [P, 2, 2, 2, P], F32R), put("VXL", [P, 2, 2, 2, P], F32R)
        PX = put("PX", [P, 3, NMEM])
        NX = put("NX", [P, 3, 4])
        put = region(arena + (2 * 4 * TW + 31) // 32 * 32, end)
        G = put("G", [P, 2, TW + 2])
        TAP = put("TAP", [P, 2, TW])
        ACTV, HID = put("ACTV", [P, TW]), put("HID", [P, TW])
        C2, RSTD2 = put("C2", [P, TW]), put("RSTD2", [P, TW])
        STF = put("STF", [P, 4, FT])
        FW = put("FW", [P, 2, 3])

        PS = ctx.enter_context(nc.psum_tensor("PS", [P, 8, 512], F32))

        def pset(s):
            return PS[:, 3 * s:3 * s + 3, 0:CW]

        def col(name, j=0, w=1):
            c = COLS[name][0] + j
            return COL[:, c:c + w]

        def kv_slot(s):
            return (WR[:, s, :], WH[:, s, :], WL[:, s, :]) if s < 2 else (WX[:, s - 2, :], WHX[:, s - 2, :], WLX[s - 2][:])

        def query_tile(t):
            return (DEC, S0, 1) if t == 0 else (P, (t - 1) * P, 0)

        def tiled(x):
            return x.rearrange("p (c w) -> p c w", c=NCH)

        def chunk(x, c):
            return x[:, c * CW:(c + 1) * CW]

        ld = sem("first_loads")
        w_raw = [sem("w_raw_even"), sem("w_raw_odd")]
        kv_raw = [sem(f"kv_raw{x}") for x in range(4)]
        w_hi, w_lo = sem("w_hi"), sem("w_lo")
        tile_done = sem("tile_done")
        kv_copy, kv_out = sem("kv_copy"), [sem(f"kv_out{x}") for x in range(4)]
        mem_hi, mem_lo = sem("mem_hi"), sem("mem_lo")
        par_kr = sem("par_impulse")
        par_ld, par_vec, par_pe, par_dma, par_act = (sem("par_" + x) for x in ("loads", "vec", "pe", "dma", "act"))
        x_ld, ready = sem("x_load"), sem("constants_ready")
        NORMS = ["inp", "x0", "f0", "c1", "x1", "f1", "fin"]
        n_act, n_sum, n_lo, n_tot, n_rs = {}, {}, {}, {}, {}
        for q in NORMS:
            n_act[q] = Steps(sem(f"norm_{q}_act"), [s + str(m) for m in range(KT) for s in ({"inp": ["hi"], "fin": ["sq"]}.get(q, ["sq", "hi"]))])
            n_sum[q] = sem(f"norm_{q}_sum")
            n_lo[q] = sem(f"norm_{q}_lo")
            n_tot[q] = sem(f"norm_{q}_total")
            n_rs[q] = sem(f"norm_{q}_rstd")
        add = {q: sem(f"add_{q}") for q in ADDS}
        names = []
        for x in INP:
            if x == "Rk":
                names += ["sin_k", "cos_k", "rot_k", "rotS_k"]
            elif x[0] == "R":
                names += [s + x[1:] for s in ("sin_", "cos_", "rot_")]
            elif x[0] == "u":
                names += [x, x + "P", x + "S"]
            elif x != "VT":
                names += [x]
        ivec = Steps(sem("inp_vec"), names)
        iact = Steps(sem("inp_act"), ["VTa", "VTb"])
        zeroed, tm_made = sem("mixer_zeroed"), sem("tm_made")
        mix_ld, uj_out, ug_in = sem("mix_loads"), sem("u_to_dram"), sem("u_by_group")
        aq = Steps(sem("scores_staged"), ["QS", "KSa", "KSb"])
        aa_act = Steps(sem("scores_act"), [f"exp{h}" for h in range(8)] + ["esink"])
        aa_vec = Steps(sem("scores_vec"), ["s0", "s1", "s2", "s3", "max", "maxs", "neg", "ds"])
        aa_pe = Steps(sem("scores_pe"), ["S0", "S1", "S2", "S3"])
        ab_act = Steps(sem("values_act"), ["PTa", "PTb", "YB"])
        ab_vec = Steps(sem("values_vec"), ["sum", "rec", "PTc", "PTd", "OSa", "OS"])
        ab_pe = Steps(sem("values_pe"), ["PTa", "PTb", "PTc", "PTd", "PV", "OT"])
        ssm_ld, cm_ld = sem("ssm_loads"), sem("ssm_cm_load")
        ssm_v, ssm_copy = sem("ssm_v"), sem("ssm_v_copied")
        ssm_rot, ssm_scan = sem("ssm_rotation"), sem("ssm_scan")
        ssm_y, ssm_act = sem("ssm_y"), sem("ssm_y_copied")
        y_out, y_in, small_out = sem("y_to_dram"), sem("y_back"), sem("new_state_out")
        four = range(4)
        glu_act = Steps(sem("glu_act"), [f"bh{j}" for j in four] + [s + str(j) for j in four for s in ("gp", "gs", "gh")]
                        + [s + str(j) for j in four for s in ("sig", "hi")])
        glu_vec = Steps(sem("glu_vec"), ["z"] + [f"bl{j}" for j in four] + [f"gl{j}" for j in four]
                        + [s + str(j) for j in four for s in ("mul", "lo")])
        xv, xa, xp, xk, xc, xe, xld, xz = {}, {}, {}, {}, {}, {}, {}, {}
        for l in (0, 1):
            def skew(steps, iterations, at, end):
                names = []
                for k in range(iterations):
                    names += [f"{x}{k - d}" for x, d in steps if 0 <= k - d < 9] + ([at[k]] if k in at else [])
                return names + [end]
            xv[l] = Steps(sem(f"x{l}_vec"), ["ql0", "ql1"] + skew([("mx", 0), ("nm", 0), ("rc", 1), ("pn", 1), ("pl", 3)], 12,
                                                                 {6: "ols", 10: "ola"}, "olb"))
            xa[l] = Steps(sem(f"x{l}_act"), ["kh", "vh", "qh0", "qh1"] + skew([("ex", 0), ("ph", 2)], 11, {5: "ohs", 9: "oha"}, "ohb"))
            xp[l] = Steps(sem(f"x{l}_pe"), skew([("S", 0), ("T", 2)], 11, {4: "Vs", 8: "Va"}, "Vb"))
            xk[l] = Steps(sem(f"x{l}_pool"), ["kl", "vl"])
            xc[l] = sem(f"x{l}_query_chunks")
            xe[l] = Steps(sem(f"x{l}_queries"), [f"e{j}" for j in range(2 * NCH)])
            xld[l], xz[l] = sem(f"x{l}_kv_loads"), sem(f"x{l}_zeroed")
        fv, fa, fz = {}, {}, {}
        for l in (0, 1):
            fv[l] = Steps(sem(f"f{l}_vec"), ["gate0", "w0", "st0", "a0", "b0", "c0", "sm0", "hid0", "gate1", "lo0", "w1", "st1",
                                             "a1", "b1", "c1", "sm1", "hid1", "lo1"])
            fa[l] = Steps(sem(f"f{l}_act"), [s + str(e) for e in (0, 1) for s in ("silu", "na", "nb", "hi")])
            fz[l] = sem(f"f{l}_zeroed")
        cv = Steps(sem("c1_vec"), [s + str(e) for e in (0, 1) for s in ("cc", "zc", "w", "st", "a", "b", "c", "cr", "hid", "lo")])
        ca = Steps(sem("c1_act"), [s + str(e) for e in (0, 1) for s in ("na", "nb", "hi")])
        cz = sem("c1_zeroed")
        st_out = {q: sem(f"{q}_state_out") for q in ("f0", "c1", "f1")}
        outs = sem("outputs")
        fin = sem("fin_y")
        mark = {"H": 26, "S": 30}

        block = ctx.enter_context(nc.Block())

        @block.vector
        def _(dv):
            def chain(s):
                count = [0]

                def do(ins):
                    count[0] += 1
                    ins.then_inc(s, 1)
                    dv.wait_ge(s, count[0])
                    return count[0]
                do.count = count
                return do

            do = chain(ready)
            do(dv.memset(EPSC[:], 1e-6))
            do(dv.memset(ONES[:], 1.0))
            dv.wait_ge(ld, 48)
            dv.wait_ge(mem_hi, 1)
            dv.tensor_tensor(ML[:], MR[:], MH[:].bitcast(F32), ALU.subtract).then_inc(mem_lo, 1)

            do = chain(par_vec)
            R = [AS[:, k, :] for k in range(24)]

            def cmul(out_r, out_i, ar, ai, br, bi, t1, t2, t3, t4):
                do(dv.tensor_tensor(t1, ar, br, ALU.mult))
                do(dv.tensor_tensor(t2, ai, bi, ALU.mult))
                do(dv.tensor_tensor(t3, ar, bi, ALU.mult))
                do(dv.tensor_tensor(t4, ai, br, ALU.mult))
                do(dv.tensor_tensor(out_r, t1, t2, ALU.subtract))
                do(dv.tensor_tensor(out_i, t3, t4, ALU.add))

            def exp(out, x, k, r, p):
                do(dv.tensor_scalar(k, x, 1.4426950408889634, ROUND, ALU.mult, ALU.add))
                do(dv.tensor_scalar(k, k, -ROUND, None, ALU.add))
                do(dv.scalar_tensor_tensor(out=r, in0=k, scalar=-LN2[0], in1=x, op0=ALU.mult, op1=ALU.add))
                do(dv.scalar_tensor_tensor(out=r, in0=k, scalar=-LN2[1], in1=r, op0=ALU.mult, op1=ALU.add))
                do(dv.tensor_scalar(p, r, CEXP[0], None, ALU.mult))
                for c in CEXP[1:]:
                    do(dv.scalar_tensor_tensor(out=p, in0=p, scalar=c, in1=r, op0=ALU.add, op1=ALU.mult))
                do(dv.tensor_scalar(k, k, -126.0, 127.0, ALU.max, ALU.min))
                do(dv.tensor_scalar(ASI[:], k, 127.0, 8388608.0, ALU.add, ALU.mult))
                do(dv.scalar_tensor_tensor(out=out, in0=p, scalar=1.0, in1=ASI[:].bitcast(F32), op0=ALU.add, op1=ALU.mult))

            dt, rho, th, cs, sn, k, r, z, p, sg = R[0:10]
            exp(dt, col("log_dt", 0, 16), k, r, p)
            do(dv.tensor_tensor(z, dt, col("a_re", 0, 16), ALU.mult))
            exp(rho, z, k, r, p)
            do(dv.tensor_tensor(th, dt, col("a_im", 0, 16), ALU.mult))
            do(dv.tensor_scalar(k, th, 0.3183098861837907, ROUND, ALU.mult, ALU.add))
            do(dv.tensor_scalar(k, k, -ROUND, None, ALU.add))
            do(dv.scalar_tensor_tensor(out=r, in0=k, scalar=-PI3[0], in1=th, op0=ALU.mult, op1=ALU.add))
            for c in PI3[1:]:
                do(dv.scalar_tensor_tensor(out=r, in0=k, scalar=-c, in1=r, op0=ALU.mult, op1=ALU.add))
            do(dv.tensor_scalar(sg, k, 0.5, ROUND, ALU.mult, ALU.add))
            do(dv.tensor_scalar(sg, sg, -ROUND, -2.0, ALU.add, ALU.mult))
            do(dv.tensor_tensor(sg, sg, k, ALU.add))
            do(dv.tensor_tensor(sg, sg, sg, ALU.mult))
            do(dv.tensor_scalar(sg, sg, -2.0, 1.0, ALU.mult, ALU.add))
            do(dv.tensor_tensor(z, r, r, ALU.mult))
            do(dv.tensor_scalar(p, z, CSIN[0], None, ALU.mult))
            for c in CSIN[1:]:
                do(dv.scalar_tensor_tensor(out=p, in0=p, scalar=c, in1=z, op0=ALU.add, op1=ALU.mult))
            do(dv.scalar_tensor_tensor(out=p, in0=p, scalar=1.0, in1=r, op0=ALU.add, op1=ALU.mult))
            do(dv.tensor_tensor(sn, p, sg, ALU.mult))
            do(dv.tensor_scalar(p, z, CCOS[0], None, ALU.mult))
            for c in CCOS[1:]:
                do(dv.scalar_tensor_tensor(out=p, in0=p, scalar=c, in1=z, op0=ALU.add, op1=ALU.mult))
            do(dv.scalar_tensor_tensor(out=cs, in0=p, scalar=1.0, in1=sg, op0=ALU.add, op1=ALU.mult))
            do(dv.memset(AR[:, :, 0], 1.0))
            do(dv.memset(AI[:, :, 0], 0.0))
            do(dv.tensor_tensor(AR[:, :, 1], rho, cs, ALU.mult))
            do(dv.tensor_tensor(AI[:, :, 1], rho, sn, ALU.mult))
            tt = [T[:].rearrange("p t i c -> p (t i c)") for T in (T1, T2)]
            tmp = [tt[0][:, 0:1024], tt[0][:, 1024:2048], tt[1][:, 0:1024], tt[1][:, 1024:2048]]

            def temps(w):
                return [x[:, 0:16 * w].rearrange("p (t w) -> p t w", t=16) for x in tmp]
            for w in (1, 2, 4):
                cmul(AR[:, :, w + 1:2 * w + 1], AI[:, :, w + 1:2 * w + 1], AR[:, :, 1:w + 1], AI[:, :, 1:w + 1],
                     AR[:, :, w:w + 1].to_broadcast([P, 16, w]), AI[:, :, w:w + 1].to_broadcast([P, 16, w]), *temps(w))
            do(dv.tensor_tensor(RHO8[:], rho, rho, ALU.mult))
            for _ in range(2):
                do(dv.tensor_tensor(RHO8[:], RHO8[:], RHO8[:], ALU.mult))
            for i in range(3):
                o = (ERP[:, :, 1], EIP[:, :, 1]) if i == 2 else (cs, sn)
                cmul(*o, cs, sn, cs, sn, *R[12:16])
            do(dv.memset(ERP[:, :, 0], 1.0))
            do(dv.memset(EIP[:, :, 0], 0.0))
            w = 1
            while w < NCK:
                cmul(ERP[:, :, w + 1:2 * w + 1], EIP[:, :, w + 1:2 * w + 1], ERP[:, :, 1:w + 1], EIP[:, :, 1:w + 1],
                     ERP[:, :, w:w + 1].to_broadcast([P, 16, w]), EIP[:, :, w:w + 1].to_broadcast([P, 16, w]), *temps(w))
                w *= 2
            lr, li = col("a_re", 0, 16), col("a_im", 0, 16)
            nr, den, d2, fr, fi, q1, q2 = R[10:17]
            ai = AI[:, :, 1]
            do(dv.tensor_scalar(nr, AR[:, :, 1], -1.0, None, ALU.add))
            do(dv.tensor_tensor(den, lr, lr, ALU.mult))
            do(dv.tensor_tensor(d2, li, li, ALU.mult))
            do(dv.tensor_tensor(den, den, d2, ALU.add))
            do(dv.reciprocal(den, den))
            do(dv.tensor_tensor(q1, nr, lr, ALU.mult))
            do(dv.tensor_tensor(q2, ai, li, ALU.mult))
            do(dv.tensor_tensor(fr, q1, q2, ALU.add))
            do(dv.tensor_tensor(fr, fr, den, ALU.mult))
            do(dv.tensor_tensor(q1, ai, lr, ALU.mult))
            do(dv.tensor_tensor(q2, nr, li, ALU.mult))
            do(dv.tensor_tensor(fi, q1, q2, ALU.subtract))
            do(dv.tensor_tensor(fi, fi, den, ALU.mult))
            dv.wait_ge(par_ld, 80)

            def b16(x):
                return x.unsqueeze(2).to_broadcast([P, 16, 16])
            cmul(BBR[:], BBI[:], b16(fr), b16(fi), BR[:], BI[:], *temps(16))
            do(dv.memset(CRD[:], 0.0))
            do(dv.memset(NCID[:], 0.0))
            for q in range(2):
                r, c = slice(64 * q, 64 * q + 64), slice(16 * q, 16 * q + 16)
                do(dv.tensor_copy(CRD[r, :, c], CR[r]))
                do(dv.tensor_scalar(NCID[r, :, c], CI[r], -1.0, None, ALU.mult))

            def pw(x, j):
                return x[:, :, j:j + 8].unsqueeze(3).to_broadcast([P, 16, 8, 16])

            def ch(x):
                return x[:].unsqueeze(2).to_broadcast([P, 16, 8, 16])
            do(dv.tensor_tensor(PR[:], pw(AR, 0), ch(BBR), ALU.mult))
            do(dv.tensor_tensor(T1[:], pw(AI, 0), ch(BBI), ALU.mult))
            do(dv.tensor_tensor(PR[:], PR[:], T1[:], ALU.subtract))
            do(dv.tensor_tensor(PI[:], pw(AR, 0), ch(BBI), ALU.mult))
            do(dv.tensor_tensor(T1[:], pw(AI, 0), ch(BBR), ALU.mult))
            mark["P"] = do(dv.tensor_tensor(PI[:], PI[:], T1[:], ALU.add))
            do(dv.tensor_tensor(T1[:], pw(AR, 1), ch(CR), ALU.mult))
            do(dv.tensor_tensor(T3[:], pw(AI, 1), ch(CI), ALU.mult))
            do(dv.tensor_tensor(T1[:], T1[:], T3[:], ALU.subtract))
            do(dv.tensor_tensor(T2[:], pw(AI, 1), ch(CR), ALU.mult))
            do(dv.tensor_tensor(T3[:], pw(AR, 1), ch(CI), ALU.mult))
            do(dv.tensor_tensor(T2[:], T2[:], T3[:], ALU.add))
            mark["C"] = do(dv.tensor_scalar(T2[:], T2[:], -1.0, None, ALU.mult))
            dv.wait_ge(par_kr, 1)
            do(dv.tensor_copy(KR[:], PS[:, 1, :]))
            mark["K"] = do(dv.tensor_tensor(KR[0:16, :], KR[0:16, :], DD[:], ALU.add))

            do = chain(n_sum["inp"])
            dv.wait_ge(x_ld, 16 * KT)
            for m in range(KT):
                for h in (slice(0, TW // 2), slice(TW // 2, TW)):
                    do(dv.tensor_tensor(SQT[:] if m else RSTD[:, h], X[:, m, h], X[:, m, h], ALU.mult))
                    if m:
                        do(dv.tensor_tensor(RSTD[:, h], RSTD[:, h], SQT[:], ALU.add))
            mark["inp"] = do.count[0]

            def norm_lo(q, m):
                dv.wait_ge(*n_act[q].at(f"hi{m}"))
                dv.scalar_tensor_tensor(out=XL[:, m, :], in0=X[:, m, :], scalar=col(GAIN[q], m), in1=XH[:, m, :].bitcast(F32),
                                        op0=ALU.mult, op1=ALU.subtract).then_inc(n_lo[q], 1)

            def last_adds(ph, first_tile, nxt):
                for m in range(KT + 1):
                    if m < KT:
                        dv.wait_ge(tile_done, first_tile + m)
                        dv.wait_ge(add[ph], ADDS[ph] - 2 * KT + m + 1)
                        dv.tensor_tensor(tiled(X[:, m, :]), tiled(X[:, m, :]), pset(m % 2), ALU.add).then_inc(add[ph], 1)
                    if m >= 1 and nxt != "fin":
                        norm_lo(nxt, m - 1)

            dv.wait_ge(par_dma, 16 * 26)
            zero = chain(zeroed)
            for m in range(KT):
                norm_lo("inp", m)
            dv.wait_ge(kv_copy, 32)
            dv.wait_ge(tile_done, N0["inp"])
            for s in kv_out:
                dv.wait_ge(s, 16)
            zero(dv.memset(UJ[:, :, :, NCK:NCK + 1], 0.0))
            zero(dv.memset(KB[:, 0:P], 0.0))
            zero(dv.memset(KB[:, 1312:1408], 0.0))
            zero(dv.memset(VB[:, 0, :], 0.0))
            mark["Z"] = zero(dv.memset(VB[:, 10, :], 0.0))
            for j, x in enumerate(INP):
                ps = pset(j % 2)
                if x != "VT":
                    dv.wait_ge(tile_done, T0["inp"] + j + 1)
                if j == 0:
                    dv.wait_ge(n_rs["inp"], 6)
                    dv.wait_ge(mix_ld, 96)
                if x in ("k", "q0", "q1", "q2", "q3"):
                    if x == "q1":
                        dv.wait_ge(*ivec.at("rotS_k"))
                    if x in ("q2", "q3"):
                        dv.wait_ge(*ivec.at({"q2": "rot_q0", "q3": "rot_q1"}[x]))
                    dv.tensor_tensor(tiled(QR[:, QSLOT[x], :]), ps, tiled(RSTD[:]), ALU.mult).then_inc(ivec.sem, 1)
                elif x == "v":
                    dv.tensor_tensor(tiled(VTT[:]), ps, tiled(RSTD[:]), ALU.mult).then_inc(ivec.sem, 1)
                elif x[0] == "u":
                    t = int(x[1])
                    if t == 1:
                        dv.wait_ge(small_out, 64)
                        dv.wait_ge(tile_done, T0["inp"] + INP.index("VT") + 1)
                        mark["KS"] = zero(dv.memset(KS[:], 0.0))
                    dv.wait_ge(*(ivec.at("rotS_k") if t == 0 else ivec.at(f"u{t - 1}S")))
                    dv.tensor_tensor(tiled(LNV[:]), ps, tiled(RSTD[:]), ALU.mult).then_inc(ivec.sem, 1)
                    dv.wait_ge(*ivec.at(x))
                    dv.tensor_copy(UJ[:, t, :, 0:NCK], LNV[:, 0:SEQ].rearrange("p (c j) -> p j c", j=CK)).then_inc(ivec.sem, 1)
                    dv.tensor_copy(UJ[:, t, :, NCK + 1:CC], LNV[:, S0:TW].rearrange("p (c j) -> p j c", j=CK)).then_inc(ivec.sem, 1)
                elif x[0] == "R":
                    y = x[1:]
                    dst = LNV[:] if y == "k" else Q[:, int(y[1]), :]
                    qr = QR[:, QSLOT[y], :]
                    dv.tensor_tensor(tiled(dst), ps, tiled(SIN[:]), ALU.mult).then_inc(ivec.sem, 1)
                    dv.wait_ge(*ivec.at(y))
                    dv.tensor_tensor(qr, qr, COS[:], ALU.mult).then_inc(ivec.sem, 1)
                    dv.wait_ge(*ivec.at("cos_" + y))
                    if y == "k":
                        dv.tensor_tensor(KB[:, P:P + SEQ], LNV[:, 0:SEQ], qr[:, 0:SEQ], ALU.add).then_inc(ivec.sem, 1)
                        dv.tensor_tensor(KB[:, 1280:1312], LNV[:, S0:TW], qr[:, S0:TW], ALU.add).then_inc(ivec.sem, 1)
                    else:
                        dv.tensor_tensor(dst, dst, qr, ALU.add).then_inc(ivec.sem, 1)

            def att(k, s, nq=P, kind=1, values=True, scores=True):
                j, z, nj = k - 1, 1 - s, P
                if scores:
                    if not (isinstance(k, int) and k < 2):
                        dv.wait_ge(*ab_pe.at("PTd", k - 2))
                    for b in range(4):
                        dv.wait_ge(*aa_pe.at(f"S{b}", k))
                        dv.scalar_tensor_tensor(out=SB[0:nq, s, 2 * b:2 * b + 2, :], in0=PS[0:nq, b, :].rearrange("p (h k) -> p h k", h=2),
                                                scalar=0.125, in1=MASK[0:nq, kind, :].unsqueeze(1).to_broadcast([nq, 2, 256]),
                                                op0=ALU.mult, op1=ALU.add).then_inc(aa_vec.sem, 1)
                if values:
                    nj = P if scores else DEC
                    dv.wait_ge(*aa_act.at("esink", j))
                    dv.tensor_tensor(SMX[0:nj, z, 32:40], SMX[0:nj, z, 16:24], SMX[0:nj, z, 24:32], ALU.add).then_inc(ab_vec.sem, 1)
                    dv.wait_ge(*ab_vec.at("sum", j))
                    dv.reciprocal(SMX[0:nj, z, 48:56], SMX[0:nj, z, 32:40]).then_inc(ab_vec.sem, 1)
                    for b, nm in ((2, "PTc"), (3, "PTd")):
                        dv.wait_ge(*ab_pe.at(nm, j))
                        dv.tensor_copy(PT[:, 2 * b:2 * b + 2, :, 0:nj],
                                       PS[:, 2 + b, :].rearrange("p (h k q) -> p h k q", h=2, k=2)[:, :, :, 0:nj]).then_inc(ab_vec.sem, 1)
                if scores:
                    dv.wait_ge(*aa_vec.at("s3", k))
                    dv.tensor_reduce(SMX[0:nq, s, 0:8], SB[0:nq, s], AX.X, ALU.max).then_inc(aa_vec.sem, 1)
                    dv.wait_ge(*aa_vec.at("max", k))
                    dv.tensor_tensor(SMX[0:nq, s, 0:8], SMX[0:nq, s, 0:8], col("sink", 0, 8)[0:nq], ALU.max).then_inc(aa_vec.sem, 1)
                    dv.wait_ge(*aa_vec.at("maxs", k))
                    dv.tensor_scalar(SMX[0:nq, s, 8:16], SMX[0:nq, s, 0:8], -1.0, None, ALU.mult).then_inc(aa_vec.sem, 1)
                    dv.tensor_tensor(SMX[0:nq, s, 40:48], col("sink", 0, 8)[0:nq], SMX[0:nq, s, 0:8], ALU.subtract).then_inc(aa_vec.sem, 1)
                if values:
                    dv.wait_ge(*ab_pe.at("PV", j))
                    dv.wait_ge(*ab_vec.at("rec", j))
                    for g in range(2):
                        dv.tensor_tensor(OS[0:nj, :].rearrange("p (j g d) -> p j g d", j=4, g=2)[:, :, g, :],
                                         PS[0:nj, 6:8, :].rearrange("p b (j g d) -> p (b j) g d", j=2, g=2)[:, :, g, 64 * g:64 * g + 64],
                                         SMX[0:nj, z, 48:56].rearrange("p (j g) -> p j g", g=2)[:, :, g].unsqueeze(2).to_broadcast([nj, 4, 64]),
                                         ALU.mult).then_inc(ab_vec.sem, 1)

            att(0, 0, kind=0, values=False)
            att(1, 1)
            att(2, 0)
            dv.memset(HR[:, :, 0], 0.0).then_inc(ssm_scan, 1)
            dv.memset(HI[:, :, 0], 0.0).then_inc(ssm_scan, 1)
            for k in range(32):
                dv.wait_ge(ssm_v, k + 1)
                dv.tensor_copy((HR, HI)[k % 2][:, k // 2, 1:CC + 1], PS[:, 4 + k % 4, 0:CC]).then_inc(ssm_copy, 1)
            for k in (3, 4, 5):
                att(k, k % 2)
            dv.wait_ge(ssm_rot, 12)
            for half in range(2):
                for lo, w, init in ((1, NCK, None), (NCK + 2, DEC // CK, ("h0_re", "h0_im"))):
                    for t in range(8 * half, 8 * half + 8):
                        for s, h, nm in ((S1, HR, 0), (S2, HI, 1)):
                            dv.tensor_tensor_scan(h[:, t, lo:lo + w], RHO8[:, t:t + 1].to_broadcast([P, w]), s[:, t, 0 if init is None else NCK:][:, 0:w],
                                                  col(init[nm], t) if init else 0.0, ALU.mult, ALU.add).then_inc(ssm_scan, 1)
                att(6 + half, half)
            att(8, 0, nq=DEC, kind=2)
            att(9, 1, scores=False)

            dv.wait_ge(*ab_act.at("YB", 8))
            dv.wait_ge(ssm_rot, mark["S"])
            dv.memset(GY[:, :, SEQ:S0], 0.0).then_inc(glu_vec.sem, 1)
            for j in range(4):
                dv.wait_ge(*glu_act.at(f"bh{j}"))
                dv.tensor_tensor(XL[:, j, :], Q[:, j, :], XH[:, j, :].bitcast(F32), ALU.subtract).then_inc(glu_vec.sem, 1)

            def out_add(c, tile):
                m = c % KT
                dv.wait_ge(tile_done, tile)
                if c >= KT:
                    dv.wait_ge(add["out"], c - KT + 1)
                dv.tensor_tensor(tiled(X[:, m, :]), tiled(X[:, m, :]), pset(m % 2), ALU.add).then_inc(add["out"], 1)

            for c in range(16):
                out_add(c, T0["outb"] + c + 1)
                if c in (8, 10, 12, 14):
                    j = (c - 8) // 2
                    dv.wait_ge(*glu_act.at(f"gh{j}"))
                    dv.tensor_tensor(GL[:, j, :], GY[:, j, :], GH[:, j, :].bitcast(F32), ALU.subtract).then_inc(glu_vec.sem, 1)
            for j in range(4):
                dv.wait_ge(*glu_act.at(f"sig{j}"))
                dv.wait_ge(*glu_vec.at(f"gl{j}"))
                dv.tensor_tensor(GY[:, j, :], GY[:, j, :], LNV[:], ALU.mult).then_inc(glu_vec.sem, 1)
                dv.wait_ge(*glu_act.at(f"hi{j}"))
                dv.tensor_tensor(XL[:, 4 + j, :], GY[:, j, :], XH[:, 4 + j, :].bitcast(F32), ALU.subtract).then_inc(glu_vec.sem, 1)
            for c in range(16, 24):
                out_add(c, T0["outa"] + c - 15)
            last_adds("out", T0["outa"] + 9, "x0")

            def cross(l, prev, nxt):
                q, v, ac, te = f"x{l}", xv[l], xa[l], xp[l]
                t0 = T0[q]
                dv.memset(HH[:, :, SEQ:S0].bitcast(F32), 0.0).then_inc(xz[l], 1)
                dv.memset(HL[:, :, SEQ:S0].bitcast(F32), 0.0).then_inc(xz[l], 1)
                dv.wait_ge(xz[l], 2)

                def take(i, j, bank, tile):
                    if j % NCH == 2:
                        dv.wait_ge(tile_done, tile)
                    elif not (isinstance(i, int) and i == 0):
                        dv.wait_ge(xc[l], i * 4 + ((0, 1, 0, 2, 3)[j] - 3))
                    dv.tensor_tensor(chunk(XQ[:, j // NCH, :], j % NCH), PS[:, bank, 0:CW], chunk(RSTD, j % NCH), ALU.mult).then_inc(xe[l].sem, 1)

                def split(i):
                    for s in (0, 1):
                        dv.wait_ge(*ac.at(f"qh{s}", i))
                        dv.tensor_tensor(XQL[:, s, :], XQ[:, s, :], XQH[:, s, :].bitcast(F32), ALU.subtract).then_inc(v.sem, 1)

                def out_low(cols, bank, high):
                    dv.wait_ge(*high)
                    w = cols.stop - cols.start
                    dv.tensor_tensor(HL[:, :, cols], PS[:, bank:bank + 2, 0:w], HH[:, :, cols].bitcast(F32), ALU.subtract).then_inc(v.sem, 1)

                def attend(i, more=True):
                    tile = i * 10 + (t0 + 3)
                    for k in range(12):
                        t = k
                        if t < 9:
                            nq = query_tile(t)[0]
                            dv.wait_ge(*te.at(f"S{t}", i))
                            if t >= 3:
                                dv.wait_ge(*ac.at(f"ex{t - 3}", i))
                            dv.tensor_reduce(NX[0:nq, t % 3, 0:1], PS[0:nq, t % 2, 0:NMEM], AX.X, ALU.max).then_inc(v.sem, 1)
                            dv.wait_ge(*v.at(f"mx{t}", i))
                            dv.tensor_scalar(NX[0:nq, t % 3, 1:2], NX[0:nq, t % 3, 0:1], -1.0 / 16, None, ALU.mult).then_inc(v.sem, 1)
                        t = k - 1
                        if 0 <= t < 9:
                            nq = query_tile(t)[0]
                            dv.wait_ge(*ac.at(f"ex{t}", i))
                            dv.reciprocal(NX[0:nq, t % 3, 3:4], NX[0:nq, t % 3, 2:3]).then_inc(v.sem, 1)
                            dv.wait_ge(*v.at(f"rc{t}", i))
                            dv.tensor_scalar(PX[0:nq, t % 3, :], PX[0:nq, t % 3, :], NX[0:nq, t % 3, 3:4], None, ALU.mult).then_inc(v.sem, 1)
                        t = k - 3
                        if 0 <= t < 9:
                            nq, c0, _ = query_tile(t)
                            dv.wait_ge(*ac.at(f"ph{t}", i))
                            dv.tensor_tensor(HL[:, :, c0:c0 + nq], PS[:, 2 + t % 2, 0:NMEM].rearrange("p (d q) -> p d q", d=2)[:, :, 0:nq],
                                             HH[:, :, c0:c0 + nq].bitcast(F32), ALU.subtract).then_inc(v.sem, 1)
                        if more and k % 2 == 0 and k:
                            j = k // 2 - 1
                            take(i + 1, j, 6 + j % 2, tile)
                        if k == 6:
                            out_low(slice(S0, TW), 4, ac.at("ohs", i))
                        if k == 10:
                            out_low(slice(0, 512), 4, ac.at("oha", i))
                    out_low(slice(512, SEQ), 4, ac.at("ohb", i))
                    if more:
                        take(i + 1, 5, 7, tile + 1)

                def round_(i):
                    attend(i)
                    for m in range(KT):
                        if m == 2:
                            split(i + 1)
                        dv.wait_ge(tile_done, i * 10 + (t0 + 5 + m))
                        if not (isinstance(i, int) and i == 0):
                            dv.wait_ge(add[q], i * 8 + (m - 7))
                        dv.tensor_tensor(tiled(X[:, m, :]), tiled(X[:, m, :]), pset(m % 2), ALU.add).then_inc(add[q], 1)

                for j in range(2 * NCH):
                    if j % NCH == 0:
                        dv.wait_ge(tile_done, t0 + j // NCH + 1)
                        dv.wait_ge(n_rs[q], 6)
                    take(0, j, j, t0 + j // NCH + 1)
                split(0)
                round_(0)
                with dv.Fori(1, HEADS - 1) as i:
                    round_(i)
                attend(HEADS - 1, more=False)
                last_adds(q, t0 + 33, nxt)

            def conv_taps(s, e, wname, width, sname, i, filled, between=None):
                w0, s0 = COLS[wname][0], COLS[sname][0]
                wc = COL[:, w0:w0 + 3 * width].rearrange("p (k f) -> p f k", k=3)
                sc = COL[:, s0:s0 + 2 * width].rearrange("p (k f) -> p f k", k=2)
                f = i * 2 + e
                dv.tensor_copy(FW[:, e, :], wc[:, bass.ds(f, 1), :].rearrange("p o k -> p (o k)")).then_inc(s.sem, 1)
                dv.wait_ge(*s.at(filled, i))
                dv.tensor_copy(G[:, e, S0:S0 + 2], sc[:, bass.ds(f, 1), :].rearrange("p o k -> p (o k)")).then_inc(s.sem, 1)
                dv.wait_ge(*s.at(f"st{e}", i))
                dv.tensor_scalar(TAP[:, e, :], G[:, e, 2:TW + 2], FW[:, e, 2:3], None, ALU.mult).then_inc(s.sem, 1)
                if between:
                    between(0)
                dv.wait_ge(*s.at(f"a{e}", i))
                dv.scalar_tensor_tensor(out=TAP[:, e, :], in0=G[:, e, 1:TW + 1], scalar=FW[:, e, 1:2], in1=TAP[:, e, :],
                                        op0=ALU.mult, op1=ALU.add).then_inc(s.sem, 1)
                if between:
                    between(1)
                dv.wait_ge(*s.at(f"b{e}", i))
                dv.scalar_tensor_tensor(out=TAP[:, e, :], in0=G[:, e, 0:TW], scalar=FW[:, e, 0:1], in1=TAP[:, e, :],
                                        op0=ALU.mult, op1=ALU.add).then_inc(s.sem, 1)

            def ffn(l, nxt):
                q, v, ac = f"f{l}", fv[l], fa[l]
                t0 = T0[q]
                dv.memset(G[:, :, 0:2], 0.0).then_inc(fz[l], 1)

                def gate(g, e, tile, first):
                    dv.wait_ge(tile_done, tile)
                    if first:
                        dv.wait_ge(n_rs[q], 6)
                    else:
                        dv.wait_ge(*ac.at(f"nb{e}", g - 1))
                    dv.tensor_tensor(tiled(G[:, e, 2:TW + 2]), pset(0), tiled(RSTD[:]), ALU.mult).then_inc(v.sem, 1)

                def taps(g, e, between=None):
                    conv_taps(v, e, f"cf_w{l}", FT, f"cf_s{l}", g, f"gate{e}", between)

                def scale(g, e):
                    dv.wait_ge(*ac.at(f"silu{e}", g))
                    dv.tensor_tensor(TAP[:, e, :], ACTV[:], RSTD[:], ALU.mult).then_inc(v.sem, 1)

                def hid(g, e, tile):
                    dv.wait_ge(tile_done, tile)
                    dv.wait_ge(*v.at(f"sm{e}", g))
                    dv.tensor_tensor(tiled(HID[:]), pset(1), tiled(TAP[:, e, :]), ALU.mult).then_inc(v.sem, 1)

                def low(g, e):
                    dv.wait_ge(*ac.at(f"hi{e}", g))
                    dv.tensor_tensor(HL[:, e, :], HID[:], HH[:, e, :].bitcast(F32), ALU.subtract).then_inc(v.sem, 1)

                def group(g, t, first):
                    gate(g, 0, t + 1, first)

                    def down_add(m):
                        dv.wait_ge(tile_done, t + (2 + m))
                        if not isinstance(g, int):
                            dv.wait_ge(add[q], g * 8 + (m - 15))
                        dv.tensor_tensor(tiled(X[:, m, :]), tiled(X[:, m, :]), pset((1 + m) % 2), ALU.add).then_inc(add[q], 1)

                    taps(g, 0, None if first else down_add)
                    if not first:
                        for m in range(2, KT):
                            down_add(m)
                    o = 1 if first else 9
                    scale(g, 0)
                    hid(g, 0, t + (o + 1))
                    gate(g, 1, t + (o + 2), first)
                    low(g, 0)
                    taps(g, 1)
                    scale(g, 1)
                    hid(g, 1, t + (o + 3))
                    low(g, 1)

                dv.wait_ge(fz[l], 1)
                group(0, t0, True)
                group(1, t0 + 4, False)
                with dv.Fori(2, 11) as g:
                    group(g, g * 12 + (t0 - 8), False)
                last_adds(q, t0 + 125, nxt)

            def conv(nxt):
                q = "c1"
                t0 = T0[q]
                dv.memset(G[:, :, 0:2], 0.0).then_inc(cz, 1)
                dv.wait_ge(n_rs[q], 6)
                dv.tensor_tensor(RSTD2[:], RSTD[:], RSTD[:], ALU.mult).then_inc(cz, 1)
                dv.wait_ge(cz, 2)

                def tile(g, e, tc, tz, tb, pc, first, between=None):
                    dv.wait_ge(tile_done, tc)
                    if e == 1:
                        dv.wait_ge(*cv.at("zc0", g))
                    elif not first:
                        dv.wait_ge(*cv.at("zc1", g - 1))
                    dv.tensor_tensor(tiled(C2[:]), pset(pc[0]), tiled(RSTD2[:]), ALU.mult).then_inc(cv.sem, 1)
                    if between:
                        between()
                    dv.wait_ge(tile_done, tz)
                    dv.wait_ge(*cv.at(f"cc{e}", g))
                    if not first:
                        dv.wait_ge(*ca.at(f"nb{e}", g - 1))
                    dv.tensor_tensor(tiled(G[:, e, 2:TW + 2]), pset(pc[1]), tiled(C2[:]), ALU.mult).then_inc(cv.sem, 1)
                    conv_taps(cv, e, "cm_w", KT, "cm_s", g, f"zc{e}")
                    dv.wait_ge(*cv.at(f"c{e}", g))
                    dv.tensor_tensor(TAP[:, e, :], TAP[:, e, :], RSTD[:], ALU.mult).then_inc(cv.sem, 1)
                    dv.wait_ge(tile_done, tb)
                    dv.wait_ge(*cv.at(f"cr{e}", g))
                    dv.tensor_tensor(tiled(HID[:]), pset(pc[2]), tiled(TAP[:, e, :]), ALU.mult).then_inc(cv.sem, 1)
                    dv.wait_ge(*ca.at(f"hi{e}", g))
                    dv.tensor_tensor(HL[:, e, :], HID[:], HH[:, e, :].bitcast(F32), ALU.subtract).then_inc(cv.sem, 1)

                tile(0, 0, t0 + 1, t0 + 2, t0 + 3, (0, 1, 0), True)
                tile(0, 1, t0 + 4, t0 + 5, t0 + 6, (1, 0, 1), True)

                def group(g, t):
                    def between():
                        for m in range(KT):
                            dv.wait_ge(tile_done, t + (2 + m))
                            if not isinstance(g, int):
                                dv.wait_ge(add[q], g * 8 + (m - 15))
                            dv.tensor_tensor(tiled(X[:, m, :]), tiled(X[:, m, :]), pset((1 + m) % 2), ALU.add).then_inc(add[q], 1)
                    tile(g, 0, t + 1, t + 10, t + 11, (0, 1, 0), False, between)
                    tile(g, 1, t + 12, t + 13, t + 14, (1, 0, 1), False)

                group(1, t0 + 6)
                with dv.Fori(2, 4) as g:
                    group(g, g * 14 + (t0 - 8))
                last_adds(q, t0 + 49, nxt)

            cross(0, "out", "f0")
            ffn(0, "c1")
            conv("x1")
            cross(1, "c1", "f1")
            ffn(1, "fin")
            dv.wait_ge(n_rs["fin"], 6)
            dv.wait_ge(add["f1"], 88)
            for m in range(KT):
                dv.scalar_tensor_tensor(out=X[:, m, :], in0=X[:, m, :], scalar=col("g_fin", m), in1=RSTD[:],
                                        op0=ALU.mult, op1=ALU.mult).then_inc(fin, 1)

        @block.tensor
        def _(pe):
            def mms(out, h, l, rh, rl, start, stop):
                pe.matmul(out, h, rh, start=start, stop=False)
                pe.matmul(out, h, rl, start=False, stop=False)
                return pe.matmul(out, l, rh, start=False, stop=stop)

            def tile_a(n, s, pset_i, kt=KT, lhs=None, H=XH, L=XL, wait_lo=True, split=None):
                if wait_lo:
                    pe.wait_ge(w_lo, n + 1)
                for k in range(kt):
                    if split:
                        pe.wait_ge(n_lo[split], k + 1)
                    wh, wl = lhs(k) if lhs else (WH[:, s, k * P:(k + 1) * P], WL[:, s, k * P:(k + 1) * P])
                    for c in range(NCH):
                        mm = mms(PS[:, 3 * pset_i + c, 0:CW], wh, wl, chunk(H[:, k, :], c), chunk(L[:, k, :], c),
                                 k == 0, k == kt - 1)
                mm.then_inc(tile_done, 1)

            def block_b(n, s, marks, H=HH, L=HL, k0=0):
                pe.wait_ge(w_lo, n + 1)
                for o in range(4):
                    pe.wait_ge(*marks[o])
                    def lhs(k):
                        return (WH[:, s, k * 512 + o * P:k * 512 + (o + 1) * P], WL[:, s, k * 512 + o * P:k * 512 + (o + 1) * P])
                    for k in range(2):
                        wh, wl = lhs(k)
                        for c in range(NCH):
                            mm = mms(PS[:, 3 * (o % 2) + c, 0:CW], wh, wl, chunk(H[:, k0 + k, :], c), chunk(L[:, k0 + k, :], c),
                                     k == 0, k == 1)
                    mm.then_inc(tile_done, 1)

            def norm_total(q):
                pe.wait_ge(n_sum[q], mark.get(q, KT))
                for c in range(NCH):
                    if c == 2:
                        pe.wait_ge(n_rs[q], 1)
                    pe.matmul(PS[:, 6 + c % 2, 0:CW], ONES[:], chunk(RSTD[:], c), start=True, stop=True).then_inc(n_tot[q], 1)

            pe.wait_ge(mem_lo, 1)
            pe.wait_ge(mem_hi, 1)
            def impulses():
                pe.wait_ge(par_vec, mark["P"])
                for t in range(16):
                    o = PS[:, 1, 32 * t:32 * t + 32]
                    pe.matmul(o, PR[:, t].rearrange("p i c -> p (i c)"), CRD[:, t, :], start=True, stop=False, skip_group_check=True)
                    mm = pe.matmul(o, PI[:, t].rearrange("p i c -> p (i c)"), NCID[:, t, :], start=False, stop=True, skip_group_check=True)
                mm.then_inc(par_kr, 1)

            def transposes():
                pe.wait_ge(par_vec, mark["C"])
                for ri in range(2):
                    for tq in range(4):
                        b = 6 + (4 * ri + tq) % 2
                        if 4 * ri + tq >= 2:
                            pe.wait_ge(par_act, 4 * ri + tq - 1)
                        for t in range(4):
                            mm = pe.transpose(PS[:, b, t * P:(t + 1) * P], (PR, PI)[ri][:, 4 * tq + t].rearrange("p i c -> p (i c)"), IDENT[:])
                        mm.then_inc(par_pe, 1)

            def quad(part, q, first=False):
                for s in range(4):
                    pe.wait_ge(w_lo, q * 4 + (s + 1))
                    _, h, l = kv_slot(s)
                    if part % 2 == 0:
                        if not (first and s < 2):
                            pe.wait_ge(kv_copy, q * 4 + (s - 1))
                        for k in range(KT):
                            w = slice(k * P, (k + 1) * P)
                            mm = mms(PS[:, 3 * (s % 2), 0:NMEM], h[:, w], l[:, w], MH[:, k, :], ML[:, k, :], k == 0, k == KT - 1)
                    else:
                        if s % 2 == 0:
                            pe.wait_ge(kv_copy, q * 4 + (s - 2))
                        for mt in range(2):
                            o = slice(mt * P, (mt + 1) * P)
                            for j in range(4):
                                k, w = 4 * (s % 2) + j, slice(j * 256, (j + 1) * 256)
                                mm = mms(PS[:, VALUE_BANKS[s // 2][mt], 0:256], MH[:, k, o], ML[:, k, o], h[:, w], l[:, w],
                                         k == 0, k == KT - 1)
                    mm.then_inc(tile_done, 1)

            quad(0, 0, True)
            quad(0, 1)
            for part in (1, 2):
                with pe.Fori(2 * part, 2 * part + 2) as q:
                    quad(part, q)
            impulses()
            quad(3, 6)
            transposes()
            quad(3, 7)
            pe.wait_ge(par_vec, mark["K"])
            pe.wait_ge(kv_copy, 32)
            evac = {x: iact.at("VTb") if x == "VT" else ivec.at("sin_" + x[1:] if x[0] == "R" else x) for x in INP}
            n = N0["inp"]
            for j, x in enumerate(INP):
                s = j % 2
                if j >= 2:
                    pe.wait_ge(*evac[INP[j - 2]])
                if x == "VT":
                    pe.wait_ge(*ivec.at("v"))
                    for t in range(9):
                        w = P if t < 8 else DEC
                        c0 = t * P if t < 8 else S0
                        mm = pe.transpose(PS[0:w, 3 * s + t // 4, (t % 4) * P:(t % 4 + 1) * P], VTT[:, c0:c0 + w], IDENT[:])
                    mm.then_inc(tile_done, 1)
                elif x[0] == "R":
                    pe.wait_ge(*ivec.at(x[1:]))
                    if x == "Rk":
                        pe.wait_ge(mix_ld, 96)
                    for c in range(NCH):
                        mm = pe.matmul(PS[:, 3 * s + c, 0:CW], ROT[:], chunk(QR[:, QSLOT[x[1:]], :], c), start=True, stop=True)
                    mm.then_inc(tile_done, 1)
                else:
                    tile_a(n, n % 2, s, split="inp" if j == 0 else None)
                    n += 1
                    if j == 0:
                        norm_total("inp")

            pe.wait_ge(*ivec.at("u3"))

            def att(k, s, nq=P, values=True, scores=True, vb=None):
                j, z, nj = k - 1, 1 - s, P if scores else DEC
                if scores:
                    pe.wait_ge(*aq.at("KSb", k))
                    if not (isinstance(k, int) and k == 0):
                        pe.wait_ge(*aa_vec.at("s3", j))
                    for h in range(4):
                        mm = pe.matmul(PS[0:nq, h, :], QS[:, h, 0:nq], KS[:], start=True, stop=True)
                        mm.then_inc(aa_pe.sem, 1)
                if not values:
                    return
                pe.wait_ge(*aa_act.at("exp7", j))
                if not (isinstance(k, int) and k == 1):
                    pe.wait_ge(*ab_act.at("YB", k - 2))
                    pe.nop(nofuse=True)
                for b in range(4):
                    if b >= 2:
                        pe.wait_ge(*ab_act.at(("PTa", "PTb")[b - 2], j))
                        pe.nop(nofuse=True)
                    for h in (2 * b, 2 * b + 1):
                        for kt in range(2):
                            mm = pe.transpose(PS[:, 4 + b % 2, ((h % 2) * 2 + kt) * P:((h % 2) * 2 + kt) * P + nj],
                                              SB[0:nj, z, h, kt * P:(kt + 1) * P], IDENT[0:nj, 0:nj])
                    mm.then_inc(ab_pe.sem, 1)
                pe.wait_ge(*ab_vec.at("PTd", j))
                for h in range(8):
                    for kt in range(2):
                        mm = pe.matmul(PS[0:nj, 6 + h // 4, h % 4 * P:h % 4 * P + P], PT[:, h, kt, 0:nj], vb(kt),
                                       start=(kt == 0), stop=(kt == 1), skip_group_check=True)
                mm.then_inc(ab_pe.sem, 1)
                pe.wait_ge(*ab_vec.at("OS", j))
                for c in range(4):
                    mm = pe.transpose(PS[:, 4, c * P:c * P + nj], OS[0:nj, c * P:(c + 1) * P], IDENT[0:nj, 0:nj])
                mm.then_inc(ab_pe.sem, 1)

            def values(k):
                if isinstance(k, int):
                    return lambda kt: VB[:, k + kt, :]
                return lambda kt: VB[:, bass.ds(k + kt, 1), :].rearrange("p o d -> p (o d)")

            att(0, 0, values=False)
            att(1, 1, vb=values(0))
            att(2, 0, vb=values(1))
            pe.wait_ge(ssm_ld, 64)
            pe.wait_ge(ug_in, 128)
            pe.wait_ge(*ab_act.at("YB", 1))
            for t in range(16):
                for ri in range(2):
                    k = 2 * t + ri
                    if k >= 4:
                        pe.wait_ge(ssm_copy, k - 3)
                    for q in range(2):
                        mm = pe.matmul(PS[64 * q:64 * q + 64, 4 + k % 4, 0:CC], BT[:, ri, t, 64 * q:64 * q + 64], UG[:, 2 * t + q, :],
                                       start=True, stop=True)
                    mm.then_inc(ssm_v, 1)
            pe.wait_ge(ssm_copy, 32)
            for k in range(3, 8):
                att(k, k % 2, vb=values(k - 1))
            att(8, 0, nq=DEC, vb=values(7))
            att(9, 1, scores=False, vb=values(9))
            pe.wait_ge(ssm_rot, mark["H"])
            pe.wait_ge(cm_ld, 32)
            pe.wait_ge(tm_made, 1)
            pe.wait_ge(*ab_act.at("YB", 8))
            for g in range(32):
                t, b = g // 2, g % 8
                if g >= 8:
                    pe.wait_ge(ssm_act, g - 7)
                o = PS[:, b, 0:CC]
                pe.matmul(o, TM[:, g, :], UG[:, g, :], start=True, stop=False)
                pe.matmul(o, CM[0][:, g, :], HR[:, t, 0:CC], start=False, stop=False)
                pe.matmul(o, CM[1][:, g, :], HI[:, t, 0:CC], start=False, stop=True).then_inc(ssm_y, 1)
            pe.wait_ge(ssm_act, 32)

            n = N0["outb"]
            for b in range(4):
                pe.wait_ge(*glu_vec.at(f"bl{2 * (b // 2) + 1}"))
                block_b(n + b, b % 2, [(add["out"], max(4 * b + o - 1, 1)) if 4 * b + o >= 2 else (ssm_act, 32) for o in range(4)],
                        H=XH, L=XL, k0=2 * (b // 2))
            n = N0["glu"]
            for o in range(4):
                s = o // 2
                if o == 0:
                    pe.wait_ge(*glu_vec.at("gl3"))
                if o < 2:
                    pe.wait_ge(add["out"], 15 + o)
                else:
                    pe.wait_ge(*glu_act.at(f"sig{o - 2}"))
                tile_a(n + s, s, o % 2, kt=4, H=GH, L=GL,
                       lhs=lambda k: (WH[:, s, k * 256 + (o % 2) * P:k * 256 + (o % 2) * P + P],
                                      WL[:, s, k * 256 + (o % 2) * P:k * 256 + (o % 2) * P + P]))
            n = N0["outa"]
            for b in range(4):
                pe.wait_ge(*glu_vec.at(f"lo{2 * (b // 2) + 1}"))
                block_b(n + b, b % 2, [(add["out"], 16 + 4 * b + o - 1) if 4 * b + o >= 2 else glu_act.at(f"sig{2 + o}") for o in range(4)],
                        H=XH, L=XL, k0=4 + 2 * (b // 2))

            def cross(l):
                q = f"x{l}"
                n = N0[q]

                v, ac, te = xv[l], xa[l], xp[l]

                def outputs(i, cols, st, bank, ready):
                    pe.wait_ge(*ready)
                    w = cols.stop - cols.start
                    for d in range(2):
                        for m in range(2):
                            mm = mms(PS[:, bank + d, 0:w], VXH[:, st, d, m, :], VXL[:, st, d, m, :], HH[:, m, cols], HL[:, m, cols], m == 0, m == 1)
                    mm.then_inc(te.sem, 1)

                def half_chunk(i, h):
                    j, s = h // 2, h // 6
                    if h % 6 == 0:
                        pe.wait_ge(w_lo, i * 4 + (n + 3 + s))
                    if h % 2 == 0 and j >= 2:
                        pe.wait_ge(*xe[l].at(f"e{j - 2}", i + 1))
                    for k in range(4 * (h % 2), 4 * (h % 2) + 4):
                        w = slice(k * P, (k + 1) * P)
                        mm = mms(PS[:, 6 + j % 2, 0:CW], WH[:, s, w], WL[:, s, w], chunk(XH[:, k, :], j % NCH), chunk(XL[:, k, :], j % NCH),
                                 k == 0, k == KT - 1)
                    if h % 2:
                        mm.then_inc(tile_done if j % NCH == 2 else xc[l], 1)

                def attend(i, more=True):
                    pe.wait_ge(*v.at("ql1", i))
                    pe.wait_ge(*xk[l].at("vl", i))
                    if not (isinstance(i, int) and i == 0):
                        pe.wait_ge(add[q], i * 8 - 1)
                    else:
                        pe.wait_ge(n_rs[q], 6)
                    for k in range(11):
                        t = k
                        if t < 9:
                            nq, c0, st = query_tile(t)
                            if t >= 2:
                                pe.wait_ge(*ac.at(f"ex{t - 2}", i))
                            for d in range(2):
                                mm = mms(PS[0:nq, t % 2, 0:NMEM], XQH[:, d, c0:c0 + nq], XQL[:, d, c0:c0 + nq], KXH[:, st, d, :], KXL[:, st, d, :],
                                         d == 0, d == 1)
                            mm.then_inc(te.sem, 1)
                        if more and k < 10:
                            half_chunk(i, k)
                        if k == 2 and not (isinstance(i, int) and i == 0):
                            pe.wait_ge(add[q], i * 8)
                            pe.nop(nofuse=True)
                        t = k - 2
                        if 0 <= t < 9:
                            nq = query_tile(t)[0]
                            pe.wait_ge(*v.at(f"pn{t}", i))
                            if t >= 2:
                                pe.wait_ge(*v.at(f"pl{t - 2}", i))
                            if t == 0:
                                pe.nop(nofuse=True)
                            for m in range(2):
                                mm = pe.transpose(PS[:, 2 + t % 2, m * P:m * P + nq], PX[0:nq, t % 3, m * P:(m + 1) * P], IDENT[0:nq, 0:nq])
                            mm.then_inc(te.sem, 1)
                        if k == 4:
                            outputs(i, slice(S0, TW), 1, 4, v.at("pl0", i))
                        if k == 8:
                            pe.wait_ge(*v.at("ols", i))
                            outputs(i, slice(0, 512), 0, 4, v.at("pl4", i))
                    if more:
                        half_chunk(i, 10)
                    pe.wait_ge(*v.at("ola", i))
                    outputs(i, slice(512, SEQ), 0, 4, v.at("pl8", i))
                    if more:
                        half_chunk(i, 11)

                def queries(nb):
                    for s in (0, 1):
                        pe.wait_ge(w_lo, nb + (s + 1))
                        pe.wait_ge(add["out" if l == 0 else "c1"], 31 + s)
                        tile_a(0, s, s, wait_lo=False, split=q if s == 0 else None)
                        if s == 0:
                            norm_total(q)

                def round_(i):
                    attend(i)
                    for b in range(2):
                        marks = [v.at("olb", i) if b == 0 and o < 2 else (add[q], i * 8 + (4 * b + o - 1)) for o in range(4)]
                        block_b(i * 4 + (n + 4 + b), b, marks)

                queries(n)
                round_(0)
                with pe.Fori(1, HEADS - 1) as i:
                    round_(i)
                i = HEADS - 1
                attend(i, more=False)
                for b in range(2):
                    block_b(n + 14 + b, b, [v.at("olb", i) if b == 0 and o < 2 else (add[q], i * 8 + (4 * b + o - 1)) for o in range(4)])

            def a_tile(n, s, ps, free, wait_x=None, q=None):
                pe.wait_ge(w_lo, n + 1)
                pe.wait_ge(*free)
                tile_a(0, s, ps, wait_lo=False, split=wait_x)
                if wait_x:
                    norm_total(wait_x)

            def down(nb, s0, ready, free, p0):
                for b in range(2):
                    pe.wait_ge(w_lo, nb + (b + 1))
                    for o in range(4):
                        if free(4 * b + o):
                            pe.wait_ge(*free(4 * b + o))
                        down_tile((s0 + b) % 2, o, (p0 + o) % 2, ready if b == 0 and o == 0 else None)

            def ffn(l):
                q, v = f"f{l}", fv[l]
                n = N0[q]
                before = add[f"x{l}"]
                a_tile(n, 0, 0, (before, 31), wait_x=q)
                a_tile(n + 1, 1, 1, (before, 32))
                a_tile(n + 2, 0, 0, v.at("gate0"))
                a_tile(n + 3, 1, 1, v.at("hid0"))
                with pe.Fori(1, 11) as g:
                    nb = g * 6 + (n - 2)
                    a_tile(nb, 0, 0, v.at("gate1", g - 1))
                    down(nb + 1, 1, (v.at("hid1", g - 1), v.at("lo1", g - 1)),
                         lambda j: None if j == 0 else v.at("gate0", g) if j == 1 else (add[q], g * 8 + (j - 9)), 1)
                    a_tile(nb + 3, 1, 1, (add[q], g * 8 - 1))
                    a_tile(nb + 4, 0, 0, (add[q], g * 8))
                    a_tile(nb + 5, 1, 1, v.at("hid0", g))
                down(n + 64, 0, (v.at("hid1", 10), v.at("lo1", 10)),
                     lambda j: None if j < 2 else (add[q], 79 + j), 0)

            def down_tile(s, o, ps, ready=None):
                for k in range(2):
                    if ready:
                        pe.wait_ge(*ready[k])
                    w = slice(k * 512 + o * P, k * 512 + (o + 1) * P)
                    for c in range(NCH):
                        mm = mms(PS[:, 3 * ps + c, 0:CW], WH[:, s, w], WL[:, s, w], chunk(HH[:, k, :], c), chunk(HL[:, k, :], c),
                                 k == 0, k == 1)
                mm.then_inc(tile_done, 1)

            def conv():
                q, n = "c1", N0["c1"]
                a_tile(n, 0, 0, (add["f0"], 87), wait_x=q)
                a_tile(n + 1, 1, 1, (add["f0"], 88))
                for b, x in enumerate(("cc0", "zc0", "hid0", "cc1")):
                    a_tile(n + 2 + b, b % 2, b % 2, cv.at(x))
                with pe.Fori(1, 4) as g:
                    nb = g * 8 + (n - 2)
                    a_tile(nb, 0, 0, cv.at("zc1", g - 1))
                    down(nb + 1, 1, (cv.at("hid1", g - 1), cv.at("lo1", g - 1)),
                         lambda j: None if j == 0 else cv.at("cc0", g) if j == 1 else (add[q], g * 8 + (j - 9)), 1)
                    a_tile(nb + 3, 1, 1, (add[q], g * 8 - 1))
                    a_tile(nb + 4, 0, 0, (add[q], g * 8))
                    for b, x in enumerate(("zc0", "hid0", "cc1")):
                        a_tile(nb + (5 + b), (1 + b) % 2, (1 + b) % 2, cv.at(x, g))
                down(n + 30, 0, (cv.at("hid1", 3), cv.at("lo1", 3)),
                     lambda j: None if j < 2 else (add[q], 23 + j), 0)

            cross(0)
            ffn(0)
            conv()
            cross(1)
            ffn(1)
            norm_total("fin")

        @block.sync
        def _(sp):
            sp.dma_start(MR[:], a["memT"]).then_inc(ld, 16)
            sp.dma_start(COL[:], a["cols"]).then_inc(ld, 16)
            sp.dma_start(IDENT[:], a["ident"]).then_inc(ld, 16)

            def block_at(n):
                return a["w"][bass.ds(n, 1)].rearrange("o p n -> (o p) n")

            for s in range(4):
                if s == 2:
                    sp.wait_ge(mem_lo, 1)
                sp.dma_start(kv_slot(s)[0], a["w"][s]).then_inc(kv_raw[s], 16)

            def pair_rows(ri, q, g):
                return a["cm"][64 * q:64 * q + 64, ri].rearrange("p (t g m) -> p t g m", t=16, g=2)[:, :, g, :]

            def kv_stream(lo, hi):
                with sp.Fori(lo, hi) as i:
                    for s in range(4):
                        sp.wait_ge(w_lo, i * 4 + (s - 3))
                        sp.dma_start(kv_slot(s)[0], block_at(i * 4 + s)).then_inc(kv_raw[s], 16)

            kv_stream(1, 3)
            for ri in range(2):
                for q in range(2):
                    sp.dma_start(pair_rows(ri, q, 1 - q), a["zeros"][0:64].rearrange("p (t m) -> p t m", t=16)).then_inc(par_dma, 16)
            for part in (range(0, 4), range(4, CK - 1)):
                kv_stream(3 + 2 * (part.start // 4), 5 + 2 * (part.start // 4))
                for j in part:
                    r = 16 * (7 - j)
                    sp.dma_start(a["tm"][0:r, j, :], a["zeros"][0:r, 0:512]).then_inc(par_dma, 16)
            kv_stream(7, N0["inp"] // 4)
            for s in (0, 1):
                sp.wait_ge(w_lo, N0["inp"] - 3 + s)
                sp.dma_start(WR[:, s, :], a["w"][N0["inp"] + s]).then_inc(w_raw[s], 16)
            sp.wait_ge(par_vec, mark["C"])
            for d, t in ((a["er"], ERP), (a["ei"], EIP)):
                sp.dma_start(d, t[:]).then_inc(par_dma, 16)
            for ri, t in enumerate((T1, T2)):
                for q in range(2):
                    sp.dma_start(pair_rows(ri, q, q), t[64 * q:64 * q + 64].rearrange("p t j h -> p t (j h)")).then_inc(par_dma, 16)
            sp.wait_ge(par_vec, mark["K"])
            for j in range(CK):
                r = 16 * (7 - j)
                sp.dma_start(a["tm"][r:P, j, :], KR[0:P - r, :]).then_inc(par_dma, 16)
            sp.wait_ge(par_act, 8)
            sp.dma_start(a["bt"], BTP[:]).then_inc(par_dma, 16)

            def stream(lo, hi):
                with sp.Fori(lo // 2, hi // 2) as i:
                    for s in (0, 1):
                        sp.wait_ge(w_lo, i * 2 + (s - 1))
                        sp.dma_start(WR[:, s, :], block_at(i * 2 + s)).then_inc(w_raw[s], 16)

            stream(N0["inp"] + 2, N0["outb"] + 2)
            sp.wait_ge(tile_done, T0["outb"])
            for t, nm in ((BT, "bt"), (ER, "er"), (EI, "ei"), (TMR, "tm")):
                if nm == "tm":
                    sp.wait_ge(*ivec.at("rot_q3"))
                sp.dma_start(t[:], a[nm]).then_inc(ssm_ld, 16)
            sp.wait_ge(*ivec.at("u3S"))
            sp.dma_start(a["uj"].rearrange("(t g) c j k -> (g c) t (j k)", g=8), UJ[:].rearrange("p t j c -> p t (j c)")).then_inc(uj_out, 16)
            sp.wait_ge(uj_out, 16)
            for r in range(CK):
                sp.dma_start(UG[16 * (7 - r):16 * (7 - r) + 16, :, :], a["uj"].rearrange("g c j k -> j c g k")[r]).then_inc(ug_in, 16)
            sp.wait_ge(ssm_v, 32)
            sp.dma_start(CM[0][:].rearrange("p g m -> p (g m)"), a["cm"][:, 0]).then_inc(cm_ld, 16)
            sp.wait_ge(ssm_rot, 24)
            sp.dma_start(CM[1][:].rearrange("p g m -> p (g m)"), a["cm"][:, 1]).then_inc(cm_ld, 16)
            sp.wait_ge(ssm_act, 32)
            for j in range(CK):
                sp.dma_start(a["yj"].rearrange("g c j k -> j c g k")[j], UG[16 * j:16 * j + 16, :, :]).then_inc(y_out, 16)
            sp.wait_ge(y_out, 16 * CK)
            sp.dma_start(UJ[:].rearrange("p t j c -> p t (j c)"), a["yj"].rearrange("(t g) c j k -> (g c) t (j k)", g=8)).then_inc(y_in, 16)
            stream(N0["outb"] + 2, NBLOCKS)
            for m in range(KT):
                sp.wait_ge(fin, m + 1)
                sp.dma_start(a["y"][:, m, :], X[:, m, :]).then_inc(outs, 16)
            sp.wait_ge(outs, 16 * KT)

        @block.gpsimd
        def _(pool):
            def lo_block(n, s):
                pool.wait_ge(w_hi, n + 1)
                pool.tensor_tensor(WL[:, s, :], WR[:, s, :], WH[:, s, :].bitcast(F32), ALU.subtract).then_inc(w_lo, 1)

            def sum_squares(q, m):
                pool.wait_ge(*n_act[q].at(f"sq{m}"))
                sq = SQ[:, m % 2, :]
                if m == 0:
                    pool.tensor_copy(RSTD[:], sq).then_inc(n_sum[q], 1)
                else:
                    pool.wait_ge(n_sum[q], m)
                    pool.tensor_tensor(RSTD[:], RSTD[:], sq, ALU.add).then_inc(n_sum[q], 1)

            done = [0]

            def blocks(upto):
                lo, hi = done[0] // 2, upto // 2
                with pool.Fori(lo, hi) as i:
                    for s in (0, 1):
                        lo_block(i * 2 + s, s)
                done[0] = upto

            with pool.Fori(0, N0["inp"] // 4) as i:
                for s in range(4):
                    pool.wait_ge(w_hi, i * 4 + (s + 1))
                    raw, h, l = kv_slot(s)
                    pool.tensor_tensor(l, raw, h.bitcast(F32), ALU.subtract).then_inc(w_lo, 1)
            done[0] = N0["inp"]
            blocks(N0["outb"])

            def do(ins):
                rot[0] += 1
                ins.then_inc(ssm_rot, 1)
                pool.wait_ge(ssm_rot, rot[0])
            rot = [0]
            segments = ((1, NCK, 0), (NCK + 2, DEC // CK, NCK))
            pool.wait_ge(tm_made, 1)
            pool.wait_ge(ssm_copy, 32)
            for lo, w, so in segments:
                hr, hi = HR[:, :, lo:lo + w], HI[:, :, lo:lo + w]
                er, ei = ER[:, :, 1:w + 1], EI[:, :, 1:w + 1]
                s1, s2 = S1[:, :, so:so + w], S2[:, :, so:so + w]
                do(pool.tensor_tensor(s1, er, hr, ALU.mult))
                do(pool.tensor_tensor(s2, ei, hi, ALU.mult))
                do(pool.tensor_tensor(s1, s1, s2, ALU.add))
                do(pool.tensor_tensor(s2, er, hi, ALU.mult))
                do(pool.tensor_tensor(hr, ei, hr, ALU.mult))
                do(pool.tensor_tensor(s2, s2, hr, ALU.subtract))
            pool.wait_ge(ssm_scan, 66)
            for lo, w, so in segments:
                hr, hi = HR[:, :, lo:lo + w], HI[:, :, lo:lo + w]
                er, ei = ER[:, :, 1:w + 1], EI[:, :, 1:w + 1]
                s1, s2 = S1[:, :, so:so + w], S2[:, :, so:so + w]
                do(pool.tensor_tensor(s1, er, hr, ALU.mult))
                do(pool.tensor_tensor(s2, ei, hi, ALU.mult))
                do(pool.tensor_tensor(hi, er, hi, ALU.mult))
                do(pool.tensor_tensor(hr, ei, hr, ALU.mult))
                do(pool.tensor_tensor(hi, hi, hr, ALU.add))
                do(pool.tensor_tensor(hr, s1, s2, ALU.subtract))
            do(pool.tensor_copy(HR[:, :, NCK + 1], col("h0_re", 0, 16)))
            do(pool.tensor_copy(HI[:, :, NCK + 1], col("h0_im", 0, 16)))
            for k, (h, c) in enumerate(((HR, NCK), (HI, NCK), (HR, CC), (HI, CC))):
                do(pool.tensor_copy(SMALL[:, 16 * k:16 * k + 16], h[:, :, c]))
            assert rot[0] == mark["S"]
            def memory_blocks(l, n):
                def low():
                    for h, x, xh, xl in (("kh", KX, KXH, KXL), ("vh", VX, VXH, VXL)):
                        pool.wait_ge(*xa[l].at(h, r))
                        pool.tensor_tensor(xl[:], x[:], xh[:].bitcast(F32), ALU.subtract).then_inc(xk[l].sem, 1)
                lo_block(n + 2, 0)
                r = 0
                low()
                lo_block(n + 3, 1)
                with pool.Fori(1, HEADS) as r:
                    for s in (0, 1):
                        lo_block(r * 4 + (n + s), s)
                    low()
                    for s in (0, 1):
                        lo_block(r * 4 + (n + 2 + s), s)

            for ph, nxt in (("out", "x0"), ("x0", "f0"), ("f0", "c1"), ("c1", "x1"), ("x1", "f1"), ("f1", "fin")):
                start = N0[nxt] if nxt != "fin" else NBLOCKS
                if ph[0] == "x":
                    memory_blocks(int(ph[1]), N0[ph])
                else:
                    blocks(start)
                for b in range(2):
                    for m in range(4):
                        sum_squares(nxt, 4 * b + m)
                    if nxt != "fin":
                        lo_block(start + b, b)
                done[0] = start + 2

        @block.scalar
        def _(act):
            def hi_block(n, s):
                act.wait_ge(w_raw[s], (n - s) * 8 + (16 - 8 * N0["inp"]))
                act.activation(WH[:, s, :], WR[:, s, :], ACT.Copy).then_inc(w_hi, 1)

            def step(n, s, tiles):
                act.wait_ge(tile_done, tiles)
                hi_block(n + 2, s)

            def norm_tile(q, m, x_final):
                act.wait_ge(*x_final)
                if q != "inp":
                    if m >= 2:
                        act.wait_ge(n_sum[q], m - 1)
                    act.activation(SQ[:, m % 2, :], X[:, m, :], ACT.Square).then_inc(n_act[q].sem, 1)
                if q != "fin":
                    act.activation(XH[:, m, :], X[:, m, :], ACT.Copy, scale=col(GAIN[q], m)).then_inc(n_act[q].sem, 1)

            def rstd(q):
                for c in range(NCH):
                    act.wait_ge(n_tot[q], c + 1)
                    act.activation(chunk(LNV[:], c), PS[:, 6 + c % 2, 0:CW], ACT.Ln, bias=EPSC[:], scale=1.0 / D).then_inc(n_rs[q], 1)
                act.wait_ge(n_rs[q], 3)
                for c in range(NCH):
                    act.activation(chunk(RSTD[:], c), chunk(LNV[:], c), ACT.Exp, scale=-0.5).then_inc(n_rs[q], 1)

            act.wait_ge(ld, 48)
            act.activation(MH[:], MR[:], ACT.Copy).then_inc(mem_hi, 1)

            def kv_hi(s, q):
                act.wait_ge(kv_raw[s], q * 16 + 16)
                raw, h, _ = kv_slot(s)
                act.activation(h, raw, ACT.Copy).then_inc(w_hi, 1)

            def kv_block(part, q, s):
                act.wait_ge(tile_done, q * 4 + (s + 1))
                if not (isinstance(q, int) and q == 7):
                    kv_hi(s, q + 1)
                elif s < 2:
                    hi_block(N0["inp"] + s, s)
                if part % 2 == 0:
                    act.activation(KVS[:, part % 2, bass.ds(q * 4 + (s - 8 * part), 1), :].rearrange("p o m -> p (o m)"),
                                   PS[:, 3 * (s % 2), 0:NMEM], ACT.Copy).then_inc(kv_copy, 1)
                elif s % 2:
                    for mt in range(2):
                        act.activation(KVS[:, part % 2, bass.ds(q * 4 + (s - 1 - 8 * part), 2), mt * P:(mt + 1) * P],
                                       PS[:, VALUE_BANKS[s // 2][mt], 0:256].rearrange("p (b c) -> p b c", b=2), ACT.Copy).then_inc(kv_copy, 1)

            def parameters():
                for k in range(8):
                    act.wait_ge(par_pe, k + 1)
                    act.activation(BTP[:, k // 4, 4 * (k % 4):4 * (k % 4) + 4, :].rearrange("p t c -> p (t c)"),
                                   PS[:, 6 + k % 2, :], ACT.Copy).then_inc(par_act, 1)

            for s in range(4):
                kv_hi(s, 0)
            for t, nm in ((BR, "b_re"), (BI, "b_im"), (CR, "c_re"), (CI, "c_im"), (DD, "d_diag")):
                act.dma_start(t[:], a[nm]).then_inc(par_ld, 16)
            for part in range(4):
                if part >= 2:
                    act.wait_ge(kv_out[part - 2], 16)
                if part < 3:
                    with act.Fori(2 * part, 2 * part + 2) as q:
                        for s in range(4):
                            kv_block(part, q, s)
                            if part < 2 and s % 2:
                                m = bass.ds(q * 2 + s // 2, 1)
                                act.dma_start(X[:, m, :], a["x"][:, m, :]).then_inc(x_ld, 16)
                else:
                    for s in range(4):
                        kv_block(3, 6, s)
                    parameters()
                    act.wait_ge(ready, 2)
                    for s in range(4):
                        kv_block(3, 7, s)
                        if s == 1:
                            act.wait_ge(par_dma, 16 * 26)
                        if s % 2:
                            for m in (s - 1, s):
                                norm_tile("inp", m, (x_ld, 16 * KT))
                act.wait_ge(kv_copy, 8 * part + 8)
                act.dma_start(a["memkv"][part], KVS[:, part % 2].rearrange("p b m -> p (b m)")).then_inc(kv_out[part], 16)

            act.dma_start(COS[:], a["cos"]).then_inc(mix_ld, 16)
            act.dma_start(SIN[:], a["sin"]).then_inc(mix_ld, 16)
            for m in range(4, KT):
                norm_tile("inp", m, (x_ld, 16 * KT))
            for s in kv_out:
                act.wait_ge(s, 16)
            act.wait_ge(n_sum["inp"], mark["inp"])
            act.dma_start(ROT[:], a["rot"]).then_inc(mix_ld, 16)
            act.dma_start(MASK[:], a["mask"]).then_inc(mix_ld, 16)
            act.dma_start(KB[:, 1152:1280], a["past_k"]).then_inc(mix_ld, 16)
            act.dma_start(VB[:, 9, :], a["past_v"]).then_inc(mix_ld, 16)
            n = N0["inp"]
            for j, x in enumerate(INP):
                if x in INP_BLOCKS:
                    if n < N0["outb"] - 2:
                        step(n, n % 2, T0["inp"] + j + 1)
                    n += 1
                if j == 0:
                    rstd("inp")
                if x == "VT":
                    s = j % 2
                    act.wait_ge(tile_done, T0["inp"] + j + 1)
                    act.wait_ge(zeroed, mark["Z"])
                    act.activation(VB[:, 1:9, :].rearrange("p (b s) c -> p b (s c)", b=2), PS[:, 3 * s:3 * s + 2, :], ACT.Copy).then_inc(iact.sem, 1)
                    act.activation(VB[0:DEC, 10, :], PS[0:DEC, 3 * s + 2, 0:P], ACT.Copy).then_inc(iact.sem, 1)
                if x == "q1":
                    act.wait_ge(*ivec.at("rotS_k"))
                    act.dma_start(a["k_new"][:, 0:P], KB[:, 1024:1152]).then_inc(small_out, 16)
                    act.dma_start(a["k_new"][:, P:P + DEC], KB[:, 1280:1312]).then_inc(small_out, 16)
                    act.dma_start(a["v_new"][:, 0:P], VTT[:, SEQ - P:SEQ]).then_inc(small_out, 16)
                    act.dma_start(a["v_new"][:, P:P + DEC], VTT[:, S0:TW]).then_inc(small_out, 16)
            def queries(k, nq=P):
                cols = slice(S0, TW) if isinstance(k, int) and k == 8 else slice(k * P, k * P + P) if isinstance(k, int) else bass.ds(k * P, P)
                return Q[:, :, cols]

            def stage(k, nq=P):
                if not (isinstance(k, int) and k == 0):
                    act.wait_ge(*aa_pe.at("S3", k - 1))
                    act.nop(nofuse=True)
                act.activation(QS[:, :, 0:nq], queries(k), ACT.Copy).then_inc(aq.sem, 1)
                for g in range(2):
                    r = slice(64 * g, 64 * g + 64)
                    act.activation(KS[r, 256 * g:256 * g + 256], KB[r, 1152:1408] if nq < P else KB[r, k * P:k * P + 256] if isinstance(k, int)
                                   else KB[r, bass.ds(k * P, 256)], ACT.Copy).then_inc(aq.sem, 1)

            def att(k, s, nq=P, values=True, scores=True, then=P):
                j, z, nj = k - 1, 1 - s, P if scores else DEC
                if values:
                    for b, nm in enumerate(("PTa", "PTb")):
                        act.wait_ge(*ab_pe.at(nm, j))
                        act.activation(PT[:, 2 * b:2 * b + 2, :, 0:nj], PS[:, 4 + b, :].rearrange("p (h k q) -> p h k q", h=2, k=2)[:, :, :, 0:nj],
                                       ACT.Copy).then_inc(ab_act.sem, 1)
                if then:
                    stage(k + 1, then)
                if scores:
                    act.wait_ge(*aa_vec.at("ds", k))
                    for h in range(8):
                        act.activation(SB[0:nq, s, h, :], SB[0:nq, s, h, :], ACT.Exp, bias=SMX[0:nq, s, 8 + h:9 + h],
                                       accum_out=SMX[0:nq, s, 16 + h:17 + h]).then_inc(aa_act.sem, 1)
                    act.activation(SMX[0:nq, s, 24:32], SMX[0:nq, s, 40:48], ACT.Exp).then_inc(aa_act.sem, 1)
                if values:
                    act.wait_ge(*ab_pe.at("OT", j))
                    act.nop(nofuse=True)
                    act.activation(Q[:, :, S0:TW] if not scores else queries(j), PS[:, 4, :].rearrange("p (j q) -> p j q", j=4)[:, :, 0:nj],
                                   ACT.Copy).then_inc(ab_act.sem, 1)

            act.wait_ge(*ivec.at("rot_q3"))
            act.wait_ge(*iact.at("VTb"))
            act.wait_ge(zeroed, mark["KS"])
            stage(0)
            att(0, 0, values=False)
            att(1, 1)
            att(2, 0)
            act.wait_ge(ssm_ld, 64)
            act.activation(TM[:].rearrange("p g (j h) -> p j g h", j=CK), TMR[:].rearrange("p j (g h) -> p j g h", g=32),
                           ACT.Copy).then_inc(tm_made, 1)
            for k in range(3, 7):
                att(k, k % 2)
            att(7, 1, then=DEC)
            att(8, 0, nq=DEC, then=0)
            att(9, 1, scores=False, then=0)
            act.wait_ge(*ab_pe.at("PTd", 8))
            for s in (0, 1):
                hi_block(N0["outb"] + s, s)

            for g in range(32):
                act.wait_ge(ssm_y, 1 + g)
                act.activation(UG[:, g, :], PS[:, g % 8, 0:CC], ACT.Copy).then_inc(ssm_act, 1)
            act.wait_ge(ssm_act, 32)
            act.wait_ge(ssm_rot, mark["S"])
            for j in range(4):
                act.activation(XH[:, j, :], Q[:, j, :], ACT.Copy).then_inc(glu_act.sem, 1)
            act.dma_start(a["ssm_new"], SMALL[:]).then_inc(small_out, 16)
            act.wait_ge(*glu_vec.at("bl3"))
            act.wait_ge(y_in, 16)
            n = N0["outb"]
            for j in range(4):
                act.activation(GY[:, j, 0:SEQ].rearrange("p (c j) -> p c j", j=CK), UJ[:, j, :, 0:NCK].rearrange("p j c -> p c j"),
                               ACT.Gelu_apprx_tanh).then_inc(glu_act.sem, 1)
                act.activation(GY[:, j, S0:TW].rearrange("p (c j) -> p c j", j=CK), UJ[:, j, :, NCK + 1:CC].rearrange("p j c -> p c j"),
                               ACT.Gelu_apprx_tanh).then_inc(glu_act.sem, 1)
                act.wait_ge(*glu_act.at(f"gs{j}"))
                act.activation(GH[:, j, :], GY[:, j, :], ACT.Copy).then_inc(glu_act.sem, 1)
                if j % 2:
                    step(n + j // 2, j // 2, T0["outb"] + 4 * (j // 2) + 4)
            for b in (2, 3):
                step(n + b, b % 2, T0["outb"] + 4 * b + 4)
            n = N0["glu"]
            for o in range(4):
                act.wait_ge(tile_done, T0["glu"] + o + 1)
                if o:
                    act.wait_ge(*glu_vec.at(f"mul{o - 1}"))
                act.activation(tiled(LNV[:]), pset(o % 2), ACT.Sigmoid).then_inc(glu_act.sem, 1)
                if o % 2:
                    step(n + o // 2, o // 2, T0["glu"] + o + 1)
                act.wait_ge(*glu_vec.at(f"mul{o}"))
                act.activation(XH[:, 4 + o, :], GY[:, o, :], ACT.Copy).then_inc(glu_act.sem, 1)

            def last_norm(ph, n, t, nxt, whole=None):
                for b in range(2):
                    for m in range(4 * b, 4 * b + 4):
                        if whole and m == 6:
                            act.wait_ge(tile_done, whole)
                        norm_tile(nxt, m, (add[ph], ADDS[ph] - KT + m + 1))
                    if nxt != "fin":
                        step(n + b, b, t + 4 * b + 4)

            n, t = N0["outa"], T0["outa"]
            for b in range(2):
                step(n + b, b % 2, t + 4 * b + 4)
            last_norm("out", n + 2, t + 8, "x0", whole=T0["x0"])

            def cross(l, nxt):
                q, v, ac, te = f"x{l}", xv[l], xa[l], xp[l]
                n, t0 = N0[q], T0[q]

                def loads(h):
                    for st, src in ((0, "memkv"), (1, "smemkv")):
                        act.dma_start(KX[:, st].rearrange("p d m -> p (d m)"), a[src][2 * l][:, bass.ds(h * 512, 512)]).then_inc(xld[l], 16)
                        act.dma_start(VX[:, st].rearrange("p d m e -> p (d m e)"), a[src][2 * l + 1][:, bass.ds(h * 512, 512)]).then_inc(xld[l], 16)

                def memory_high(i):
                    act.wait_ge(xld[l], i * 64 + 64)
                    act.activation(KXH[:], KX[:], ACT.Copy).then_inc(ac.sem, 1)
                    act.activation(VXH[:], VX[:], ACT.Copy).then_inc(ac.sem, 1)

                def query_high(i):
                    for s in (0, 1):
                        act.wait_ge(*xe[l].at(f"e{NCH * s + 2}", i))
                        act.activation(XQH[:, s, :], XQ[:, s, :], ACT.Copy).then_inc(ac.sem, 1)

                def out_high(cols, bank, made):
                    act.wait_ge(*made)
                    act.activation(HH[:, :, cols], PS[:, bank:bank + 2, 0:cols.stop - cols.start], ACT.Copy).then_inc(ac.sem, 1)

                def attend(i, more=True):
                    if more:
                        act.wait_ge(*xk[l].at("vl", i))
                        act.wait_ge(*ac.at("vh", i))
                        loads(i + 1)
                    for k in range(11):
                        t = k
                        if t < 9:
                            nq = query_tile(t)[0]
                            act.wait_ge(*v.at(f"nm{t}", i))
                            if t >= 3:
                                act.wait_ge(*te.at(f"T{t - 3}", i))
                            act.activation(PX[0:nq, t % 3, :], PS[0:nq, t % 2, 0:NMEM], ACT.Exp, bias=NX[0:nq, t % 3, 1:2], scale=1.0 / 16,
                                           accum_out=NX[0:nq, t % 3, 2:3]).then_inc(ac.sem, 1)
                        t = k - 2
                        if 0 <= t < 9:
                            nq, c0, _ = query_tile(t)
                            act.wait_ge(*te.at(f"T{t}", i))
                            act.activation(HH[:, :, c0:c0 + nq], PS[:, 2 + t % 2, 0:NMEM].rearrange("p (d q) -> p d q", d=2)[:, :, 0:nq],
                                           ACT.Copy).then_inc(ac.sem, 1)
                        if more and k == 7:
                            step(i * 4 + (n + 2), 0, i * 10 + (t0 + 3))
                        if k == 5:
                            out_high(slice(S0, TW), 4, te.at("Vs", i))
                        if k == 9:
                            out_high(slice(0, 512), 4, te.at("Va", i))
                    out_high(slice(512, SEQ), 4, te.at("Vb", i))

                def round_(i):
                    attend(i)
                    step(i * 4 + (n + 3), 1, i * 10 + (t0 + 4))
                    memory_high(i + 1)
                    query_high(i + 1)
                    for s in (0, 1):
                        step(i * 4 + (n + 4 + s), s, i * 10 + (t0 + 8 + 4 * s))

                loads(0)
                for s in (0, 1):
                    step(n + s, s, t0 + s + 1)
                    if s == 0:
                        rstd(q)
                        memory_high(0)
                query_high(0)
                round_(0)
                with act.Fori(1, HEADS - 1) as i:
                    round_(i)
                attend(HEADS - 1, more=False)
                last_norm(q, n + 14, t0 + 32, nxt)

            def new_states(s, g, e):
                act.activation(STF[:, 0:2, bass.ds(g * 2 + e, 1)].rearrange("p s o -> p (s o)"), G[:, e, SEQ:SEQ + 2], ACT.Copy).then_inc(s.sem, 1)
                act.activation(STF[:, 2:4, bass.ds(g * 2 + e, 1)].rearrange("p s o -> p (s o)"), G[:, e, TW:TW + 2], ACT.Copy).then_inc(s.sem, 1)

            def ffn(l, nxt):
                q, v, ac = f"f{l}", fv[l], fa[l]
                n, t0 = N0[q], T0[q]

                def gated(g, e):
                    act.wait_ge(*v.at(f"c{e}", g))
                    if e == 1:
                        act.wait_ge(*v.at("sm0", g))
                    elif not (isinstance(g, int) and g == 0):
                        act.wait_ge(*v.at("sm1", g - 1))
                    act.activation(ACTV[:], TAP[:, e, :], ACT.Silu).then_inc(ac.sem, 1)
                    new_states(ac, g, e)

                def high(g, e):
                    act.wait_ge(*v.at(f"hid{e}", g))
                    act.activation(HH[:, e, :], HID[:], ACT.Copy).then_inc(ac.sem, 1)

                def group(g, nb, t, first=False):
                    step(nb, 0, t + 1)
                    if first:
                        rstd(q)
                    o, b0 = (1, 1) if first else (9, 3)
                    gated(g, 0)
                    if not first:
                        for b in range(2):
                            step(nb + (1 + b), (1 + b) % 2, t + (5 + 4 * b))
                    step(nb + b0, b0 % 2, t + (o + 1))
                    high(g, 0)
                    step(nb + (b0 + 1), (b0 + 1) % 2, t + (o + 2))
                    gated(g, 1)
                    step(nb + (b0 + 2), (b0 + 2) % 2, t + (o + 3))
                    high(g, 1)

                group(0, n, t0, True)
                with act.Fori(1, 11) as g:
                    group(g, g * 6 + (n - 2), g * 12 + (t0 - 8))
                act.wait_ge(*ac.at("nb1", 10))
                act.dma_start(a[f"st_f{l}"], STF[:]).then_inc(st_out[q], 16)
                last_norm(q, n + 64, t0 + 124, nxt)
                act.wait_ge(st_out[q], 16)

            def conv(nxt):
                n, t0 = N0["c1"], T0["c1"]

                def high(g, e):
                    act.wait_ge(*cv.at(f"zc{e}", g))
                    act.nop(nofuse=True)
                    new_states(ca, g, e)
                    act.wait_ge(*cv.at(f"hid{e}", g))
                    act.activation(HH[:, e, :], HID[:], ACT.Copy).then_inc(ca.sem, 1)

                def group(g, nb, t, first=False):
                    step(nb, 0, t + 1)
                    if first:
                        rstd("c1")
                    o, b0 = (1, 1) if first else (9, 3)
                    if not first:
                        for b in range(2):
                            step(nb + (1 + b), (1 + b) % 2, t + (5 + 4 * b))
                    step(nb + b0, b0 % 2, t + (o + 1))
                    step(nb + (b0 + 1), (b0 + 1) % 2, t + (o + 2))
                    high(g, 0)
                    for b in (2, 3, 4):
                        step(nb + (b0 + b), (b0 + b) % 2, t + (o + b + 1))
                    high(g, 1)

                group(0, n, t0, True)
                with act.Fori(1, 4) as g:
                    group(g, g * 8 + (n - 2), g * 14 + (t0 - 8))
                act.wait_ge(*ca.at("hi1", 3))
                act.dma_start(a["st_c1"], STF[:, :, 0:KT]).then_inc(st_out["c1"], 16)
                last_norm("c1", n + 30, t0 + 48, nxt)
                act.wait_ge(st_out["c1"], 16)

            cross(0, "f0")
            ffn(0, "c1")
            conv("x1")
            cross(1, "f1")
            ffn(1, "fin")
            rstd("fin")
            act.wait_ge(small_out, 80)




def _layout(i):
    f = {k: np.asarray(v) for k, v in i.items()}

    def kblocks(w):
        k, n = w.shape
        return w.reshape(KT, P, n // P, P).transpose(2, 1, 0, 3).reshape(n // P, P, BLK)

    def rows2(w):
        n = w.shape[0]
        return w.reshape(n // 256, 2, P, 2, 512).transpose(0, 3, 2, 1, 4).reshape(-1, P, BLK)

    pair = np.array([h * 64 + d for j in range(4) for h in (j, j + 4) for d in range(64)])
    we = f["w_in_even"][0]
    u, q, k, v = we[:, :512], we[:, 512:1024][:, pair], we[:, 1024:1152], we[:, 1152:1280]
    inp = {"k": kblocks(k)[0], "v": kblocks(v)[0]}
    inp.update({f"u{t}": kblocks(u)[t] for t in range(4)})
    inp.update({f"q{t}": kblocks(q)[t] for t in range(4)})
    wg = f["w_glu"][0].reshape(4, P, 2, 256).transpose(2, 1, 0, 3).reshape(2, P, BLK)
    wo = f["w_out_even"][0]
    wo = np.concatenate([wo[:512], wo[512:][pair]])
    blocks = []
    for l in (0, 1):
        wkv = f["xattn_wkv"][l]
        blocks += list(kblocks(wkv[:, :D]))
        blocks += list(wkv[:, D:].reshape(2, 4, P, 4, 256).transpose(3, 0, 2, 1, 4).reshape(8, P, BLK))
    wo = list(rows2(wo))
    blocks += [inp[x] for x in INP_BLOCKS] + wo[4:] + list(wg) + wo[:4]

    def skewed(a_of, na, down, groups):
        down = list(rows2(down))
        for g in range(groups):
            aa = a_of(g)
            blocks.append(aa[0])
            if g:
                blocks.extend(down[2 * g - 2:2 * g])
            blocks.extend(aa[1:])
        blocks.extend(down[-2:])

    for l in (0, 1):
        if l == 1:
            w = kblocks(f["w_in_odd"][0])
            skewed(lambda g: [w[c * KT + 2 * g + e] for e in (0, 1) for c in (1, 2, 0)], 6, f["w_out_odd"][0], 4)
        wq, wx = kblocks(f["xattn_wq"][l]), rows2(f["xattn_wo"][l])
        blocks += list(wq[0:2])
        for h in range(HEADS):
            blocks += list(wq[2 * h + 2:2 * h + 4]) + list(wx[2 * h:2 * h + 2])
        w = kblocks(f["ffn_w_up"][l])
        skewed(lambda g: [w[c * FT + 2 * g + e] for e in (0, 1) for c in (0, 1)], 4, f["ffn_w_down"][l], 11)
    w = np.stack(blocks)
    assert w.shape == (NBLOCKS, P, BLK)

    def feat(x):
        return x.reshape(x.shape[0], -1, P).transpose(2, 1, 0)

    cols = np.zeros((P, NCOL), np.float32)

    def put(name, x):
        c, n = COLS[name]
        cols[:, c:c + n] = x.reshape(P, n)
    for nm, key in (("mix", "norm_mix"), ("x", "norm_xattn"), ("f", "norm_ffn")):
        for l in (0, 1):
            put(f"g_{nm}{l}", f[key][l].reshape(KT, P).T)
    put("g_fin", f["norm_final"].reshape(KT, P).T)
    put("cm_w", f["conv_mix_w"][0].reshape(3 * KT, P).T)
    put("cm_s", f["state_conv_mix"][0, 0].reshape(2 * KT, P).T)
    for l in (0, 1):
        put(f"cf_w{l}", f["ffn_conv_w"][l].reshape(3 * FT, P).T)
        put(f"cf_s{l}", f["state_conv_ffn"][l, 0].reshape(2 * FT, P).T)
    put("sink", np.broadcast_to(f["attn_sinks"][0][[0, 4, 1, 5, 2, 6, 3, 7]], (P, 8)))
    for nm, key in (("a_re", "ssm_a_re"), ("a_im", "ssm_a_im"), ("log_dt", "ssm_log_dt")):
        put(nm, f[key][0].reshape(16, P).T)
    put("h0_re", f["state_ssm_re"][0, 0].reshape(16, P).T)
    put("h0_im", f["state_ssm_im"][0, 0].reshape(16, P).T)

    x = np.zeros((P, KT, TW), np.float32)
    x[:, :, :SEQ] = feat(f["x_prompt"][0])
    x[:, :, S0:] = feat(f["x_sample"][0])
    smem = []
    for l in (0, 1):
        smem.append(feat(f["cache_mem_k"][l, 0].reshape(NMEM, D)).reshape(P, 2048))
        smem.append(f["cache_mem_v"][l, 0].reshape(2, P, KT, P).transpose(1, 2, 0, 3).reshape(P, 2048))

    def state(x):
        return x.reshape(16, P, -1).transpose(1, 0, 2)

    def cstate(x):
        return x.reshape(16, 2, 16, 64).transpose(1, 3, 0, 2).reshape(P, 16, 16)
    dd = np.zeros((16, 32, 16), np.float32)
    dd[np.arange(16), :, np.arange(16)] = f["ssm_d"][0].T

    inv = np.float32(10000.0) ** (-np.arange(32, dtype=np.float32) * np.float32(2.0) / np.float32(64))
    pos = np.zeros(TW, np.float32)
    pos[:SEQ], pos[S0:] = np.arange(SEQ), 512 + np.arange(DEC)
    ang = (pos[None, :] * inv[:, None]).astype(np.float32)
    rot = np.zeros((P, P), np.float32)
    for b in (0, 64):
        for m in range(32):
            rot[b + 32 + m, b + m] = -1.0
            rot[b + m, b + 32 + m] = 1.0
    mask = np.full((P, 3, 256), NEG, np.float32)
    mask[:64, 0, 128:192] = 0
    mask[64:, 0, 128:256] = 0
    mask[:64, 1, 0:192] = 0
    mask[64:, 1, 64:256] = 0
    mask[:, 2, 0:160] = 0
    return {
        "w": w, "cols": cols, "x": x, "memT": np.ascontiguousarray(feat(f["mem_prompt"][0])), "smemkv": np.stack(smem),
        "past_k": f["cache_win_k"][0, 0].reshape(128, P).T, "past_v": f["cache_win_v"][0, 0].reshape(128, P),
        "b_re": state(f["ssm_b_re"][0]), "b_im": state(f["ssm_b_im"][0]),
        "c_re": cstate(f["ssm_c_re"][0]), "c_im": cstate(f["ssm_c_im"][0]), "d_diag": dd.reshape(16, 512),
        "ident": np.eye(P, dtype=np.float32), "zeros": np.zeros((P, 2048), np.float32), "rot": rot, "mask": mask,
        "cos": np.tile(np.cos(ang.astype(np.float64)).astype(np.float32), (4, 1)),
        "sin": np.tile(np.sin(ang.astype(np.float64)).astype(np.float32), (4, 1)),
    }


_OUTS = {"y": (P, KT, TW), "memkv": (4, P, 2048), "k_new": (P, P + DEC), "v_new": (P, P + DEC), "ssm_new": (P, 64),
         "st_f0": (P, 4, FT), "st_f1": (P, 4, FT), "st_c1": (P, 4, KT)}
_SCRATCH = {"uj": (32, 16, CK, CC), "yj": (32, 16, CK, CC), "bt": (P, 2, 16, P), "er": (P, 16, NCK + 1), "ei": (P, 16, NCK + 1),
            "cm": (P, 2, 4096), "tm": (P, CK, 512)}


def kernel(**inputs):
    import concourse.bacc as _bacc
    from concourse.bass_utils import run_bass_kernel_spmd as _run

    nc = _bacc.Bacc("TRN2", target_bir_lowering=False, num_devices=1)
    arrays = {f"in_{k}": np.ascontiguousarray(v) for k, v in _layout(inputs).items()}
    a = {k[3:]: nc.dram_tensor(k, v.shape, F32, kind="ExternalInput").ap() for k, v in arrays.items()}
    for k, s in _OUTS.items():
        a[k] = nc.dram_tensor(f"out_{k}", s, F32, kind="ExternalOutput").ap()
    for k, s in _SCRATCH.items():
        a[k] = nc.dram_tensor(f"scratch_{k}", s, F32, kind="Internal").ap()
    build(nc, a)
    r = _run(nc, [arrays], core_ids=[0]).results[0]
    o = {k: np.asarray(r[f"out_{k}"]) for k in _OUTS}

    def tokens(x):
        return np.ascontiguousarray(x.transpose(2, 1, 0)).reshape(x.shape[2], -1)
    y = tokens(o["y"])
    yp, ys = y[None, :SEQ], y[None, S0:]
    kw, vw = o["k_new"].T, o["v_new"].T
    ssm = [o["ssm_new"][:, 16 * k:16 * k + 16].T.reshape(1, 1, 32, 64) for k in range(4)]
    conv = {q: o[q].transpose(1, 2, 0).reshape(4, -1) for q in ("st_f0", "st_f1", "st_c1")}
    cf = np.stack([conv["st_f0"], conv["st_f1"]])
    mk = np.stack([tokens(o["memkv"][2 * l].reshape(P, KT, NMEM)) for l in (0, 1)])
    mv = np.stack([o["memkv"][2 * l + 1].reshape(P, KT, 2, P).transpose(2, 0, 1, 3).reshape(NMEM, D) for l in (0, 1)])
    out = (yp, ys, kw[:P].reshape(1, 1, P, 2, 64), vw[:P].reshape(1, 1, P, 2, 64), ssm[0], ssm[1],
           conv["st_c1"][None, None, 0:2], cf[:, None, 0:2], mk.reshape(2, 1, NMEM, HEADS, 256), mv.reshape(2, 1, NMEM, HEADS, 256),
           kw[P:].reshape(1, 1, DEC, 2, 64), vw[P:].reshape(1, 1, DEC, 2, 64), ssm[2], ssm[3],
           conv["st_c1"][None, None, 2:4], cf[:, None, 2:4])
    return tuple(np.ascontiguousarray(x) for x in out)
```
